# Optimizing a Trainium2 kernel written in Bass

```python
import math
import jax, jax.numpy as jnp
from jax import lax
import numpy as np

D_MODEL = 1024
BATCH = 1
SEQ = 256
DEPTH = 2

N_META = 16
Q_BLOCK = 128
EPS = 1e-6

SSM_WIDTH = 256
SSM_GROUP = 16
SSM_GROUPS = SSM_WIDTH // SSM_GROUP
SSM_STATE = 64
DIFF_HEADS = 4
DIFF_QK_DIM = 64
DIFF_V_DIM = 2 * DIFF_QK_DIM
DIFF_WIDTH = DIFF_HEADS * DIFF_V_DIM
FOX_HEADS = 4
FOX_HEAD_DIM = 64
FOX_WIDTH = FOX_HEADS * FOX_HEAD_DIM
MIX_WIDTH = SSM_WIDTH + DIFF_WIDTH + FOX_WIDTH
IN_SPLIT = (SSM_WIDTH, DIFF_WIDTH, DIFF_WIDTH, DIFF_WIDTH,
            FOX_WIDTH, FOX_WIDTH, FOX_WIDTH, FOX_HEADS)
IN_WIDTH = SSM_WIDTH + 3 * DIFF_WIDTH + 3 * FOX_WIDTH + FOX_HEADS
D_FF_DENSE = 2816
N_EXPERTS = 8
TOP_K = 2
D_FF_EXPERT = 3584
N_DENSE = (DEPTH + 1) // 2
N_MOE = DEPTH // 2

kernel_name = "hymba_s5_diffattn_fox_moe_trunk"

def _rmsnorm(x, g):
    xf = x.astype(jnp.float32)
    y = xf * lax.rsqrt(jnp.mean(xf * xf, axis=-1, keepdims=True) + EPS)
    return (y * g.astype(jnp.float32)).astype(x.dtype)

def _heads(t, n_heads, *tail):
    return jnp.moveaxis(t.reshape(t.shape[:2] + (n_heads,) + tail), 2, 1)

def _merge_heads(o):
    b, h, l, d = o.shape
    return jnp.moveaxis(o, 1, 2).reshape(b, l, h * d)

def _block_sweep(block_fn, q_args, n_meta):
    L = q_args[0].shape[2]
    pos = jnp.arange(L, dtype=jnp.int32)
    meta_out = block_fn(*[a[:, :, :n_meta] for a in q_args], pos[:n_meta])
    n_blk = (L - n_meta) // Q_BLOCK

    def to_blocks(a):
        r = a[:, :, n_meta:]
        r = r.reshape(r.shape[:2] + (n_blk, Q_BLOCK) + r.shape[3:])
        return jnp.moveaxis(r, 2, 0)

    blocks = tuple(to_blocks(a) for a in q_args) + (pos[n_meta:].reshape(n_blk, Q_BLOCK),)
    real = lax.map(lambda args: block_fn(*args), blocks)
    real = jnp.moveaxis(real, 0, 2)
    real = real.reshape(real.shape[:2] + (n_blk * Q_BLOCK,) + real.shape[4:])
    return jnp.concatenate([meta_out, real], axis=2)

def _complex_affine_combine(e1, e2):
    ar1, ai1, br1, bi1 = e1
    ar2, ai2, br2, bi2 = e2
    ar = ar2 * ar1 - ai2 * ai1
    ai = ar2 * ai1 + ai2 * ar1
    br = ar2 * br1 - ai2 * bi1 + br2
    bi = ar2 * bi1 + ai2 * br1 + bi2
    return (ar, ai, br, bi)

def _s5(u, lam_re, lam_im, log_dt, b_re, b_im, c_re, c_im, d_skip, w_glu):
    bsz, L, _ = u.shape
    f32 = jnp.float32
    uf = u.astype(f32).reshape(bsz, L, SSM_GROUPS, SSM_GROUP)
    dt = jnp.exp(log_dt.astype(f32))[:, None]
    lr = lam_re.astype(f32)
    li = lam_im.astype(f32)
    mag = jnp.exp(lr * dt)
    ab_re = mag * jnp.cos(li * dt)
    ab_im = mag * jnp.sin(li * dt)
    den = lr * lr + li * li
    nr = ab_re - 1.0
    ni = ab_im
    coef_re = (nr * lr + ni * li) / den
    coef_im = (ni * lr - nr * li) / den
    bu_r = jnp.einsum('blgc,gnc->blgn', uf, b_re.astype(f32))
    bu_i = jnp.einsum('blgc,gnc->blgn', uf, b_im.astype(f32))
    bu_re = coef_re * bu_r - coef_im * bu_i
    bu_im = coef_re * bu_i + coef_im * bu_r
    shape = bu_re.shape
    a_re = jnp.broadcast_to(ab_re, shape)
    a_im = jnp.broadcast_to(ab_im, shape)
    _, _, x_re, x_im = lax.associative_scan(_complex_affine_combine,
                                            (a_re, a_im, bu_re, bu_im), axis=1)
    y = (jnp.einsum('blgn,gcn->blgc', x_re, c_re.astype(f32))
         - jnp.einsum('blgn,gcn->blgc', x_im, c_im.astype(f32))
         + d_skip.astype(f32) * uf)
    y = jax.nn.gelu(y.reshape(bsz, L, SSM_WIDTH))
    g = y @ w_glu.astype(f32)
    out = g[..., :SSM_WIDTH] * jax.nn.sigmoid(g[..., SSM_WIDTH:])
    return out.astype(u.dtype)

def _diff_attention(q, k, v, lam, lam_init, subln_g):
    f32 = jnp.float32
    L = k.shape[2]
    k_pos = jnp.arange(L, dtype=jnp.int32)
    scale = DIFF_QK_DIM ** -0.5
    vf = v.astype(f32)

    def block(qb, q_pos):
        s = jnp.einsum('bhqmd,bhkmd->bhmqk', qb, k, preferred_element_type=f32) * scale
        mask = k_pos[None, :] <= q_pos[:, None]
        p = jax.nn.softmax(jnp.where(mask, s, -jnp.inf), axis=-1)
        a = p[:, :, 0] - lam * p[:, :, 1]
        return jnp.einsum('bhqk,bhkd->bhqd', a, vf)

    o = _block_sweep(block, (q,), N_META)
    o = _rmsnorm(o, subln_g) * (1.0 - lam_init)
    return _merge_heads(o)

def _forgetting_attention(q, k, v, log_f):
    f32 = jnp.float32
    L = k.shape[2]
    k_pos = jnp.arange(L, dtype=jnp.int32)
    scale = FOX_HEAD_DIM ** -0.5
    cum = jnp.cumsum(log_f, axis=-1)
    vf = v.astype(f32)

    def block(qb, cq, q_pos):
        s = jnp.einsum('bhqd,bhkd->bhqk', qb, k, preferred_element_type=f32) * scale
        s = s + cq[..., :, None] - cum[:, :, None, :]
        mask = k_pos[None, :] <= q_pos[:, None]
        p = jax.nn.softmax(jnp.where(mask, s, -jnp.inf), axis=-1)
        return jnp.einsum('bhqk,bhkd->bhqd', p, vf)

    o = _block_sweep(block, (q, cum), N_META)
    return _merge_heads(o)

def _swiglu(h, w1, w3, w2):
    return (jax.nn.silu(h @ w1) * (h @ w3)) @ w2

def _moe(h, w_router, w1, w3, w2):
    f32 = jnp.float32
    logits = (h @ w_router).astype(f32)
    top_v, top_i = lax.top_k(logits, TOP_K)
    gw = jax.nn.softmax(top_v, axis=-1)
    gate = jnp.sum(jax.nn.one_hot(top_i, N_EXPERTS, dtype=f32) * gw[..., None], axis=-2)
    y = jnp.zeros(h.shape, f32)
    for e in range(N_EXPERTS):
        y = y + gate[..., e:e + 1] * _swiglu(h, w1[e], w3[e], w2[e]).astype(f32)
    return y.astype(h.dtype)

def setup_inputs(seed: int = 0) -> dict:
    key = jax.random.key(seed)
    ks = jax.random.split(key, 32)
    f32 = jnp.float32
    nrm = lambda k, shape, s: jax.random.normal(k, shape, f32) * s
    n_idx = jnp.arange(SSM_STATE, dtype=f32)
    lam_re = -0.5 + nrm(ks[5], (DEPTH, SSM_GROUPS, SSM_STATE), 0.01)
    lam_im = math.pi * n_idx + nrm(ks[6], (DEPTH, SSM_GROUPS, SSM_STATE), 0.01)
    return {
        "x": nrm(ks[0], (BATCH, SEQ, D_MODEL), 1.0),
        "meta_tokens": nrm(ks[1], (N_META, D_MODEL), 1.0),
        "norm_mix_g": 1.0 + nrm(ks[2], (DEPTH, D_MODEL), 0.02),
        "w_in": nrm(ks[3], (DEPTH, D_MODEL, IN_WIDTH), D_MODEL ** -0.5),
        "w_out": nrm(ks[4], (DEPTH, MIX_WIDTH, D_MODEL), MIX_WIDTH ** -0.5),
        "ssm_lambda_re": lam_re,
        "ssm_lambda_im": lam_im,
        "ssm_log_dt": jax.random.uniform(ks[7], (DEPTH, SSM_GROUPS), f32,
                                         math.log(1e-3), math.log(1e-1)),
        "ssm_b_re": nrm(ks[8], (DEPTH, SSM_GROUPS, SSM_STATE, SSM_GROUP), (2 * SSM_GROUP) ** -0.5),
        "ssm_b_im": nrm(ks[9], (DEPTH, SSM_GROUPS, SSM_STATE, SSM_GROUP), (2 * SSM_GROUP) ** -0.5),
        "ssm_c_re": nrm(ks[10], (DEPTH, SSM_GROUPS, SSM_GROUP, SSM_STATE), (2 * SSM_STATE) ** -0.5),
        "ssm_c_im": nrm(ks[11], (DEPTH, SSM_GROUPS, SSM_GROUP, SSM_STATE), (2 * SSM_STATE) ** -0.5),
        "ssm_d": nrm(ks[12], (DEPTH, SSM_GROUPS, SSM_GROUP), 1.0),
        "ssm_w_glu": nrm(ks[13], (DEPTH, SSM_WIDTH, 2 * SSM_WIDTH), SSM_WIDTH ** -0.5),
        "diff_lambda_q1": nrm(ks[14], (DEPTH, DIFF_QK_DIM), 0.1),
        "diff_lambda_k1": nrm(ks[15], (DEPTH, DIFF_QK_DIM), 0.1),
        "diff_lambda_q2": nrm(ks[16], (DEPTH, DIFF_QK_DIM), 0.1),
        "diff_lambda_k2": nrm(ks[17], (DEPTH, DIFF_QK_DIM), 0.1),
        "diff_subln_g": 1.0 + nrm(ks[18], (DEPTH, DIFF_V_DIM), 0.02),
        "fox_forget_b": jax.random.uniform(ks[19], (DEPTH, FOX_HEADS), f32, 2.0, 5.0),
        "norm_ffn_g": 1.0 + nrm(ks[20], (DEPTH, D_MODEL), 0.02),
        "dense_w1": nrm(ks[21], (N_DENSE, D_MODEL, D_FF_DENSE), D_MODEL ** -0.5),
        "dense_w3": nrm(ks[22], (N_DENSE, D_MODEL, D_FF_DENSE), D_MODEL ** -0.5),
        "dense_w2": nrm(ks[23], (N_DENSE, D_FF_DENSE, D_MODEL), D_FF_DENSE ** -0.5),
        "moe_router": nrm(ks[24], (N_MOE, D_MODEL, N_EXPERTS), D_MODEL ** -0.5),
        "moe_w1": nrm(ks[25], (N_MOE, N_EXPERTS, D_MODEL, D_FF_EXPERT), D_MODEL ** -0.5),
        "moe_w3": nrm(ks[26], (N_MOE, N_EXPERTS, D_MODEL, D_FF_EXPERT), D_MODEL ** -0.5),
        "moe_w2": nrm(ks[27], (N_MOE, N_EXPERTS, D_FF_EXPERT, D_MODEL), D_FF_EXPERT ** -0.5),
        "final_norm_g": 1.0 + nrm(ks[28], (D_MODEL,), 0.02),
    }

def reference(x, meta_tokens, norm_mix_g, w_in, w_out, ssm_lambda_re, ssm_lambda_im,
              ssm_log_dt, ssm_b_re, ssm_b_im, ssm_c_re, ssm_c_im, ssm_d, ssm_w_glu,
              diff_lambda_q1, diff_lambda_k1, diff_lambda_q2, diff_lambda_k2, diff_subln_g,
              fox_forget_b, norm_ffn_g, dense_w1, dense_w3, dense_w2,
              moe_router, moe_w1, moe_w3, moe_w2, final_norm_g):
    f32 = jnp.float32
    bsz = x.shape[0]
    meta = jnp.broadcast_to(meta_tokens[None].astype(x.dtype), (bsz, N_META, D_MODEL))
    res = jnp.concatenate([meta, x], axis=1)
    offs = np.cumsum(np.array(IN_SPLIT))[:-1].tolist()
    for l in range(DEPTH):
        h = _rmsnorm(res, norm_mix_g[l])
        z = h @ w_in[l]
        u, dq, dk, dv, fq, fk, fv, fg = jnp.split(z, offs, axis=-1)

        ssm_out = _s5(u, ssm_lambda_re[l], ssm_lambda_im[l], ssm_log_dt[l],
                      ssm_b_re[l], ssm_b_im[l], ssm_c_re[l], ssm_c_im[l],
                      ssm_d[l], ssm_w_glu[l])

        lam_init = 0.8 - 0.6 * math.exp(-0.3 * l)
        lam = (jnp.exp(jnp.sum(diff_lambda_q1[l].astype(f32) * diff_lambda_k1[l].astype(f32)))
               - jnp.exp(jnp.sum(diff_lambda_q2[l].astype(f32) * diff_lambda_k2[l].astype(f32)))
               + lam_init)
        diff_out = _diff_attention(_heads(dq, DIFF_HEADS, 2, DIFF_QK_DIM),
                                   _heads(dk, DIFF_HEADS, 2, DIFF_QK_DIM),
                                   _heads(dv, DIFF_HEADS, DIFF_V_DIM),
                                   lam, lam_init, diff_subln_g[l])

        log_f = jax.nn.log_sigmoid(fg.astype(f32) + fox_forget_b[l].astype(f32))
        fox_out = _forgetting_attention(_heads(fq, FOX_HEADS, FOX_HEAD_DIM),
                                        _heads(fk, FOX_HEADS, FOX_HEAD_DIM),
                                        _heads(fv, FOX_HEADS, FOX_HEAD_DIM),
                                        jnp.moveaxis(log_f, 2, 1))

        mixed = jnp.concatenate([ssm_out.astype(res.dtype), diff_out.astype(res.dtype),
                                 fox_out.astype(res.dtype)], axis=-1)
        res = res + mixed @ w_out[l]

        h = _rmsnorm(res, norm_ffn_g[l])
        if l % 2 == 0:
            ffn = _swiglu(h, dense_w1[l // 2], dense_w3[l // 2], dense_w2[l // 2])
        else:
            ffn = _moe(h, moe_router[l // 2], moe_w1[l // 2], moe_w3[l // 2], moe_w2[l // 2])
        res = res + ffn
    return _rmsnorm(res, final_norm_g)[:, N_META:]


_drawn_inputs = setup_inputs


def setup_inputs(seed=0):
    import zlib

    import numpy as np

    out = dict(_drawn_inputs(seed))
    spreads = {}
    factors = {'ssm_lambda_re': 200.0,
     'ssm_b_im': 10.061,
     'ssm_c_re': 13.32,
     'diff_subln_g': 2.839,
     'final_norm_g': 20.082,
     'ssm_lambda_im': 2.784,
     'ssm_log_dt': 2.901,
     'ssm_b_re': 52.84,
     'ssm_c_im': 8.0,
     'norm_ffn_g': 2.87}
    for name, (base, spread) in spreads.items():
        noise = np.random.default_rng([zlib.crc32(name.encode()), seed]).standard_normal(out[name].shape)
        drawn = base * np.exp(spread * noise) if base else spread * noise
        out[name] = __import__('jax').numpy.asarray(drawn.astype(out[name].dtype))
    for name, factor in factors.items():
        out[name] = (out[name] * factor).astype(out[name].dtype)
    return out
```

```python
import math

import concourse.bass as bass
from concourse import mybir
from contextlib import ExitStack

F32 = mybir.dt.float32
I32 = mybir.dt.int32
ALU = mybir.AluOpType
ACT = mybir.ActivationFunctionType
AX = mybir.AxisListType

P = 128
DEPTH = 2
D = 1024
KD = D // P
N_META, SEQ = 16, 256
L = N_META + SEQ
TT = [(0, 128), (128, 128), (256, 16)]
RT = SEQ // P
EPS = 1e-6
SSM_W, SSM_C, STATE = 256, 16, 64
NST = 8
DH, DQK, DV = 4, 64, 128
FH, FD = 4, 64
FF = 2816
NFF = FF // P
NE, FE = 8, 3584
NFB = FE // 512
MAX_JOBS = 11
SCALE = DQK ** -0.5
MAGIC = 12582912.0
LN2_HI, LN2_LO = 0.693359375, -2.12194440e-4
SIN_2PI = 6.2831850
NEG = -1.0e30
SLOT = 4096
RING, MRING = 5, 7
UNITS = [(k, h, t) for k in ("d", "f") for h in range(4) for t in range(3)]


def build(nc, a, out):
    ctx = ExitStack()
    with ctx:
        ctx.enter_context(nc.allow_non_contiguous_dma(reason="small parameter loads"))

        def sb(name, cols, dt=F32):
            return ctx.enter_context(nc.sbuf_tensor(name, [P, cols], dt))

        ring = sb("weight_ring", RING * SLOT)
        late = sb("late_region", 2 * SLOT)
        region = {n: sb(n, KD * L) for n in ("resT", "hT", "mixedT", "cosT", "sinT", "foxqk")}
        attn = sb("attn_temps", 2720)
        bank = [ctx.enter_context(nc.psum_tensor(f"bank{i}", [P, 512], F32)) for i in range(8)]

        def cut(tensor, start, *dims):
            n = math.prod(dims)
            v = tensor[:, start:start + n]
            if len(dims) == 2:
                v = v.rearrange("p (a b) -> p a b", b=dims[1])
            if len(dims) == 3:
                v = v.rearrange("p (a b c) -> p a b c", b=dims[1], c=dims[2])
            return v

        resT, hT, mixedT = (cut(region[n], 0, KD, L) for n in ("resT", "hT", "mixedT"))
        cosT, sinT = (cut(region[n], 0, NST, L) for n in ("cosT", "sinT"))
        fqa, fka = cut(region["foxqk"], 0, FH, L), cut(region["foxqk"], FH * L, FH, L)
        sqT = mixedT
        dqT, dkT = cut(late, 0, DH, L), cut(late, 1088, DH, L)
        uT = cut(late, 2176, 2, L)
        vtok = cut(late, 2720, 3, 768)
        w_scan = cut(late, 5024, 2, 2, L)
        x_ssm = cut(late, 6112, 2, 2, L)
        t_dve, t_pool = cut(late, 7200, L), cut(late, 7472, L)
        gT = cut(late, 0, NFF, L)
        silu_t = cut(late, NFF * L, 2, L)
        xtok = cut(late, 0, 3, D)
        s_buf, e_buf, a_buf = cut(attn, 0, 2, 2, L), cut(attn, 1088, 2, 2, L), cut(attn, 2176, 2, L)
        aT = cut(region["hT"], 0, 2, 3, L)
        o_buf_t, sq_o_t, rs_t = sb("o_buf", 2 * L), sb("o_square", 2 * L), sb("rstd", L)
        rs0_t = sb("rstd_first", L)
        o_buf, sq_o = cut(o_buf_t, 0, 2, L), cut(sq_o_t, 0, 2, L)
        fgz, fgm, fgc = (cut(attn, i * L, L) for i in range(3))
        ys, yq, ye, gy = (cut(region["cosT"], i * 544, 2, L) for i in range(4))
        glu_e = cut(region["sinT"], 0, 2, L)
        racc = cut(region["foxqk"], 0, RT, D)
        mhT = cut(region["hT"], 0, KD, SEQ)
        htok = cut(region["cosT"], 0, RT, D)
        g_ffn_b, g_fin_b = cut(region["sinT"], 0, D), cut(region["sinT"], D, D)
        hTe, ysb = cut(region["mixedT"], 0, KD, P), cut(region["mixedT"], D, D)
        e1, g_e = cut(region["resT"], 0, 2, 512), cut(region["resT"], 1024, 2, 512)
        gTe = cut(attn, 0, 2, 512)
        sel, selg, scat = cut(attn, 1024, RT, P), cut(attn, 1280, RT, P), cut(attn, 1536, SEQ)
        const_t = sb("constants", 6 * P + 2 * L + 9)
        ident, avgD, avgV, onesF, tri, slot_iota = (cut(const_t, i * P, P) for i in range(6))
        time_iota, ones_row = cut(const_t, 6 * P, L), cut(const_t, 6 * P + L, L)
        expert_iota = cut(const_t, 6 * P + 2 * L, 8)
        eps_col = cut(const_t, 6 * P + 2 * L + 8, 1)
        mask_t = sb("causal_mask", 3 * L)
        mask = cut(mask_t, 0, 3, L)
        rows_t, prm_t = sb("param_rows", P), sb("param_cols", 70 + 16)
        prm = prm_t
        dt_rows, dt_wide = sb("dt_rows", 2), sb("dt_wide", P)
        b_raw_t, c_raw_t = sb("b_raw", 2 * NST * 16), sb("c_raw", 4 * STATE)
        b_raw, c_raw = cut(b_raw_t, 0, 2, NST, 16), cut(c_raw_t, 0, 2, 2, STATE)
        b_exp_t, c_exp_t = sb("b_blocks", 512), sb("c_blocks", 512)
        b_exp, c_exp = cut(b_exp_t, 0, 2, NST, 32), cut(c_exp_t, 0, 4, P)
        bT_t, cT_t = sb("bT", 512), sb("cT", 512)
        bT, cT = cut(bT_t, 0, 2, 2, P), cut(cT_t, 0, 2, 2, P)
        glu_t = sb("w_glu", 1024)
        w_glu = cut(glu_t, 0, 2, 512)
        lam_t = sb("lambda_vectors", 4 * 2 * 64)
        lam_v = cut(lam_t, 0, 4, 2, 64)
        fb_t = sb("forget_bias", 2)
        router_t = sb("router", KD * NE)
        router = cut(router_t, 0, KD, NE)
        small = sb("small", 340)
        ints = sb("ints", 20, I32)

        def sm(i, n=8):
            return small[:, i:i + n]

        events = {}

        def ev(name):
            if name not in events:
                events[name] = ctx.enter_context(nc.semaphore(name))
            return events[name]

        bank_full = [ctx.enter_context(nc.semaphore(f"bank_full{b}")) for b in range(6)]
        bank_free = [ctx.enter_context(nc.semaphore(f"bank_free{b}")) for b in range(6)]
        slot_full = [ctx.enter_context(nc.semaphore(f"slot_full{s}")) for s in range(RING)]
        chunk_used = ctx.enter_context(nc.semaphore("chunk_used"))
        mslot_full = [ctx.enter_context(nc.semaphore(f"expert_slot_full{s}")) for s in range(MRING)]
        mchunk_used = ctx.enter_context(nc.semaphore("expert_chunk_used"))
        groups = {}

        def open_group(pe, name):
            n = len(groups)
            groups[name] = (n % 6, n // 6)
            if n >= 6:
                pe.wait_ge(bank_free[n % 6], n // 6)
            return bank[n % 6]

        def close_group(ins, name):
            ins.then_inc(bank_full[groups[name][0]], 1)

        def take(eng, name):
            b, use = groups[name]
            eng.wait_ge(bank_full[b], use + 1)
            return bank[b]

        def release(ins, name):
            ins.then_inc(bank_free[groups[name][0]], 1)

        def evacuated(eng, name):
            b, use = groups[name]
            eng.wait_ge(bank_free[b], use + 1)

        class Chain:

            def __init__(self, eng, sem):
                self.eng, self.sem, self.base, self.n = eng, sem, 0, 0

            def __call__(self, ins):
                self.n += 1
                ins.then_inc(self.sem, 1)
                self.eng.wait_ge(self.sem, self.base + self.n)

        chunks = []

        def chunk(name, src, k, cols):
            v = ring[:, (len(chunks) % RING) * SLOT:(len(chunks) % RING) * SLOT + k * cols]
            chunks.append((name, src, v.rearrange("p (k n) -> p k n", n=cols)))

        for l in range(DEPTH):
            w_in = a["w_in"][l, :, :].rearrange("(k p) n -> p k n", p=P)
            for name, lo, hi in (("u", 0, 256), ("fvg", 2304, 2564), ("dq", 256, 768), ("dk", 768, 1280),
                                 ("dv", 1280, 1792), ("fqk", 1792, 2304)):
                chunk(f"{name}{l}", w_in[:, :, lo:hi], KD, hi - lo)
            w_out = a["w_out"][l, :, :].rearrange("(k p) n -> p k n", p=P)
            for half in range(2):
                chunk(f"out{l}{half}", w_out[:, :, 512 * half:512 * half + 512], KD, 512)
            if l == 0:
                w1, w3 = (a[n][0, :, :].rearrange("(k p) n -> p k n", p=P) for n in ("dense_w1", "dense_w3"))
                w2 = a["dense_w2"][0, :, :].rearrange("(k p) n -> p k n", p=P)
                for fb in range(0, FF, 512):
                    n = min(512, FF - fb)
                    chunk(f"w1_{fb}", w1[:, :, fb:fb + n], KD, n)
                    chunk(f"w3_{fb}", w3[:, :, fb:fb + n], KD, n)
                for half in range(2):
                    for f in range(0, NFF, 8):
                        n = min(8, NFF - f)
                        chunk(f"w2_{half}_{f}", w2[:, f:f + n, 512 * half:512 * half + 512], n, 512)
        where = {c[0]: i for i, c in enumerate(chunks)}

        def chunk_ready(pe, name):
            i = where[name]
            pe.wait_ge(slot_full[i % RING], 16 * (i // RING + 1))
            return chunks[i][2]

        order = [(0, "w1"), (0, "w3")]
        for fb in range(1, NFB):
            order += [(fb, "w1"), (fb, "w3"), (fb - 1, "w2")]
        order += [(NFB - 1, "w2")]
        NC = len(order)
        assert NC % MRING == 0

        def mslot(c):
            s = c % MRING
            t, o = (ring, s) if s < RING else (late, s - RING)
            return t[:, o * SLOT:(o + 1) * SLOT]

        def expert_chunk(e, c):
            fb, kind = order[c]
            if kind == "w2":
                src = a["moe_w2"][0, e, 512 * fb:512 * fb + 512, :].rearrange("(k p) n -> p k n", p=P)
                return src, mslot(c).rearrange("p (k n) -> p k n", n=D)
            src = a[f"moe_{kind}"][0, e, :, 512 * fb:512 * fb + 512].rearrange("(k p) n -> p k n", p=P)
            return src, mslot(c).rearrange("p (k n) -> p k n", n=512)

        N_PARAM = 10

        block = ctx.enter_context(nc.Block())

        @block.tensor
        def _(pe):
            def mm(o, lhsT, rhs, start, stop):
                return nc.tensor.matmul(o, lhsT, rhs, start=start, stop=stop)

            def done_with_chunk(ins):
                ins.then_inc(chunk_used, 1)

            def transposed_params():
                pe.wait_ge(ev("identity_ready"), 2)
                pe.wait_ge(ev("params_loaded"), 16 * N_PARAM)
                b = open_group(pe, "prm")
                close_group(nc.tensor.transpose(b[:, 0:70], rows_t[0:70, :], ident[0:70, 0:70]), "prm")
                pe.wait_ge(ev("dt_wide_ready"), 1)
                b = open_group(pe, "ldt")
                close_group(nc.tensor.transpose(b[:, 0:16], dt_wide[0:16, :], ident[0:16, 0:16]), "ldt")

            def ssm_weights(l):
                pe.wait_ge(ev(f"b_blocks{l}"), 1)
                b = open_group(pe, f"bT{l}")
                for m in range(2):
                    for c in range(2):
                        ins = nc.tensor.transpose(b[:, (2 * m + c) * P:(2 * m + c + 1) * P],
                                                  b_exp[:, c, 4 * m:4 * m + 4, :], ident)
                close_group(ins, f"bT{l}")
                pe.wait_ge(ev(f"c_blocks{l}"), 1)
                b = open_group(pe, f"cT{l}")
                for i in range(4):
                    ins = nc.tensor.transpose(b[:, i * P:(i + 1) * P], c_exp[:, i, :], ident)
                close_group(ins, f"cT{l}")

            def feature_norm(n):
                b = open_group(pe, f"ssq{n}")
                for k in range(KD):
                    if k == 0:
                        pe.wait_ge(ev("constants_ready"), 1)
                        pe.wait_ge(ev(f"squares_act{n}"), 1)
                    if k == KD // 2:
                        pe.wait_ge(ev(f"squares_dve{n}"), 1)
                    ins = mm(b[:, 0:L], avgD, sqT[:, k, :], k == 0, k == KD - 1)
                close_group(ins, f"ssq{n}")

            def project(n, name, w, lo, m, rhs_ready):
                b = open_group(pe, name)
                for k in range(KD):
                    if rhs_ready:
                        pe.wait_ge(ev(f"h{n}"), k + 1)
                    ins = mm(b[0:m, 0:L], w[:, k, lo:lo + m], hT[:, k, :], k == 0, k == KD - 1)
                close_group(ins, name)
                return ins

            def ssm_in(l, i):
                r = i % 4
                if i == 0:
                    evacuated(pe, f"bT{l}")
                    evacuated(pe, f"z{l}u1")
                for c in range(2):
                    name = f"bu{l}{i}{c}"
                    b = open_group(pe, name)
                    close_group(mm(b[:, 0:L], bT[32 * r:32 * r + 32, i // 4, c, :],
                                   uT[32 * r:32 * r + 32, i // 4, :], True, True), name)

            def ssm_out(l, i):
                r, m = i % 4, i // 4
                if i == 0:
                    evacuated(pe, f"cT{l}")
                pe.wait_ge(ev(f"x_ready{l}"), i + 1)
                for c in range(2):
                    ins = mm(bank[6 + m][32 * r:32 * r + 32, 0:L], cT[:, m, c, 32 * r:32 * r + 32],
                             x_ssm[:, i % 2, c, :], c == 0, c == 1)
                ins.then_inc(ev(f"y_done{l}"), 1)

            def mixer_inputs(l, n):
                steps = []

                def feature(cname, key, cols, last):
                    def f(key=key, cols=cols, last=last):
                        w = chunk_ready(pe, f"{cname}{l}")
                        ins = project(n, f"z{l}{key}", w, cols[0], cols[1], False)
                        if last:
                            pe.wait_ge(bank_full[groups[f"z{l}{key}"][0]], groups[f"z{l}{key}"][1] + 1)
                            pe.sem_inc(chunk_used, 1)
                    steps.append(f)

                def tokens(cname, key, cols, t, last):
                    def f():
                        w = chunk_ready(pe, f"{cname}{l}")
                        q0, qn = TT[t]
                        name = f"z{l}{key}{t}"
                        b = open_group(pe, name)
                        for k in range(KD):
                            ins = mm(b[0:qn, 0:cols], hT[:, k, q0:q0 + qn], w[:, k, 0:cols], k == 0, k == KD - 1)
                        close_group(ins, name)
                        if last:
                            pe.wait_ge(bank_full[groups[name][0]], groups[name][1] + 1)
                            pe.sem_inc(chunk_used, 1)
                    steps.append(f)

                w = chunk_ready(pe, f"u{l}")
                for m in range(2):
                    ins = project(n, f"z{l}u{m}", w, P * m, P, m == 0)
                name = f"z{l}u1"
                pe.wait_ge(bank_full[groups[name][0]], groups[name][1] + 1)
                pe.sem_inc(chunk_used, 1)
                for t in range(3):
                    tokens("fvg", "fv", 256, t, False)
                feature("fvg", "fg", (256, FH), True)
                for cname in ("dq", "dk"):
                    for h in range(DH):
                        feature(cname, f"{cname}{h}", (P * h, P), h == DH - 1)
                for t in range(3):
                    tokens("dv", "dv", 512, t, t == 2)
                for i in range(4):
                    feature("fqk", f"fqk{i}", (P * i, P), i == 3)
                for j, step in enumerate(steps):
                    step()
                    i = j // 2
                    if j % 2 == 0 and i < NST:
                        if i == 0:
                            ssm_weights(l)
                        ssm_in(l, i)
                        if i >= 2:
                            ssm_out(l, i - 2)
                ssm_out(l, NST - 2)
                ssm_out(l, NST - 1)

            def scores(l, u):
                kind, h, t = UNITS[u]
                (q0, qn), kmax = TT[t], sum(TT[t])
                if u == 0:
                    evacuated(pe, f"z{l}dk3")
                    evacuated(pe, f"z{l}dq3")
                if kind == "f" and h == 0 and t == 0:
                    evacuated(pe, f"z{l}fqk3")
                    pe.wait_ge(ev(f"decay_rows{l}"), 2)
                for m in range(2 if kind == "d" else 1):
                    name = f"s{l}_{u}_{m}"
                    b = open_group(pe, name)
                    if kind == "d":
                        q, k = (x[64 * m:64 * m + 64, h, :] for x in (dqT, dkT))
                    else:
                        q, k = fqa[0:100, h, :], fka[0:100, h, :]
                    close_group(mm(b[0:qn, 0:kmax], q[:, q0:q0 + qn], k[:, 0:kmax], True, True), name)

            def turn_probs(l, u):
                _, _, t = UNITS[u]
                q0, qn = TT[t]
                pe.wait_ge(ev(f"probs{l}"), u + 1)
                name = f"at{l}_{u}"
                b = open_group(pe, name)
                for kt in range(t + 1):
                    k0, kn = TT[kt]
                    ins = nc.tensor.transpose(b[0:kn, P * kt:P * kt + qn], a_buf[0:qn, u % 2, k0:k0 + kn],
                                              ident[0:qn, 0:qn])
                close_group(ins, name)

            def values(l, u):
                kind, h, _ = UNITS[u]
                evacuated(pe, f"at{l}_{u}")
                if kind == "f":
                    evacuated(pe, f"z{l}fv2")
                    v, dv = vtok[:, :, 512 + FD * h:512 + FD * h + FD], FD
                else:
                    evacuated(pe, f"z{l}dv2")
                    v, dv = vtok[:, :, DV * h:DV * h + DV], DV
                name = f"o{l}_{u}"
                b = open_group(pe, name)
                for kt, (k0, kn) in enumerate(TT):
                    ins = mm(b[0:dv, k0:L], v[0:kn, kt, :], aT[0:kn, (u // 3) % 2, kt, k0:L], kt == 0, kt == 2)
                close_group(ins, name)

            def head_norm(l, u):
                h = UNITS[u][1]
                pe.wait_ge(ev(f"o_square{l}"), h + 1)
                name = f"hn{l}_{h}"
                b = open_group(pe, name)
                close_group(mm(b[:, 0:L], avgV, sq_o[:, h % 2, :], True, True), name)

            def glu(l):
                pe.wait_ge(ev("glu_loaded"), 16 * (l + 1))
                pe.wait_ge(ev(f"gelu_ready{l}"), 1)
                for m in range(4):
                    name = f"glu{l}{m}"
                    b = open_group(pe, name)
                    for k in range(2):
                        ins = mm(b[:, 0:L], w_glu[:, k, P * m:P * m + P], gy[:, k, :], k == 0, k == 1)
                    close_group(ins, name)

            def attention(l):
                scores(l, 0)
                for u in range(len(UNITS) + 2):
                    if u + 1 < len(UNITS):
                        scores(l, u + 1)
                    if 1 <= u <= len(UNITS) and UNITS[u - 1][2] == 2:
                        values(l, u - 1)
                    if u >= 2 and UNITS[u - 2][2] == 2 and UNITS[u - 2][0] == "d":
                        head_norm(l, u - 2)
                    if u < len(UNITS):
                        turn_probs(l, u)
                    if u == 4:
                        glu(l)

            def mix_ready(l):
                pe.wait_ge(ev(f"diff_out{l}"), DH)
                for h in range(FH):
                    evacuated(pe, f"o{l}_{12 + 3 * h + 2}")
                pe.wait_ge(ev(f"ssm_out{l}"), 2)

            def output_projection_features(l):
                for half in range(2):
                    w = chunk_ready(pe, f"out{l}{half}")
                    for m in range(4):
                        name = f"r{l}{4 * half + m}"
                        b = open_group(pe, name)
                        for k in range(KD):
                            ins = mm(b[:, 0:L], w[:, k, P * m:P * m + P], mixedT[:, k, :], k == 0, k == KD - 1)
                        close_group(ins, name)
                    pe.wait_ge(bank_full[groups[name][0]], groups[name][1] + 1)
                    pe.sem_inc(chunk_used, 1)

            def output_projection_tokens(l):
                for half in range(2):
                    w = chunk_ready(pe, f"out{l}{half}")
                    for t in range(RT):
                        tok = slice(N_META + P * t, N_META + P * t + P)
                        name = f"rt{t}{half}"
                        b = open_group(pe, name)
                        for k in range(KD):
                            mm(b[:, :], mixedT[:, k, tok], w[:, k, :], k == 0, False)
                        for j in range(4):
                            ins = mm(b[:, P * j:P * j + P], resT[:, 4 * half + j, tok], ident, False, j == 3)
                        close_group(ins, name)
                    pe.wait_ge(bank_full[groups[name][0]], groups[name][1] + 1)
                    pe.sem_inc(chunk_used, 1)

            def dense():
                for fb in range(0, FF, 512):
                    w1, w3 = chunk_ready(pe, f"w1_{fb}"), chunk_ready(pe, f"w3_{fb}")
                    for i in range(min(512, FF - fb) // P):
                        f = fb // P + i
                        project(1, f"fa{f}", w1, P * i, P, f == 0)
                        project(1, f"fb{f}", w3, P * i, P, False)
                    pe.wait_ge(bank_full[groups[f"fb{f}"][0]], groups[f"fb{f}"][1] + 1)
                    pe.sem_inc(chunk_used, 2)
                for half in range(2):
                    bs = [open_group(pe, f"y{4 * half + m}") for m in range(4)]
                    for f0 in range(0, NFF, 8):
                        w = chunk_ready(pe, f"w2_{half}_{f0}")
                        fn = min(8, NFF - f0)
                        for m in range(4):
                            for f in range(f0, f0 + fn):
                                if half == 0 and m == 0:
                                    evacuated(pe, f"fb{f}")
                                ins = mm(bs[m][:, 0:L], w[:, f - f0, P * m:P * m + P], gT[:, f, :],
                                         f == 0, f == NFF - 1)
                            if f0 + fn == NFF:
                                close_group(ins, f"y{4 * half + m}")
                        if f0 + fn < NFF:
                            ins.then_inc(chunk_used, 1)
                        else:
                            pe.wait_ge(bank_full[groups[f"y{4 * half + 3}"][0]], groups[f"y{4 * half + 3}"][1] + 1)
                            pe.sem_inc(chunk_used, 1)

            pe.wait_ge(ev("identity_ready"), 2)
            pe.wait_ge(ev("x_loaded"), 16 * 4)
            for k in range(KD):
                b = open_group(pe, f"xT{k}")
                for t, (q0, qn) in enumerate(TT):
                    ins = nc.tensor.transpose(b[:, q0:q0 + qn], xtok[0:qn, t, P * k:P * k + P], ident[0:qn, 0:qn])
                close_group(ins, f"xT{k}")
            transposed_params()
            for l in range(DEPTH):
                feature_norm(2 * l)
                mixer_inputs(l, 2 * l)
                attention(l)
                mix_ready(l)
                if l == 0:
                    output_projection_features(l)
                    feature_norm(1)
                    dense()
            output_projection_tokens(1)

            for j in range(4):
                b = open_group(pe, f"mh{j}")
                for k in range(2):
                    for t in range(RT):
                        if j == 0 and k == 0:
                            pe.wait_ge(ev("htok"), t + 1)
                        ins = nc.tensor.transpose(b[:, (2 * k + t) * P:(2 * k + t + 1) * P],
                                                  htok[:, t, (2 * j + k) * P:(2 * j + k + 1) * P], ident)
                close_group(ins, f"mh{j}")
            for t in range(RT):
                b = open_group(pe, f"lg{t}")
                for k in range(KD):
                    if t == 0 and k % 2 == 0:
                        evacuated(pe, f"mh{k // 2}")
                    ins = mm(b[:, 0:NE], mhT[:, k, P * t:P * t + P], router[:, k, :], k == 0, k == KD - 1)
                close_group(ins, f"lg{t}")
            chosen = sm(48, 16)
            pe.wait_ge(ev("chosen"), 1)
            for name, mats in (("rank0", [(tri, 0)]), ("rank1", [(onesF, 0), (tri, 1)]),
                               ("count", [(onesF, 0), (onesF, 1)])):
                b = open_group(pe, name)
                for i, (m, t) in enumerate(mats):
                    ins = mm(b[:, 0:NE], m, chosen[:, NE * t:NE * t + NE], i == 0, i == len(mats) - 1)
                close_group(ins, name)
            n_groups = len(groups)
            for b in range(6):
                uses = (n_groups - 1 - b) // 6 + 1
                pe.wait_ge(bank_free[b], uses)

            def gather(j, ahead):
                pe.wait_ge(ev("sel_ready"), j + 1 + ahead)
                for d in range(KD):
                    b = bank[5 - d // 4]
                    for t in range(RT):
                        ins = mm(b[:, P * (d % 4):P * (d % 4) + P], htok[:, t, P * d:P * d + P], sel[:, t, :],
                                 t == 0, t == 1)
                    if d % 4 == 3:
                        ins.then_inc(ev("gathered"), 1)

            def up(j, fb, kind):
                c = order.index((fb, kind))
                pe.wait_ge(mslot_full[c % MRING], 16 * (3 * j + c // MRING + 1))
                w = mslot(c).rearrange("p (k n) -> p k n", n=512)
                b = bank[2 * (fb % 2) + (kind == "w3")]
                if kind == "w1" and fb >= 2:
                    pe.wait_ge(ev("g_ready"), 7 * j + fb - 1)
                for k in range(KD):
                    ins = mm(b[:, :], hTe[:, k, :], w[:, k, :], k == 0, k == KD - 1)
                ins.then_inc(ev("up_done"), 1)
                pe.wait_ge(ev("up_done"), 14 * j + 2 * fb + 1 + (kind == "w3"))
                pe.sem_inc(mchunk_used, 1)

            def turn(j, fb):
                pe.wait_ge(ev("g_ready"), 7 * j + fb + 1)
                for i in range(4):
                    ins = nc.tensor.transpose(bank[4][:, P * i:P * i + P], g_e[:, fb % 2, P * i:P * i + P], ident)
                ins.then_inc(ev("turned"), 1)

            def down(j, fb):
                c = order.index((fb, "w2"))
                pe.wait_ge(mslot_full[c % MRING], 16 * (3 * j + c // MRING + 1))
                pe.wait_ge(ev("turn_evac"), 7 * j + fb + 1)
                w = mslot(c).rearrange("p (k n) -> p k n", n=D)
                for i in range(4):
                    for half in range(2):
                        ins = mm(bank[6 + half][:, :], gTe[:, fb % 2, P * i:P * i + P],
                                 w[:, i, 512 * half:512 * half + 512], fb == 0 and i == 0, fb == 6 and i == 3)
                ins.then_inc(mchunk_used, 1)

            gather(0, 0)
            pe.wait_ge(ev("jobs_ready"), 1)
            n_jobs = pe.value_load(ints[0:1, 3:4], min_val=NE, max_val=MAX_JOBS)
            with pe.Fori(0, n_jobs) as j:
                pe.wait_ge(ev("gather_evac"), 2 * j + 2)
                for fb in range(NFB):
                    if fb == 0:
                        pe.wait_ge(ev("added"), 4 * j + 1)
                    up(j, fb, "w1")
                    if fb:
                        turn(j, fb - 1)
                    up(j, fb, "w3")
                    if fb == 3:
                        pe.wait_ge(ev("selg_ready"), j + 1)
                        for t in range(RT):
                            ins = nc.tensor.transpose(bank[5][:, P * t:P * t + P], selg[:, t, :], ident)
                        ins.then_inc(ev("scat_turned"), 1)
                    if fb:
                        down(j, fb - 1)
                pe.wait_ge(ev("scat_evac"), j + 1)
                gather(j, 1)
                pe.wait_ge(ev("gather_evac"), 2 * j + 4)
                turn(j, NFB - 1)
                down(j, NFB - 1)
                pe.wait_ge(ev("y_evac"), 2 * j + 2)
                for i in range(4):
                    t, half = i // 2, i % 2
                    mm(bank[i][:, :], scat[:, P * t:P * t + P], ysb[:, 512 * half:512 * half + 512],
                       True, True).then_inc(ev("scattered"), 1)

        @block.sync
        def _(sp):
            for i, (name, src, dst) in enumerate(chunks):
                if i >= RING:
                    sp.wait_ge(chunk_used, i - RING + 1)
                sp.dma_start(dst, src).then_inc(slot_full[i % RING], 16)

            def load(e, c):
                src, dst = expert_chunk(e, c)
                sp.dma_start(dst, src).then_inc(mslot_full[c % MRING], 16)

            n = len(chunks)
            for c in range(MRING):
                if c < RING:
                    sp.wait_ge(chunk_used, n - RING + (c - n) % RING + 1)
                elif c == RING:
                    sp.wait_ge(chunk_used, n - 1)
                load(0, c)
            with sp.Fori(0, NE - 1) as e:
                for c in range(NC):
                    ee = e if c + MRING < NC else e + 1
                    sp.wait_ge(mchunk_used, NC * e + c + 1)
                    load(ee, (c + MRING) % NC)
            for c in range(MRING, NC):
                sp.wait_ge(mchunk_used, NC * (NE - 1) + c - MRING + 1)
                load(NE - 1, c)
            sp.wait_ge(ev("jobs_ready"), 1)
            n_jobs = sp.value_load(ints[0:1, 3:4], min_val=NE, max_val=MAX_JOBS)
            with sp.If(n_jobs > NE):
                with sp.Fori(NE, n_jobs) as j:
                    e = sp.value_load(ints[0:1, bass.ds(j - NE, 1)], min_val=0, max_val=NE - 1)
                    for c in range(NC):
                        sp.wait_ge(mchunk_used, NC * j + c - MRING + 1)
                        load(e, c)
            sp.wait_ge(ev("out_ready"), 2)
            for t in range(RT):
                sp.dma_start(out[0, P * t:P * t + P, :], racc[:, t, :]).then_inc(ev("out_stored"), 16)
            sp.wait_ge(ev("out_stored"), 16 * RT)

        @block.gpsimd
        def _(pool):
            g = nc.gpsimd
            memsets = Chain(pool, ev("pool_memsets"))
            memsets(g.memset(ident, 0.0))
            memsets(g.memset(mask_t[:, :], 0.0))
            memsets(g.memset(tri, 1.0))
            g.affine_select(out=ident, in_=ident, compare_op=ALU.not_equal, fill=1.0, base=0,
                            pattern=[[-1, P]], channel_multiplier=1).then_inc(ev("identity_ready"), 2)
            pool.wait_ge(ev("identity_ready"), 2)
            setup = Chain(pool, ev("pool_setup"))
            setup(g.affine_select(out=mask, in_=mask, compare_op=ALU.is_ge, fill=NEG, base=0,
                                  pattern=[[P, 3], [-1, L]], channel_multiplier=1))
            setup(g.affine_select(out=tri, in_=tri, compare_op=ALU.is_ge, fill=0.0, base=-1,
                                  pattern=[[1, P]], channel_multiplier=-1))
            setup(g.memset(avgD, 1.0 / D))
            setup(g.memset(avgV, 1.0 / DV))
            setup(g.memset(eps_col, EPS))
            setup(g.memset(onesF, 1.0))
            setup(g.memset(ones_row, 1.0))
            setup(g.memset(b_exp_t[:, :], 0.0))
            setup(g.iota(slot_iota, [[1, P]], base=0, channel_multiplier=0, allow_small_or_imprecise_dtypes=True))
            setup(g.iota(time_iota, [[1, L]], base=0, channel_multiplier=0, allow_small_or_imprecise_dtypes=True))
            setup(g.iota(expert_iota, [[1, NE]], base=0, channel_multiplier=0, allow_small_or_imprecise_dtypes=True))
            g.iota(ints[:, 8:9], [[0, 1]], base=0, channel_multiplier=1).then_inc(ev("constants_ready"), 1)
            pool.wait_ge(ev("constants_ready"), 1)
            setup(g.memset(region["foxqk"][64:P, :], 0.0))
            setup(g.memset(fka[64:68, :, :], 1.0))
            setup(g.memset(fqa[96:100, :, :], 1.0 / SCALE))
            for i, v in enumerate((fka[64:68, :, :], fqa[96:100, :, :])):
                g.affine_select(out=v, in_=v, compare_op=ALU.is_equal, fill=0.0, base=0,
                                pattern=[[-1, FH], [0, L]], channel_multiplier=1).then_inc(ev("fox_select"), 1)
                pool.wait_ge(ev("fox_select"), i + 1)
            for l in range(DEPTH):
                step = Chain(pool, ev(f"pool_steps{l}"))
                for i in range(NST):
                    pool.wait_ge(ev(f"w_ready{l}"), i + 1)
                    if i >= 2:
                        pool.wait_ge(ev(f"y_done{l}"), i - 1)
                    co, si = cosT[:, i, :], sinT[:, i, :]
                    w0, w1 = w_scan[:, i % 2, 0, :], w_scan[:, i % 2, 1, :]
                    x0, x1 = x_ssm[:, i % 2, 0, :], x_ssm[:, i % 2, 1, :]
                    step(g.tensor_tensor(x0, w0, co, ALU.mult))
                    step(g.tensor_tensor(t_pool, w1, si, ALU.mult))
                    step(g.tensor_tensor(x0, x0, t_pool, ALU.subtract))
                    step(g.tensor_tensor(x1, w0, si, ALU.mult))
                    step(g.tensor_tensor(t_pool, w1, co, ALU.mult))
                    g.tensor_tensor(x1, x1, t_pool, ALU.add).then_inc(ev(f"x_ready{l}"), 1)
                    pool.wait_ge(ev(f"x_ready{l}"), i + 1)

        @block.scalar
        def _(act):
            chain = Chain(act, ev("act_steps"))
            x, meta = a["x"], a["meta_tokens"]
            act.dma_start(xtok[0:N_META, 0, :], meta[:, :]).then_inc(ev("x_loaded"), 16)
            act.dma_start(xtok[N_META:P, 0, :], x[0, 0:P - N_META, :]).then_inc(ev("x_loaded"), 16)
            act.dma_start(xtok[:, 1, :], x[0, P - N_META:2 * P - N_META, :]).then_inc(ev("x_loaded"), 16)
            act.dma_start(xtok[0:N_META, 2, :], x[0, SEQ - N_META:SEQ, :]).then_inc(ev("x_loaded"), 16)

            def param(dst, src):
                act.dma_start(dst, src).then_inc(ev("params_loaded"), 16)

            param(rows_t[0:16, :], a["norm_mix_g"].rearrange("l (k p) -> (l k) p", p=P))
            param(rows_t[16:32, :], a["norm_ffn_g"].rearrange("l (k p) -> (l k) p", p=P))
            param(rows_t[32:34, :], a["diff_subln_g"][:, :])
            param(rows_t[34:38, :], a["ssm_d"].rearrange("l (m g) c -> (l m) (g c)", m=2))
            param(rows_t[38:54, :], a["ssm_lambda_re"].rearrange("l (i g) n -> (l i) (g n)", g=2))
            param(rows_t[54:70, :], a["ssm_lambda_im"].rearrange("l (i g) n -> (l i) (g n)", g=2))
            param(dt_rows[0:16, :], a["ssm_log_dt"].rearrange("l (i g) -> (l i) g", g=2))
            param(fb_t[0:FH, :], a["fox_forget_b"].rearrange("l h -> h l"))
            param(router[:, :, :], a["moe_router"][0, :, :].rearrange("(k p) e -> p k e", p=P))
            for i, n in enumerate(("q1", "k1", "q2", "k2")):
                act.dma_start(lam_v[:, i, :, :], a[f"diff_lambda_{n}"].partition_broadcast(P)).then_inc(ev("lam_loaded"), 16)
            param(sm(320, 1), a["diff_lambda_q1"][0, 0:1].partition_broadcast(P))

            def load_ssm(l):
                if l:
                    act.wait_ge(ev(f"c_blocks{l - 1}"), 1)
                for c, n in enumerate(("re", "im")):
                    act.dma_start(b_raw[:, c, :, :], a[f"ssm_b_{n}"][l, :, :, :].rearrange(
                        "(i g) n c -> (g n) i c", g=2)).then_inc(ev("ssm_loaded"), 16)
                    act.dma_start(c_raw[:, :, c, :], a[f"ssm_c_{n}"][l, :, :, :].rearrange(
                        "(m g) c n -> (g c) m n", m=2)).then_inc(ev("ssm_loaded"), 16)
                act.dma_start(w_glu[:, :, :], a["ssm_w_glu"][l, :, :].rearrange("(k p) n -> p k n", p=P)
                              ).then_inc(ev("glu_loaded"), 16)

            load_ssm(0)

            def squares(n, count):
                act.wait_ge(ev(f"res{n}"), 4)
                if n:
                    act.wait_ge(ev(f"res{n}"), count)
                nc.scalar.activation(sqT[:, 0:4, :], resT[:, 0:4, :], ACT.Square).then_inc(ev(f"squares_act{n}"), 1)

            def copy(dst, src):
                return nc.scalar.activation(dst, src, ACT.Copy)

            def rstd_first(x, event):
                chain(nc.scalar.activation(rs0_t[:, :], x, ACT.Ln, bias=eps_col))
                nc.scalar.activation(rs0_t[:, :], rs0_t[:, :], ACT.Exp, scale=-0.5).then_inc(ev(event), 1)

            def norm_rstd(n):
                rstd_first(take(act, f"ssq{n}")[:, 0:L], f"rstd_first{n}")

            def head_rstd(l, u):
                h = UNITS[u][1]
                b = take(act, f"hn{l}_{h}")
                if h:
                    act.wait_ge(ev(f"diff_out{l}"), h)
                rstd_first(b[:, 0:L], f"head_rstd_first{l}")

            def token_rstd(squares, event):
                act.wait_ge(ev(squares), RT)
                chain(nc.scalar.activation(sm(114, 2), sm(100, 2), ACT.Ln, bias=eps_col, scale=1.0 / D))
                nc.scalar.activation(sm(114, 2), sm(114, 2), ACT.Exp, scale=-0.5).then_inc(ev(event), 1)

            def params_turned():
                b = take(act, "prm")
                release(copy(prm[:, 0:70], b[:, 0:70]), "prm")
                b = take(act, "ldt")
                release(copy(prm[:, 70:86], b[:, 0:16]), "ldt")

            def ssm_tables(l):
                act.wait_ge(ev(f"phases{l}"), 1)
                nc.scalar.activation(sinT, sinT, ACT.Sin, scale=SIN_2PI)
                nc.scalar.activation(cosT, cosT, ACT.Sin, scale=SIN_2PI)
                nc.scalar.activation(sm(0), sm(8), ACT.Sin, scale=SIN_2PI)
                nc.scalar.activation(sm(16), sm(8), ACT.Sin, scale=SIN_2PI / 2).then_inc(ev(f"tables{l}"), 1)

            def ssm_weights(l):
                b = take(act, f"bT{l}")
                release(copy(bT_t[:, :], b[:, :]), f"bT{l}")
                b = take(act, f"cT{l}")
                bv, cv = (v.rearrange("p (m c n) -> p m c n", m=2, c=2) for v in (b[:, :], cT_t[:, :]))
                nc.scalar.activation(cv[:, :, 0, :], bv[:, :, 0, :], ACT.Copy)
                release(nc.scalar.activation(cv[:, :, 1, :], bv[:, :, 1, :], ACT.Copy, scale=-1.0), f"cT{l}")

            def mixer_evac(l):
                for m in range(2):
                    b = take(act, f"z{l}u{m}")
                    release(copy(uT[:, m, :], b[:, 0:L]), f"z{l}u{m}")
                b = take(act, f"z{l}fv0")
                release(copy(vtok[0:P, 0, 512:768], b[0:P, 0:256]), f"z{l}fv0")
                ssm_weights(l)
                for t in (1, 2):
                    b = take(act, f"z{l}fv{t}")
                    qn = TT[t][1]
                    release(copy(vtok[0:qn, t, 512:768], b[0:qn, 0:256]), f"z{l}fv{t}")
                b = take(act, f"z{l}fg")
                release(nc.scalar.activation(fgz[0:FH, :], b[0:FH, 0:L], ACT.Identity, bias=fb_t[0:FH, l:l + 1]),
                        f"z{l}fg")
                for n, dst in (("dq", dqT), ("dk", dkT)):
                    for h in range(DH):
                        b = take(act, f"z{l}{n}{h}")
                        release(copy(dst[:, h, :], b[:, 0:L]), f"z{l}{n}{h}")
                    if n == "dq":
                        act.wait_ge(ev(f"fg_abs{l}"), 1)
                        nc.scalar.activation(fgm[0:FH, :], fgm[0:FH, :], ACT.Exp).then_inc(ev(f"fg_exp{l}"), 1)
                        act.wait_ge(ev(f"fg_exp{l}"), 1)
                        nc.scalar.activation(fgm[0:FH, :], fgm[0:FH, :], ACT.Ln, bias=onesF[0:FH, 0:1]
                                             ).then_inc(ev(f"fg_ln{l}"), 1)
                for t in range(3):
                    b = take(act, f"z{l}dv{t}")
                    qn = TT[t][1]
                    release(copy(vtok[0:qn, t, 0:512], b[0:qn, :]), f"z{l}dv{t}")
                act.wait_ge(ev("fox_select"), 2)
                for i in range(4):
                    b = take(act, f"z{l}fqk{i}")
                    dst, h = (fqa, fka)[i // 2], 2 * (i % 2)
                    copy(dst[0:64, h, :], b[0:64, 0:L])
                    release(copy(dst[0:64, h + 1, :], b[64:P, 0:L]), f"z{l}fqk{i}")

            def gelu(l):
                act.wait_ge(ev(f"gelu_arg{l}"), 1)
                nc.scalar.activation(ye, yq, ACT.Exp, scale=-2.0 * math.sqrt(2.0 / math.pi)).then_inc(ev(f"gelu_exp{l}"), 1)

            def glu(l):
                for m in range(2):
                    b = take(act, f"glu{l}{2 + m}")
                    release(nc.scalar.activation(glu_e[:, m, :], b[:, 0:L], ACT.Exp, scale=-1.0), f"glu{l}{2 + m}")

            def exps(l, u):
                kind, h, t = UNITS[u]
                qn, kmax = TT[t][1], sum(TT[t])
                act.wait_ge(ev(f"scores{l}"), u + 1)
                for m in range(2 if kind == "d" else 1):
                    at = 24 + 4 * (u % 2) + m
                    nc.scalar.activation(e_buf[0:qn, u % 2, m, 0:kmax], s_buf[0:qn, u % 2, m, 0:kmax], ACT.Exp,
                                         bias=small[0:qn, at:at + 1], accum_out=small[0:qn, at + 2:at + 3]
                                         ).then_inc(ev(f"exps{l}{kind}"), 1)

            def probs_evac(l, u):
                t = UNITS[u][2]
                q0, qn = TT[t]
                name = f"at{l}_{u}"
                b = take(act, name)
                hp = (u // 3) % 2
                full = min(t + 1, 2)
                ins = copy(aT[:, hp, 0:full, q0:q0 + qn],
                           b[:, 0:P * full].rearrange("p (k q) -> p k q", q=P)[:, :, 0:qn])
                if t == 2:
                    ins = copy(aT[0:qn, hp, 2, q0:q0 + qn], b[0:qn, 2 * P:2 * P + qn])
                release(ins, name)

            def head_out(l, u):
                kind, h, _ = UNITS[u]
                name = f"o{l}_{u}"
                b = take(act, name)
                if kind == "f":
                    release(copy(mixedT[64 * (h % 2):64 * (h % 2) + 64, 6 + h // 2, :], b[0:64, 0:L]), name)
                    return
                if h >= 2:
                    act.wait_ge(ev(f"diff_out{l}"), h - 1)
                release(copy(o_buf[:, h % 2, :], b[:, 0:L]), name)
                evacuated(act, name)
                nc.scalar.activation(sq_o[:, h % 2, :], o_buf[:, h % 2, :], ACT.Square).then_inc(ev(f"o_square{l}"), 1)

            def attention(l):
                exps(l, 0)
                for u in range(len(UNITS) + 1):
                    if u + 1 < len(UNITS):
                        exps(l, u + 1)
                    if u >= 1 and UNITS[u - 1][2] == 2:
                        head_out(l, u - 1)
                    if u >= 2 and UNITS[u - 2][2] == 2 and UNITS[u - 2][0] == "d":
                        head_rstd(l, u - 2)
                    if u < len(UNITS):
                        probs_evac(l, u)
                    if u == 1:
                        gelu(l)
                    if u == 4:
                        glu(l)

            act.wait_ge(ev("lam_dots"), 4)
            nc.scalar.activation(sm(32, 4), sm(36, 4), ACT.Exp).then_inc(ev("lam_exp"), 1)
            squares(0, 8)
            params_turned()
            norm_rstd(0)
            ssm_tables(0)
            for l in range(DEPTH):
                mixer_evac(l)
                attention(l)
                if l == 0:
                    load_ssm(1)
                    squares(1, 8)
                    norm_rstd(1)
                    for f in range(NFF):
                        b = take(act, f"fa{f}")
                        if f >= 2:
                            evacuated(act, f"fb{f - 2}")
                        nc.scalar.activation(silu_t[:, f % 2, :], b[:, 0:L], ACT.Exp, scale=-1.0
                                             ).then_inc(ev("dense_exp"), 1)
                    ssm_tables(1)
                    squares(2, 8)
                    norm_rstd(2)

            for half in range(2):
                for t in range(RT):
                    b = take(act, f"rt{t}{half}")
                    release(copy(racc[:, t, 512 * half:512 * half + 512], b[:, :]), f"rt{t}{half}")
            act.wait_ge(ev("ssm_out1"), 2)
            act.dma_start(g_ffn_b, a["norm_ffn_g"][1, :].partition_broadcast(P)).then_inc(ev("row_gains"), 16)
            act.dma_start(g_fin_b, a["final_norm_g"].partition_broadcast(P)).then_inc(ev("row_gains"), 16)
            evacuated(act, "rt01")
            evacuated(act, "rt11")
            for t in range(RT):
                nc.scalar.activation(htok[:, t, :], racc[:, t, :], ACT.Square, accum_out=sm(100 + t, 1)
                                     ).then_inc(ev("token_squares"), 1)
            token_rstd("token_squares", "token_rstd_first")
            for j in range(4):
                b = take(act, f"mh{j}")
                release(copy(mhT[:, 2 * j:2 * j + 2, :], b[:, :].rearrange("p (k t) -> p k t", k=2)), f"mh{j}")
            act.wait_ge(ev("margin"), 1)
            nc.scalar.activation(sm(104, 2), sm(106, 2), ACT.Exp).then_inc(ev("margin_exp"), 1)

            def gather_evac():
                ins = copy(hTe[:, 0:4, :], bank[5][:, :].rearrange("p (k s) -> p k s", k=4))
                ins.then_inc(ev("gather_evac"), 1)

            act.wait_ge(ev("gathered"), 1)
            gather_evac()
            act.wait_ge(ev("jobs_ready"), 1)
            n_jobs = act.value_load(ints[0:1, 3:4], min_val=NE, max_val=MAX_JOBS)
            with act.Fori(0, n_jobs) as j:
                def turn_evac(fb):
                    act.wait_ge(ev("turned"), 7 * j + fb + 1)
                    nc.scalar.activation(gTe[:, fb % 2, :], bank[4][:, :], ACT.Copy).then_inc(ev("turn_evac"), 1)

                for fb in range(NFB):
                    act.wait_ge(ev("up_done"), 14 * j + 2 * fb + 1)
                    nc.scalar.activation(e1[:, fb % 2, :], bank[2 * (fb % 2)][:, :], ACT.Exp, scale=-1.0
                                         ).then_inc(ev("silu_exp"), 1)
                    if fb:
                        turn_evac(fb - 1)
                    if fb == 3:
                        act.wait_ge(ev("scat_turned"), j + 1)
                        copy(scat, bank[5][:, 0:SEQ]).then_inc(ev("scat_evac"), 1)
                act.wait_ge(ev("gathered"), 2 * j + 3)
                gather_evac()
                turn_evac(NFB - 1)
                act.wait_ge(mchunk_used, NC * j + NC)
                copy(ysb[:, 0:512], bank[6][:, :]).then_inc(ev("y_evac"), 1)

            act.wait_ge(ev("final_ready"), 1)
            for t in range(RT):
                nc.scalar.activation(htok[:, t, :], racc[:, t, :], ACT.Square, accum_out=sm(100 + t, 1)
                                     ).then_inc(ev("final_squares"), 1)
            token_rstd("final_squares", "final_rstd_first")

        @block.vector
        def _(dve):
            v = nc.vector
            step = Chain(dve, ev("dve_steps"))

            dve.wait_ge(ev("params_loaded"), 16 * N_PARAM)
            dve.wait_ge(ev("constants_ready"), 1)
            for g in range(2):
                ins = v.tensor_copy(dt_wide[0:16, 64 * g:64 * g + 64], dt_rows[0:16, g:g + 1].to_broadcast([16, 64]))
            ins.then_inc(ev("dt_wide_ready"), 1)
            dve.wait_ge(ev("lam_loaded"), 16 * 4)
            step(v.tensor_tensor(lam_v[:, 0, :, :], lam_v[:, 0, :, :], lam_v[:, 1, :, :], ALU.mult))
            step(v.tensor_tensor(lam_v[:, 2, :, :], lam_v[:, 2, :, :], lam_v[:, 3, :, :], ALU.mult))
            for i in range(2):
                for l in range(DEPTH):
                    v.tensor_reduce(sm(36 + 2 * i + l, 1), lam_v[:, 2 * i, l, :], AX.X, ALU.add).then_inc(ev("lam_dots"), 1)
            step(v.tensor_single_scalar(ints[:, 9:10], ints[:, 8:9], 16, ALU.bitwise_and))
            step(v.tensor_copy(sm(42, 1), ints[:, 9:10]))
            step(v.tensor_scalar(sm(41, 1), sm(42, 1), 1.0 / 16, None, ALU.mult))
            step(v.tensor_scalar(sm(40, 1), sm(41, 1), -1.0, 1.0, ALU.mult, ALU.add))
            dve.wait_ge(ev("lam_exp"), 1)
            step(v.tensor_tensor(sm(44, 2), sm(34, 2), sm(32, 2), ALU.subtract))
            for l in range(DEPTH):
                lam_init = 0.8 - 0.6 * math.exp(-0.3 * l)
                step(v.tensor_scalar(sm(44 + l, 1), sm(44 + l, 1), -lam_init, None, ALU.add))
            for k in range(KD):
                b = take(dve, f"xT{k}")
                release(v.tensor_copy(resT[:, k, :], b[:, 0:L]), f"xT{k}")
                evacuated(dve, f"xT{k}")
                dve.sem_inc(ev("res0"), 1)

            def squares(n):
                v.tensor_tensor(sqT[:, 4:8, :], resT[:, 4:8, :], resT[:, 4:8, :], ALU.mult).then_inc(ev(f"squares_dve{n}"), 1)

            def rsqrt(x, name):
                step(v.tensor_tensor(rs_t[:, :], rs0_t[:, :], rs0_t[:, :], ALU.mult))
                release(v.scalar_tensor_tensor(rs_t[:, :], x, EPS, rs_t[:, :], ALU.add, ALU.mult), name)
                evacuated(dve, name)
                step(v.tensor_scalar(rs_t[:, :], rs_t[:, :], -0.5, 1.5, ALU.mult, ALU.add))
                step(v.tensor_tensor(rs_t[:, :], rs_t[:, :], rs0_t[:, :], ALU.mult))

            def normalise(n):
                l, kind = n // 2, n % 2
                b = take(dve, f"ssq{n}")
                dve.wait_ge(ev(f"rstd_first{n}"), 1)
                rsqrt(b[:, 0:L], f"ssq{n}")
                for k in range(KD):
                    col = 16 * kind + 8 * l + k
                    v.scalar_tensor_tensor(hT[:, k, :], resT[:, k, :], prm[:, col:col + 1], rs_t[:, :],
                                           ALU.mult, ALU.mult).then_inc(ev(f"h{n}"), 1)

            def ssm_prepare(l):
                x, k, f, q, dt, lr, li = (sm(120 + 8 * i) for i in range(7))
                e, r, th, cm, ni, den, cr, ci, nr = (sm(176 + 8 * i) for i in range(9))
                lr, li = prm[:, 38 + 8 * l:46 + 8 * l], prm[:, 54 + 8 * l:62 + 8 * l]
                t1, t2 = sm(248), sm(256)
                mag = sm(264)
                step(v.tensor_scalar(x, prm[:, 70 + 8 * l:78 + 8 * l], -87.0, 88.0, ALU.max, ALU.min))
                step(v.tensor_scalar(k, x, 1.0 / math.log(2.0), MAGIC, ALU.mult, ALU.add))
                step(v.tensor_scalar(k, k, -MAGIC, None, ALU.add))
                step(v.scalar_tensor_tensor(f, k, -LN2_HI, x, ALU.mult, ALU.add))
                step(v.scalar_tensor_tensor(f, k, -LN2_LO, f, ALU.mult, ALU.add))
                step(v.tensor_scalar(q, f, 1.0 / math.factorial(7), None, ALU.mult))
                for n in range(6, 0, -1):
                    step(v.scalar_tensor_tensor(q, q, 1.0 / math.factorial(n), f, ALU.add, ALU.mult))
                step(v.tensor_scalar(k, k, 127.0, 8388608.0, ALU.add, ALU.mult))
                step(v.tensor_copy(ints[:, 0:8], k))
                step(v.scalar_tensor_tensor(dt, q, 1.0, ints[:, 0:8].bitcast(F32), ALU.add, ALU.mult))
                step(v.tensor_tensor(r, lr, dt, ALU.mult))
                step(v.tensor_scalar(r, r, -60.0, 60.0, ALU.max, ALU.min))
                step(v.tensor_scalar(r, r, 1.0 / 256, None, ALU.mult))
                step(v.tensor_scalar(e, r, 1.0 / 120, None, ALU.mult))
                for n in (4, 3, 2, 1):
                    step(v.scalar_tensor_tensor(e, e, 1.0 / math.factorial(n), r, ALU.add, ALU.mult))
                for _ in range(8):
                    step(v.scalar_tensor_tensor(e, e, 2.0, e, ALU.add, ALU.mult))
                step(v.tensor_scalar(mag, e, 1.0, None, ALU.add))
                step(v.tensor_tensor(th, li, dt, ALU.mult))
                step(v.tensor_scalar(th, th, 1.0 / (2.0 * math.pi), None, ALU.mult))
                step(v.tensor_scalar(t1, th, MAGIC, -MAGIC, ALU.add, ALU.add))
                step(v.tensor_tensor(sm(8), th, t1, ALU.subtract))
                for i in range(NST):
                    step(v.tensor_scalar(sinT[:, i, :], time_iota, th[:, i:i + 1], None, ALU.mult))
                    step(v.tensor_scalar(cosT[:, i, :], sinT[:, i, :], 0.25, None, ALU.add))
                    for tab in (sinT, cosT):
                        step(v.tensor_scalar(t_dve, tab[:, i, :], MAGIC, -MAGIC, ALU.add, ALU.add))
                        ins = v.tensor_tensor(tab[:, i, :], tab[:, i, :], t_dve, ALU.subtract)
                        if i == NST - 1 and tab is cosT:
                            ins.then_inc(ev(f"phases{l}"), 1)
                        else:
                            step(ins)
                dve.wait_ge(ev(f"tables{l}"), 1)
                step(v.scalar_tensor_tensor(cm, sm(16), -2.0, sm(16), ALU.mult, ALU.mult))
                step(v.tensor_scalar(t1, cm, 1.0, None, ALU.add))
                step(v.tensor_tensor(t1, e, t1, ALU.mult))
                step(v.tensor_tensor(nr, t1, cm, ALU.add))
                step(v.tensor_tensor(ni, mag, sm(0), ALU.mult))
                step(v.tensor_tensor(t1, lr, lr, ALU.mult))
                step(v.tensor_tensor(t2, li, li, ALU.mult))
                step(v.tensor_tensor(den, t1, t2, ALU.add))
                step(v.reciprocal(den, den))
                for o, p0, p1, op in ((cr, nr, ni, ALU.add), (ci, ni, nr, ALU.subtract)):
                    step(v.tensor_tensor(t1, p0, lr, ALU.mult))
                    step(v.tensor_tensor(t2, p1, li, ALU.mult))
                    step(v.tensor_tensor(t1, t1, t2, op))
                    step(v.tensor_tensor(o, t1, den, ALU.mult))
                dve.wait_ge(ev("ssm_loaded"), 64 * (l + 1))
                br, bi = b_raw[:, 0, :, :], b_raw[:, 1, :, :]
                crb, cib = (w.unsqueeze(2).to_broadcast([P, NST, 16]) for w in (cr, ci))
                ta, tb = cut(rs_t, 0, NST, 16), cut(rs_t, P, NST, 16)
                for c, (p0, p1, op) in enumerate(((br, bi, ALU.subtract), (bi, br, ALU.add))):
                    step(v.tensor_tensor(ta, p0, crb, ALU.mult))
                    step(v.tensor_tensor(tb, p1, cib, ALU.mult))
                    for g in range(2):
                        hs = slice(64 * g, 64 * g + 64)
                        step(v.tensor_tensor(b_exp[hs, c, :, 16 * g:16 * g + 16], ta[hs], tb[hs], op))
                dve.sem_inc(ev(f"b_blocks{l}"), 1)
                cflat = c_raw_t[:, :].rearrange("p (i n) -> p i n", n=STATE)
                for g in range(2):
                    step(v.tensor_scalar(c_exp[:, :, 64 * g:64 * g + 64], cflat, sm(40 + g, 1), None, ALU.mult))
                dve.sem_inc(ev(f"c_blocks{l}"), 1)

            def ssm_scan(l, i):
                co, si = cosT[:, i, :], sinT[:, i, :]
                bre = take(dve, f"bu{l}{i}0")[:, 0:L]
                bim = take(dve, f"bu{l}{i}1")[:, 0:L]
                if i >= 2:
                    dve.wait_ge(ev(f"x_ready{l}"), i - 1)
                w0, w1 = w_scan[:, i % 2, 0, :], w_scan[:, i % 2, 1, :]
                v.tensor_tensor(w0, bre, co, ALU.mult)
                step(v.tensor_tensor(t_dve, bim, si, ALU.mult))
                step(v.tensor_tensor(w0, w0, t_dve, ALU.add))
                release(v.tensor_tensor(w1, bim, co, ALU.mult), f"bu{l}{i}1")
                evacuated(dve, f"bu{l}{i}1")
                release(v.tensor_tensor(t_dve, bre, si, ALU.mult), f"bu{l}{i}0")
                evacuated(dve, f"bu{l}{i}0")
                step(v.tensor_tensor(w1, w1, t_dve, ALU.subtract))
                m = sm(264)[:, i:i + 1].to_broadcast([P, L])
                step(v.tensor_tensor_scan(w0, m, w0, 0.0, ALU.mult, ALU.add))
                v.tensor_tensor_scan(w1, m, w1, 0.0, ALU.mult, ALU.add).then_inc(ev(f"w_ready{l}"), 1)
                dve.wait_ge(ev(f"w_ready{l}"), i + 1)

            def forget_gate(l):
                evacuated(dve, f"z{l}fg")
                v.scalar_tensor_tensor(fgm[0:FH, :], fgz[0:FH, :], -1.0, fgz[0:FH, :], ALU.mult, ALU.min).then_inc(ev(f"fg_abs{l}"), 1)

            def decay(l):
                dve.wait_ge(ev(f"fg_ln{l}"), 1)
                step(v.scalar_tensor_tensor(fgz[0:FH, :], fgz[0:FH, :], 0.0, fgm[0:FH, :], ALU.min, ALU.subtract))
                step(v.tensor_tensor_scan(fgc[0:FH, :], ones_row[0:FH, :], fgz[0:FH, :], 0.0, ALU.mult, ALU.add))
                dve.wait_ge(ev("fox_select"), 2)
                c = fgc[0:FH, :].unsqueeze(1).to_broadcast([FH, FH, L])
                v.tensor_scalar(fqa[64:68, :, :], c, 1.0 / SCALE, None, ALU.mult).then_inc(ev(f"decay_rows{l}"), 1)
                v.tensor_scalar(fka[96:100, :, :], c, -1.0, None, ALU.mult).then_inc(ev(f"decay_rows{l}"), 1)
                dve.wait_ge(ev(f"decay_rows{l}"), 2)

            def gelu(l):
                dve.wait_ge(ev(f"y_done{l}"), NST)
                for m in range(2):
                    col = 34 + 2 * l + m
                    step(v.scalar_tensor_tensor(ys[:, m, :], uT[:, m, :], prm[:, col:col + 1], bank[6 + m][:, 0:L],
                                                ALU.mult, ALU.add))
                step(v.tensor_tensor(yq, ys, ys, ALU.mult))
                step(v.tensor_scalar(yq, yq, 0.044715, 1.0, ALU.mult, ALU.add))
                v.tensor_tensor(yq, yq, ys, ALU.mult).then_inc(ev(f"gelu_arg{l}"), 1)

            def gelu_end(l):
                dve.wait_ge(ev(f"gelu_exp{l}"), 1)
                step(v.tensor_scalar(ye, ye, 1.0, None, ALU.add))
                step(v.reciprocal(ye, ye))
                v.tensor_tensor(gy, ys, ye, ALU.mult).then_inc(ev(f"gelu_ready{l}"), 1)

            def glu(l):
                for m in range(2):
                    evacuated(dve, f"glu{l}{2 + m}")
                step(v.tensor_scalar(glu_e, glu_e, 1.0, None, ALU.add))
                step(v.reciprocal(glu_e, glu_e))
                for m in range(2):
                    b = take(dve, f"glu{l}{m}")
                    release(v.tensor_tensor(mixedT[:, m, :], glu_e[:, m, :], b[:, 0:L], ALU.mult), f"glu{l}{m}")
                    evacuated(dve, f"glu{l}{m}")
                    dve.sem_inc(ev(f"ssm_out{l}"), 1)

            def unit_scores(l, u):
                kind, h, t = UNITS[u]
                qn, kmax = TT[t][1], sum(TT[t])
                maps = 2 if kind == "d" else 1
                for m in range(maps):
                    name = f"s{l}_{u}_{m}"
                    b = take(dve, name)
                    release(v.scalar_tensor_tensor(s_buf[0:qn, u % 2, m, 0:kmax], b[0:qn, 0:kmax], SCALE,
                                                   mask[0:qn, t, 0:kmax], ALU.mult, ALU.add), name)
                    evacuated(dve, name)
                at = 24 + 4 * (u % 2)
                v.tensor_reduce(small[0:qn, at:at + maps], s_buf[0:qn, u % 2, 0:maps, 0:kmax], AX.X, ALU.max,
                                negate=True).then_inc(ev(f"scores{l}"), 1)

            def unit_probs(l, u):
                kind, h, t = UNITS[u]
                qn, kmax = TT[t][1], sum(TT[t])
                maps = 2 if kind == "d" else 1
                done = 2 * (u + 1) if kind == "d" else u - 11
                dve.wait_ge(ev(f"exps{l}{kind}"), done)
                if u >= 2:
                    take(dve, f"at{l}_{u - 2}")
                at = 24 + 4 * (u % 2) + 2
                su = small[0:qn, at:at + 2]
                step(v.reciprocal(su[:, 0:maps], su[:, 0:maps]))
                o, e = a_buf[0:qn, u % 2, 0:kmax], e_buf[0:qn, u % 2, :, 0:kmax]
                if kind == "d":
                    step(v.tensor_scalar(su[:, 1:2], su[:, 1:2], sm(44 + l, 1)[0:qn], None, ALU.mult))
                    step(v.tensor_scalar(o, e[:, 0, :], su[:, 0:1], None, ALU.mult))
                    ins = v.scalar_tensor_tensor(o, e[:, 1, :], su[:, 1:2], o, ALU.mult, ALU.add)
                else:
                    ins = v.tensor_scalar(o, e[:, 0, :], su[:, 0:1], None, ALU.mult)
                ins.then_inc(ev(f"probs{l}"), 1)

            def head_norm(l, h):
                b = take(dve, f"hn{l}_{h}")
                dve.wait_ge(ev(f"head_rstd_first{l}"), h + 1)
                rsqrt(b[:, 0:L], f"hn{l}_{h}")
                v.scalar_tensor_tensor(mixedT[:, 2 + h, :], o_buf[:, h % 2, :], sm(46 + l, 1), rs_t[:, :],
                                       ALU.mult, ALU.mult).then_inc(ev(f"diff_out{l}"), 1)
                dve.wait_ge(ev(f"diff_out{l}"), h + 1)

            def attention(l):
                gelu(l)
                unit_scores(l, 0)
                for u in range(len(UNITS) + 2):
                    if u + 1 < len(UNITS):
                        unit_scores(l, u + 1)
                    if u < len(UNITS):
                        unit_probs(l, u)
                    if u >= 2 and UNITS[u - 2][2] == 2 and UNITS[u - 2][0] == "d":
                        head_norm(l, UNITS[u - 2][1])
                    if u == 2:
                        gelu_end(l)
                    if u == 5:
                        glu(l)

            def dense():
                for f in range(NFF):
                    dve.wait_ge(ev("dense_exp"), f + 1)
                    s = silu_t[:, f % 2, :]
                    step(v.tensor_scalar(s, s, 1.0, None, ALU.add))
                    step(v.reciprocal(s, s))
                    ba = take(dve, f"fa{f}")
                    release(v.tensor_tensor(s, s, ba[:, 0:L], ALU.mult), f"fa{f}")
                    evacuated(dve, f"fa{f}")
                    bb = take(dve, f"fb{f}")
                    release(v.tensor_tensor(gT[:, f, :], s, bb[:, 0:L], ALU.mult), f"fb{f}")
                    evacuated(dve, f"fb{f}")

            def add_residual(prefix, n):
                for k in range(KD):
                    b = take(dve, f"{prefix}{k}")
                    release(v.tensor_tensor(resT[:, k, :], resT[:, k, :], b[:, 0:L], ALU.add), f"{prefix}{k}")
                    evacuated(dve, f"{prefix}{k}")
                    dve.sem_inc(ev(f"res{n}"), 1)

            squares(0)
            evacuated(dve, "prm")
            evacuated(dve, "ldt")
            for l in range(DEPTH):
                lam_init = 0.8 - 0.6 * math.exp(-0.3 * l)
                step(v.tensor_scalar(sm(46 + l, 1), prm[:, 32 + l:33 + l], 1.0 - lam_init, None, ALU.mult))
            normalise(0)
            dve.wait_ge(ev("h0"), KD)
            ssm_prepare(0)
            for l in range(DEPTH):
                for i in range(NST):
                    ssm_scan(l, i)
                    if i == 2:
                        forget_gate(l)
                decay(l)
                attention(l)
                if l == 0:
                    add_residual("r0", 1)
                    squares(1)
                    normalise(1)
                    dense()
                    ssm_prepare(1)
                    add_residual("y", 2)
                    squares(2)
                    normalise(2)
                    dve.wait_ge(ev("h2"), KD)

            def token_rstd(step, event):
                dve.wait_ge(ev(event), 1)
                step(v.tensor_scalar(sm(116, 2), sm(100, 2), 1.0 / D, EPS, ALU.mult, ALU.add))
                step(v.tensor_tensor(sm(116, 2), sm(116, 2), sm(114, 2), ALU.mult))
                step(v.tensor_tensor(sm(116, 2), sm(116, 2), sm(114, 2), ALU.mult))
                step(v.tensor_scalar(sm(116, 2), sm(116, 2), -0.5, 1.5, ALU.mult, ALU.add))
                step(v.tensor_tensor(sm(102, 2), sm(116, 2), sm(114, 2), ALU.mult))

            token_rstd(step, "token_rstd_first")
            dve.wait_ge(ev("row_gains"), 32)
            for t in range(RT):
                v.scalar_tensor_tensor(htok[:, t, :], racc[:, t, :], sm(102 + t, 1), g_ffn_b, ALU.mult, ALU.mult
                                       ).then_inc(ev("htok"), 1)
            lg, gate, chosen, pos = sm(272, 16), sm(288, 16), sm(48, 16), sm(64, 16)
            eq, cs, sel1, sel2 = sm(304, 16), sm(120, 16), sm(136, 16), sm(152, 16)
            m1, m2 = sm(168, 2), sm(170, 2)
            g1, g2, den = sm(108, 2), sm(110, 2), sm(112, 2)

            def two(w):
                return w.rearrange("p (t e) -> p t e", t=RT)

            for t in range(RT):
                b = take(dve, f"lg{t}")
                release(v.tensor_copy(lg[:, NE * t:NE * t + NE], b[:, 0:NE]), f"lg{t}")
                evacuated(dve, f"lg{t}")

            def first_largest(best, pick):
                step(v.tensor_reduce(best, two(lg), AX.X, ALU.max))
                step(v.tensor_tensor(two(eq), two(lg), best.unsqueeze(2).to_broadcast([P, RT, NE]), ALU.is_equal))
                for t in range(RT):
                    w = slice(NE * t, NE * t + NE)
                    step(v.tensor_tensor_scan(cs[:, w], ones_row[:, 0:NE], eq[:, w], 0.0, ALU.mult, ALU.add))
                step(v.scalar_tensor_tensor(pick, cs, 1.0, eq, ALU.is_equal, ALU.mult))

            first_largest(m1, sel1)
            step(v.scalar_tensor_tensor(lg, sel1, NEG, lg, ALU.mult, ALU.add))
            first_largest(m2, sel2)
            v.tensor_tensor(sm(106, 2), m2, m1, ALU.subtract).then_inc(ev("margin"), 1)
            v.tensor_tensor(chosen, sel1, sel2, ALU.add).then_inc(ev("chosen"), 1)
            dve.wait_ge(ev("chosen"), 1)
            dve.wait_ge(ev("margin_exp"), 1)
            step(v.tensor_scalar(den, sm(104, 2), 1.0, None, ALU.add))
            step(v.reciprocal(g1, den))
            step(v.tensor_tensor(g2, g1, sm(104, 2), ALU.mult))
            for t in range(RT):
                w = slice(NE * t, NE * t + NE)
                step(v.tensor_scalar(gate[:, w], sel1[:, w], g1[:, t:t + 1], None, ALU.mult))
                step(v.scalar_tensor_tensor(gate[:, w], sel2[:, w], g2[:, t:t + 1], gate[:, w], ALU.mult, ALU.add))
            for t in range(RT):
                w = slice(NE * t, NE * t + NE)
                b = take(dve, f"rank{t}")
                release(v.scalar_tensor_tensor(pos[:, w], b[:, 0:NE], 1.0, chosen[:, w], ALU.add, ALU.mult), f"rank{t}")
                evacuated(dve, f"rank{t}")
            step(v.tensor_scalar(pos, pos, -1.0, None, ALU.add))
            jpos_t, jgate_t = sb("job_place", RT * 12), sb("job_gate", RT * 12)
            jpos, jgate = cut(jpos_t, 0, RT, 12), cut(jgate_t, 0, RT, 12)
            step(v.tensor_copy(jpos[:, :, 0:NE], two(pos)))
            step(v.tensor_copy(jgate[:, :, 0:NE], two(gate)))
            step(v.memset(jpos[:, :, NE:12], -1.0e6))
            step(v.memset(jgate[:, :, NE:12], 0.0))
            full, before, pick, tmp, row = (sm(176 + 8 * i) for i in range(5))
            b = take(dve, "count")
            release(v.tensor_scalar(full, b[:, 0:NE], float(P), None, ALU.is_gt), "count")
            evacuated(dve, "count")
            step(v.tensor_tensor_scan(before, ones_row[:, 0:NE], full, 0.0, ALU.mult, ALU.add))
            step(v.tensor_scalar(row[:, 3:4], before[:, NE - 1:NE], float(NE), None, ALU.add))
            wide = eq
            for n in range(3):
                step(v.scalar_tensor_tensor(pick, before, float(n + 1), full, ALU.is_equal, ALU.mult))
                step(v.tensor_tensor(tmp, pick, expert_iota, ALU.mult))
                step(v.tensor_reduce(row[:, n:n + 1], tmp, AX.X, ALU.add))
                step(v.tensor_reduce(sm(232, 1), pick, AX.X, ALU.add))
                step(v.tensor_scalar(sm(232, 1), sm(232, 1), -1.0, 1.0e6, ALU.add, ALU.mult))
                pb = pick.unsqueeze(1).to_broadcast([P, RT, NE])
                step(v.scalar_tensor_tensor(two(wide), two(pos), -float(P), pb, ALU.add, ALU.mult))
                step(v.tensor_reduce(jpos[:, :, NE + n], two(wide), AX.X, ALU.add))
                step(v.tensor_scalar(jpos[:, :, NE + n], jpos[:, :, NE + n], sm(232, 1), None, ALU.add))
                step(v.tensor_tensor(two(wide), two(gate), pb, ALU.mult))
                step(v.tensor_reduce(jgate[:, :, NE + n], two(wide), AX.X, ALU.add))
            v.tensor_copy(ints[:, 0:4], row[:, 0:4]).then_inc(ev("jobs_ready"), 1)
            dve.wait_ge(ev("jobs_ready"), 1)

            cur_t = sb("current_job", 8)
            moe_step = Chain(dve, ev("expert_steps"))

            def select(j):
                moe_step(v.tensor_copy(cur_t[:, 0:2], jpos[:, :, bass.ds(j, 1)] if not isinstance(j, int)
                                       else jpos[:, :, j:j + 1]))
                for t in range(RT):
                    ins = v.tensor_scalar(sel[:, t, :], slot_iota, cur_t[:, t:t + 1], None, ALU.is_equal)
                ins.then_inc(ev("sel_ready"), 1)

            def gather_evac(n):
                dve.wait_ge(ev("gathered"), n)
                v.tensor_copy(hTe[:, 4:8, :], bank[4][:, :].rearrange("p (k s) -> p k s", k=4)
                              ).then_inc(ev("gather_evac"), 1)

            dve.sem_inc(ev("added"), 1)
            select(0)
            first = moe_step.n
            gather_evac(2)
            n_jobs = dve.value_load(ints[0:1, 3:4], min_val=NE, max_val=MAX_JOBS)
            STEPS = 3 + 3 * NFB
            with dve.Fori(0, n_jobs) as j:
                moe_step.base, moe_step.n = STEPS * j + first, 0
                moe_step(v.tensor_copy(cur_t[:, 2:4], jpos[:, :, bass.ds(j, 1)]))
                moe_step(v.tensor_copy(cur_t[:, 4:6], jgate[:, :, bass.ds(j, 1)]))
                for t in range(RT):
                    ins = v.tensor_scalar(selg[:, t, :], slot_iota, cur_t[:, 2 + t:3 + t], cur_t[:, 4 + t:5 + t],
                                          ALU.is_equal, ALU.mult)
                ins.then_inc(ev("selg_ready"), 1)
                for fb in range(NFB):
                    dve.wait_ge(ev("silu_exp"), 7 * j + fb + 1)
                    s = e1[:, fb % 2, :]
                    moe_step(v.tensor_scalar(s, s, 1.0, None, ALU.add))
                    moe_step(v.reciprocal(s, s))
                    moe_step(v.tensor_tensor(s, s, bank[2 * (fb % 2)][:, :], ALU.mult))
                    dve.wait_ge(ev("up_done"), 14 * j + 2 * fb + 2)
                    v.tensor_tensor(g_e[:, fb % 2, :], s, bank[2 * (fb % 2) + 1][:, :], ALU.mult
                                    ).then_inc(ev("g_ready"), 1)
                    if fb == 4:
                        select(j + 1)
                assert moe_step.n == STEPS
                gather_evac(2 * j + 4)
                dve.wait_ge(mchunk_used, NC * j + NC)
                v.tensor_copy(ysb[:, 512:D], bank[7][:, :]).then_inc(ev("y_evac"), 1)
                for i in range(4):
                    r = racc[:, i // 2, 512 * (i % 2):512 * (i % 2) + 512]
                    dve.wait_ge(ev("scattered"), 4 * j + i + 1)
                    v.tensor_tensor(r, r, bank[i][:, :], ALU.add).then_inc(ev("added"), 1)
                dve.wait_ge(ev("added"), 4 * j + 5)

            end = Chain(dve, ev("final_steps"))
            dve.sem_inc(ev("final_ready"), 1)
            token_rstd(end, "final_rstd_first")
            for t in range(RT):
                v.scalar_tensor_tensor(racc[:, t, :], racc[:, t, :], sm(102 + t, 1), g_fin_b, ALU.mult, ALU.mult
                                       ).then_inc(ev("out_ready"), 1)


_INS = ["x", "meta_tokens", "norm_mix_g", "w_in", "w_out", "ssm_lambda_re", "ssm_lambda_im", "ssm_log_dt",
        "ssm_b_re", "ssm_b_im", "ssm_c_re", "ssm_c_im", "ssm_d", "ssm_w_glu", "diff_lambda_q1", "diff_lambda_k1",
        "diff_lambda_q2", "diff_lambda_k2", "diff_subln_g", "fox_forget_b", "norm_ffn_g", "dense_w1", "dense_w3",
        "dense_w2", "moe_router", "moe_w1", "moe_w3", "moe_w2", "final_norm_g"]


def kernel(**inputs):
    import numpy as _np
    import concourse.bacc as _bacc
    from concourse import mybir as _mybir
    from concourse.bass_utils import run_bass_kernel_spmd as _run

    nc = _bacc.Bacc("TRN2", target_bir_lowering=False, num_devices=1)
    arrays, args = {}, {}
    for name in _INS:
        x = _np.ascontiguousarray(inputs[name])
        arrays[f"in_{name}"] = x
        args[name] = nc.dram_tensor(f"in_{name}", x.shape, _mybir.dt.from_np(x.dtype), kind="ExternalInput").ap()
    out = nc.dram_tensor("out_0", (1, SEQ, D), _mybir.dt.float32, kind="ExternalOutput").ap()
    build(nc, args, out)
    r = _run(nc, [arrays], core_ids=[0])
    return r.results[0]["out_0"]
```

```python
import math

import concourse.bass as bass
from concourse import mybir
from contextlib import ExitStack

F32 = mybir.dt.float32
I32 = mybir.dt.int32
F32R = mybir.dt.float32r
ALU = mybir.AluOpType
ACT = mybir.ActivationFunctionType
AX = mybir.AxisListType

P = 128
DEPTH = 2
D = 1024
KD = D // P
N_META, SEQ = 16, 256
L = N_META + SEQ
TT = [(0, 128), (128, 128), (256, 16)]
RT = SEQ // P
EPS = 1e-6
SSM_W, SSM_C, STATE = 256, 16, 64
NST = 8
DH, DQK, DV = 4, 64, 128
FH, FD = 4, 64
FF = 2816
NFF = FF // P
NE, FE = 8, 3584
NFB = FE // 512
MAX_JOBS = 11
SCALE = DQK ** -0.5
MAGIC = 12582912.0
LN2_HI, LN2_LO = 0.693359375, -2.12194440e-4
SIN_2PI = 6.2831850
NEG = -1.0e30
SLOT = 4096
RING = 5
HALF = SLOT // 2
MRING, SPLITS = 7, 3
UNITS = [(k, h, t) for k in ("d", "f") for h in range(4) for t in range(3)]


def build(nc, a, out):
    ctx = ExitStack()
    with ctx:
        ctx.enter_context(nc.allow_non_contiguous_dma(reason="small parameter loads"))

        def sb(name, cols, dt=F32):
            return ctx.enter_context(nc.sbuf_tensor(name, [P, cols], dt))

        ring_at = -(-nc.sbuf_base // 32) * 32
        ring = sb("weight_ring", RING * SLOT)
        late = sb("late_region", 2 * SLOT)
        res_at = ring_at + 4 * (RING + 2) * SLOT
        region = {n: sb(n, KD * L) for n in ("resT", "mixedT", "hT", "cosT", "sinT", "foxqk")}
        attn = sb("attn_temps", 2720)
        bank = [ctx.enter_context(nc.psum_tensor(f"bank{i}", [P, 512], F32)) for i in range(8)]

        def cut(tensor, start, *dims):
            n = math.prod(dims)
            v = tensor[:, start:start + n]
            if len(dims) == 2:
                v = v.rearrange("p (a b) -> p a b", b=dims[1])
            if len(dims) == 3:
                v = v.rearrange("p (a b c) -> p a b c", b=dims[1], c=dims[2])
            return v

        resT, hT, mixedT = (cut(region[n], 0, KD, L) for n in ("resT", "hT", "mixedT"))
        cosT, sinT = (cut(region[n], 0, NST, L) for n in ("cosT", "sinT"))
        fqa, fka = cut(region["foxqk"], 0, FH, L), cut(region["foxqk"], FH * L, FH, L)
        sqT = mixedT
        dqT, dkT = cut(late, 0, DH, L), cut(late, 1088, DH, L)
        uT = cut(late, 2176, 2, L)
        vtok = cut(late, 2720, 3, 768)
        w_scan = cut(late, 5024, 2, 2, L)
        x_ssm = cut(late, 6112, 2, 2, L)
        t_dve, t_pool = cut(late, 7200, L), cut(late, 7472, L)
        gT = cut(late, 0, NFF, L)
        silu_t = cut(late, NFF * L, 2, L)
        xtok = cut(late, 0, 3, D)
        s_buf = [cut(attn, 0, 2, L), cut(attn, 544, 2, L), cut(region["sinT"], 1088, 2, L)]
        e_buf = [cut(attn, 1088, 2, L), cut(attn, 1632, 2, L), cut(region["sinT"], 544, 2, L)]
        a_buf = cut(attn, 2176, 2, L)
        aT = cut(late, 5024, 2, 3, L)
        o_buf_t, sq_o_t, rs_t = sb("o_buf", 2 * L), sb("o_square", 2 * L), sb("rstd", L)
        rs0_t = sb("rstd_first", L)
        o_buf, sq_o = cut(o_buf_t, 0, 2, L), cut(sq_o_t, 0, 2, L)
        fgz, fgm, fgc = (cut(attn, i * L, L) for i in range(3))
        ys, yq, ye, gy = (cut(region["cosT"], i * 544, 2, L) for i in range(4))
        glu_e = cut(region["sinT"], 0, 2, L)
        racc = cut(region["foxqk"], 0, RT, D)
        mhT = cut(region["hT"], 0, KD, SEQ)
        htok = cut(region["cosT"], 0, RT, D)
        g_ffn_b, g_fin_b = cut(region["sinT"], 0, D), cut(region["sinT"], D, D)
        ysb = cut(region["hT"], 0, D)
        def split_pair(name, at, *dims):
            n = math.prod(dims)
            pair = []
            for i, part in enumerate(("hi", "lo")):
                t = nc.alloc_sbuf_tensor_at(f"{name}_{part}", [P, n], F32R, offset=at + 4 * n * i)
                pair.append(t[:, :].rearrange("p (a b) -> p a b", b=dims[-1]))
            return pair

        w_hi, w_lo = split_pair("weights", ring_at + 4 * MRING * HALF, SPLITS, HALF)
        gT_hi, gT_lo = split_pair("expert_gT", res_at, 2, 512)
        h_hi, h_lo = split_pair("expert_hT", res_at + 4 * KD * L, KD, P)
        e1, g_e = cut(attn, 0, 2, 512), cut(region["hT"], 1024, 2, 512)
        sel, selg, scat = cut(attn, 1024, RT, P), cut(attn, 1280, RT, P), cut(attn, 1536, SEQ)
        const_t = sb("constants", 6 * P + 2 * L + 9)
        ident, avgD, avgV, onesF, tri, slot_iota = (cut(const_t, i * P, P) for i in range(6))
        time_iota, ones_row = cut(const_t, 6 * P, L), cut(const_t, 6 * P + L, L)
        expert_iota = cut(const_t, 6 * P + 2 * L, 8)
        eps_col = cut(const_t, 6 * P + 2 * L + 8, 1)
        mask_t = sb("causal_mask", 3 * L)
        mask = cut(mask_t, 0, 3, L)
        rows_t, prm_t = sb("param_rows", P), sb("param_cols", 70 + 16)
        prm = prm_t
        dt_rows, dt_wide = sb("dt_rows", 2), sb("dt_wide", P)
        b_raw_t, c_raw_t = sb("b_raw", 2 * NST * 16), sb("c_raw", 4 * STATE)
        b_raw, c_raw = cut(b_raw_t, 0, 2, NST, 16), cut(c_raw_t, 0, 2, 2, STATE)
        b_exp_t, c_exp_t = sb("b_blocks", 512), sb("c_blocks", 512)
        b_exp, c_exp = cut(b_exp_t, 0, 2, NST, 32), cut(c_exp_t, 0, 4, P)
        bT_t, cT_t = sb("bT", 512), sb("cT", 512)
        bT, cT = cut(bT_t, 0, 2, 2, P), cut(cT_t, 0, 2, 2, P)
        glu_t = sb("w_glu", 1024)
        w_glu = cut(glu_t, 0, 2, 512)
        lam_t = sb("lambda_vectors", 4 * 2 * 64)
        lam_v = cut(lam_t, 0, 4, 2, 64)
        fb_t = sb("forget_bias", 2)
        router_t = sb("router", KD * NE)
        router = cut(router_t, 0, KD, NE)
        small = sb("small", 340)
        ints = sb("ints", 20, I32)

        def sm(i, n=8):
            return small[:, i:i + n]

        events = {}

        def ev(name):
            if name not in events:
                events[name] = ctx.enter_context(nc.semaphore(name))
            return events[name]

        bank_full = [ctx.enter_context(nc.semaphore(f"bank_full{b}")) for b in range(6)]
        bank_free = [ctx.enter_context(nc.semaphore(f"bank_free{b}")) for b in range(6)]
        slot_full = [ctx.enter_context(nc.semaphore(f"slot_full{s}")) for s in range(RING)]
        chunk_used = ctx.enter_context(nc.semaphore("chunk_used"))
        mslot_full = [ctx.enter_context(nc.semaphore(f"expert_slot_full{s}")) for s in range(MRING)]
        mchunk_used = ctx.enter_context(nc.semaphore("expert_chunk_used"))
        groups = {}

        def open_group(pe, name):
            n = len(groups)
            groups[name] = (n % 6, n // 6)
            if n >= 6:
                pe.wait_ge(bank_free[n % 6], n // 6)
            return bank[n % 6]

        def close_group(ins, name):
            ins.then_inc(bank_full[groups[name][0]], 1)

        def take(eng, name):
            b, use = groups[name]
            eng.wait_ge(bank_full[b], use + 1)
            return bank[b]

        def release(ins, name):
            ins.then_inc(bank_free[groups[name][0]], 1)

        def evacuated(eng, name):
            b, use = groups[name]
            eng.wait_ge(bank_free[b], use + 1)

        class Chain:

            def __init__(self, eng, sem):
                self.eng, self.sem, self.base, self.n = eng, sem, 0, 0

            def __call__(self, ins):
                self.n += 1
                ins.then_inc(self.sem, 1)
                self.eng.wait_ge(self.sem, self.base + self.n)

        chunks = []

        def chunk(name, src, k, cols):
            v = ring[:, (len(chunks) % RING) * SLOT:(len(chunks) % RING) * SLOT + k * cols]
            chunks.append((name, src, v.rearrange("p (k n) -> p k n", n=cols)))

        for l in range(DEPTH):
            w_in = a["w_in"][l, :, :].rearrange("(k p) n -> p k n", p=P)
            for name, lo, hi in (("u", 0, 256), ("fvg", 2304, 2564), ("dq", 256, 768), ("dk", 768, 1280),
                                 ("dv", 1280, 1792), ("fqk", 1792, 2304)):
                chunk(f"{name}{l}", w_in[:, :, lo:hi], KD, hi - lo)
            w_out = a["w_out"][l, :, :].rearrange("(k p) n -> p k n", p=P)
            for half in range(2):
                chunk(f"out{l}{half}", w_out[:, :, 512 * half:512 * half + 512], KD, 512)
            if l == 0:
                w1, w3 = (a[n][0, :, :].rearrange("(k p) n -> p k n", p=P) for n in ("dense_w1", "dense_w3"))
                w2 = a["dense_w2"][0, :, :].rearrange("(k p) n -> p k n", p=P)
                for fb in range(0, FF, 512):
                    n = min(512, FF - fb)
                    chunk(f"w1_{fb}", w1[:, :, fb:fb + n], KD, n)
                    chunk(f"w3_{fb}", w3[:, :, fb:fb + n], KD, n)
                for half in range(2):
                    for f in range(0, NFF, 8):
                        n = min(8, NFF - f)
                        chunk(f"w2_{half}_{f}", w2[:, f:f + n, 512 * half:512 * half + 512], n, 512)
        where = {c[0]: i for i, c in enumerate(chunks)}

        def chunk_ready(pe, name):
            i = where[name]
            pe.wait_ge(slot_full[i % RING], 16 * (i // RING + 1))
            return chunks[i][2]

        order = [(0, "w1"), (0, "w3")]
        for fb in range(1, NFB):
            order += [(fb, "w1"), (fb, "w3"), (fb - 1, "w2")]
        order += [(NFB - 1, "w2")]
        NC = 2 * len(order)
        assert NC % MRING == 0 and NC % SPLITS == 0

        def mslot(c):
            return ring[:, (c % MRING) * HALF:(c % MRING) * HALF + HALF]

        def expert_chunk(e, c):
            (fb, kind), half = order[c // 2], c % 2
            if kind == "w2":
                lo = 512 * fb + 256 * half
                src = a["moe_w2"][0, e, lo:lo + 256, :].rearrange("(k p) n -> p k n", p=P)
                return src, mslot(c).rearrange("p (k n) -> p k n", n=D)
            src = a[f"moe_{kind}"][0, e, 512 * half:512 * half + 512, 512 * fb:512 * fb + 512]
            return src.rearrange("(k p) n -> p k n", p=P), mslot(c).rearrange("p (k n) -> p k n", n=512)

        def last_chunk(fb, kind):
            return 2 * order.index((fb, kind)) + 1

        silu_after = {last_chunk(fb, "w1"): fb for fb in range(NFB)}
        gate_after = {last_chunk(fb, "w3"): fb for fb in range(NFB)}
        turn_after = {last_chunk(fb + 1, "w1"): fb for fb in range(NFB - 1)}
        FIRST_DOWN = last_chunk(0, "w2") - 1
        SCATTER_AFTER = last_chunk(3, "w3") + 1
        GATHER_AFTER = NC - 3

        N_PARAM = 10
        EARLY = 12
        SSM_AT = [{5: 0, 7: 1, 8: 2, 10: 3, 11: 4}, {0: 0, 1: 1, 3: 2, 4: 3, 6: 4, 7: 5, 9: 6, 10: 7}]

        def phase_tile(engine, step, i, tmp):
            step(engine.tensor_scalar(sinT[:, i, :], time_iota, sm(192)[:, i:i + 1], None, ALU.mult))
            step(engine.tensor_scalar(cosT[:, i, :], sinT[:, i, :], 0.25, None, ALU.add))
            for tab in (sinT, cosT):
                step(engine.tensor_scalar(tmp, tab[:, i, :], MAGIC, -MAGIC, ALU.add, ALU.add))
                step(engine.tensor_tensor(tab[:, i, :], tab[:, i, :], tmp, ALU.subtract))

        block = ctx.enter_context(nc.Block())

        @block.tensor
        def _(pe):
            def mm(o, lhsT, rhs, start, stop):
                return nc.tensor.matmul(o, lhsT, rhs, start=start, stop=stop)

            def done_with_chunk(ins):
                ins.then_inc(chunk_used, 1)

            def transposed_params():
                pe.wait_ge(ev("identity_ready"), 2)
                pe.wait_ge(ev("params_loaded"), 16 * N_PARAM)
                b = open_group(pe, "prm")
                close_group(nc.tensor.transpose(b[:, 0:70], rows_t[0:70, :], ident[0:70, 0:70]), "prm")
                pe.wait_ge(ev("dt_wide_ready"), 1)
                b = open_group(pe, "ldt")
                close_group(nc.tensor.transpose(b[:, 0:16], dt_wide[0:16, :], ident[0:16, 0:16]), "ldt")

            def ssm_weights(l):
                pe.wait_ge(ev(f"b_blocks{l}"), 1)
                b = open_group(pe, f"bT{l}")
                for m in range(2):
                    for c in range(2):
                        ins = nc.tensor.transpose(b[:, (2 * m + c) * P:(2 * m + c + 1) * P],
                                                  b_exp[:, c, 4 * m:4 * m + 4, :], ident)
                close_group(ins, f"bT{l}")
                pe.wait_ge(ev(f"c_blocks{l}"), 1)
                b = open_group(pe, f"cT{l}")
                for i in range(4):
                    ins = nc.tensor.transpose(b[:, i * P:(i + 1) * P], c_exp[:, i, :], ident)
                close_group(ins, f"cT{l}")

            def feature_norm(n):
                b = open_group(pe, f"ssq{n}")
                for k in range(KD):
                    if k == 0:
                        pe.wait_ge(ev("constants_ready"), 1)
                        pe.wait_ge(ev(f"squares_act{n}"), 1)
                    if k == KD // 2:
                        pe.wait_ge(ev(f"squares_dve{n}"), 1)
                    ins = mm(b[:, 0:L], avgD, sqT[:, k, :], k == 0, k == KD - 1)
                close_group(ins, f"ssq{n}")

            def project(n, name, w, lo, m, rhs_ready):
                b = open_group(pe, name)
                for k in range(KD):
                    if rhs_ready:
                        pe.wait_ge(ev(f"h{n}"), k + 1)
                    ins = mm(b[0:m, 0:L], w[:, k, lo:lo + m], hT[:, k, :], k == 0, k == KD - 1)
                close_group(ins, name)
                return ins

            def ssm_in(l, i):
                r = i % 4
                if i == 0:
                    evacuated(pe, f"bT{l}")
                    evacuated(pe, f"z{l}u1")
                for c in range(2):
                    name = f"bu{l}{i}{c}"
                    b = open_group(pe, name)
                    close_group(mm(b[:, 0:L], bT[32 * r:32 * r + 32, i // 4, c, :],
                                   uT[32 * r:32 * r + 32, i // 4, :], True, True), name)

            def ssm_out(l, i):
                r, m = i % 4, i // 4
                if i == 0:
                    evacuated(pe, f"cT{l}")
                pe.wait_ge(ev(f"x_ready{l}"), i + 1)
                for c in range(2):
                    ins = mm(bank[6 + m][32 * r:32 * r + 32, 0:L], cT[:, m, c, 32 * r:32 * r + 32],
                             x_ssm[:, i % 2, c, :], c == 0, c == 1)
                ins.then_inc(ev(f"y_done{l}"), 1)

            def mixer_inputs(l, n):
                steps = []

                def feature(cname, key, cols, last):
                    def f(key=key, cols=cols, last=last):
                        w = chunk_ready(pe, f"{cname}{l}")
                        ins = project(n, f"z{l}{key}", w, cols[0], cols[1], False)
                        if last:
                            pe.wait_ge(bank_full[groups[f"z{l}{key}"][0]], groups[f"z{l}{key}"][1] + 1)
                            pe.sem_inc(chunk_used, 1)
                    steps.append(f)

                def tokens(cname, key, cols, t, last):
                    def f():
                        w = chunk_ready(pe, f"{cname}{l}")
                        q0, qn = TT[t]
                        name = f"z{l}{key}{t}"
                        b = open_group(pe, name)
                        for k in range(KD):
                            ins = mm(b[0:qn, 0:cols], hT[:, k, q0:q0 + qn], w[:, k, 0:cols], k == 0, k == KD - 1)
                        close_group(ins, name)
                        if last:
                            pe.wait_ge(bank_full[groups[name][0]], groups[name][1] + 1)
                            pe.sem_inc(chunk_used, 1)
                    steps.append(f)

                w = chunk_ready(pe, f"u{l}")
                for m in range(2):
                    ins = project(n, f"z{l}u{m}", w, P * m, P, m == 0)
                name = f"z{l}u1"
                pe.wait_ge(bank_full[groups[name][0]], groups[name][1] + 1)
                pe.sem_inc(chunk_used, 1)
                for t in range(3):
                    tokens("fvg", "fv", 256, t, False)
                feature("fvg", "fg", (256, FH), True)
                for cname in ("dq", "dk"):
                    for h in range(DH):
                        feature(cname, f"{cname}{h}", (P * h, P), h == DH - 1)
                for t in range(3):
                    tokens("dv", "dv", 512, t, t == 2)
                for i in range(4):
                    feature("fqk", f"fqk{i}", (P * i, P), i == 3)
                def tile_of_states(i):
                    if i == 0:
                        ssm_weights(l)
                    ssm_in(l, i)
                    if i >= 2:
                        ssm_out(l, i - 2)

                for j in range(EARLY):
                    steps[j]()
                    if j in SSM_AT[l]:
                        tile_of_states(SSM_AT[l][j])
                for i in range(len(SSM_AT[l]), NST):
                    tile_of_states(i)
                return steps[EARLY:]

            def scores(l, u):
                kind, h, t = UNITS[u]
                (q0, qn), kmax = TT[t], sum(TT[t])
                if u == 0:
                    evacuated(pe, f"z{l}dk3")
                    evacuated(pe, f"z{l}dq3")
                if kind == "f" and h == 0 and t == 0:
                    evacuated(pe, f"z{l}fqk3")
                    pe.wait_ge(ev(f"decay_rows{l}"), 2)
                for m in range(2 if kind == "d" else 1):
                    name = f"s{l}_{u}_{m}"
                    b = open_group(pe, name)
                    if kind == "d":
                        q, k = (x[64 * m:64 * m + 64, h, :] for x in (dqT, dkT))
                    else:
                        q, k = fqa[0:100, h, :], fka[0:100, h, :]
                    close_group(mm(b[0:qn, 0:kmax], q[:, q0:q0 + qn], k[:, 0:kmax], True, True), name)

            def turn_probs(l, u):
                _, _, t = UNITS[u]
                q0, qn = TT[t]
                pe.wait_ge(ev(f"probs{l}"), u + 1)
                name = f"at{l}_{u}"
                b = open_group(pe, name)
                for kt in range(t + 1):
                    k0, kn = TT[kt]
                    ins = nc.tensor.transpose(b[0:kn, P * kt:P * kt + qn], a_buf[0:qn, u % 2, k0:k0 + kn],
                                              ident[0:qn, 0:qn])
                close_group(ins, name)

            def values(l, u):
                kind, h, _ = UNITS[u]
                evacuated(pe, f"at{l}_{u}")
                if kind == "f":
                    evacuated(pe, f"z{l}fv2")
                    v, dv = vtok[:, :, 512 + FD * h:512 + FD * h + FD], FD
                else:
                    evacuated(pe, f"z{l}dv2")
                    v, dv = vtok[:, :, DV * h:DV * h + DV], DV
                name = f"o{l}_{u}"
                b = open_group(pe, name)
                for kt, (k0, kn) in enumerate(TT):
                    ins = mm(b[0:dv, k0:L], v[0:kn, kt, :], aT[0:kn, (u // 3) % 2, kt, k0:L], kt == 0, kt == 2)
                close_group(ins, name)

            def head_norm(l, u):
                h = UNITS[u][1]
                pe.wait_ge(ev(f"o_square{l}"), h + 1)
                name = f"hn{l}_{h}"
                b = open_group(pe, name)
                close_group(mm(b[:, 0:L], avgV, sq_o[:, h % 2, :], True, True), name)

            def glu(l):
                pe.wait_ge(ev("glu_loaded"), 16 * (l + 1))
                pe.wait_ge(ev(f"gelu_ready{l}"), 1)
                for m in range(4):
                    name = f"glu{l}{m}"
                    b = open_group(pe, name)
                    for k in range(2):
                        ins = mm(b[:, 0:L], w_glu[:, k, P * m:P * m + P], gy[:, k, :], k == 0, k == 1)
                    close_group(ins, name)

            def attention(l, projections):
                scores(l, 0)
                scores(l, 1)
                ssm_out(l, NST - 2)
                ssm_out(l, NST - 1)
                for u in range(len(UNITS) + 2):
                    if u + 2 < len(UNITS):
                        scores(l, u + 2)
                    if u < len(projections):
                        projections[u]()
                    if 1 <= u <= len(UNITS) and UNITS[u - 1][2] == 2:
                        values(l, u - 1)
                    if u >= 2 and UNITS[u - 2][2] == 2 and UNITS[u - 2][0] == "d":
                        head_norm(l, u - 2)
                    if u < len(UNITS):
                        turn_probs(l, u)
                    if u == 4:
                        glu(l)

            def mix_ready(l, k):
                if k == 0:
                    pe.wait_ge(ev(f"ssm_out{l}"), 2)
                elif k == 2:
                    pe.wait_ge(ev(f"diff_out{l}"), DH)
                elif k == 6:
                    for h in range(FH):
                        evacuated(pe, f"o{l}_{12 + 3 * h + 2}")

            def output_projection_features(l):
                for half in range(2):
                    w = chunk_ready(pe, f"out{l}{half}")
                    for m in range(4):
                        name = f"r{l}{4 * half + m}"
                        b = open_group(pe, name)
                        for k in range(KD):
                            if half == 0 and m == 0:
                                mix_ready(l, k)
                            ins = mm(b[:, 0:L], w[:, k, P * m:P * m + P], mixedT[:, k, :], k == 0, k == KD - 1)
                        close_group(ins, name)
                    pe.wait_ge(bank_full[groups[name][0]], groups[name][1] + 1)
                    pe.sem_inc(chunk_used, 1)

            def output_projection_tokens(l):
                for half in range(2):
                    w = chunk_ready(pe, f"out{l}{half}")
                    for t in range(RT):
                        tok = slice(N_META + P * t, N_META + P * t + P)
                        name = f"rt{t}{half}"
                        b = open_group(pe, name)
                        for k in range(KD):
                            if half == 0 and t == 0:
                                mix_ready(l, k)
                            mm(b[:, :], mixedT[:, k, tok], w[:, k, :], k == 0, False)
                        for j in range(4):
                            ins = mm(b[:, P * j:P * j + P], resT[:, 4 * half + j, tok], ident, False, j == 3)
                        close_group(ins, name)
                    pe.wait_ge(bank_full[groups[name][0]], groups[name][1] + 1)
                    pe.sem_inc(chunk_used, 1)

            def dense():
                for fb in range(0, FF, 512):
                    w1, w3 = chunk_ready(pe, f"w1_{fb}"), chunk_ready(pe, f"w3_{fb}")
                    for i in range(min(512, FF - fb) // P):
                        f = fb // P + i
                        project(1, f"fa{f}", w1, P * i, P, f == 0)
                        project(1, f"fb{f}", w3, P * i, P, False)
                    pe.wait_ge(bank_full[groups[f"fb{f}"][0]], groups[f"fb{f}"][1] + 1)
                    pe.sem_inc(chunk_used, 2)
                for half in range(2):
                    bs = [open_group(pe, f"y{4 * half + m}") for m in range(4)]
                    for f0 in range(0, NFF, 8):
                        w = chunk_ready(pe, f"w2_{half}_{f0}")
                        fn = min(8, NFF - f0)
                        for m in range(4):
                            for f in range(f0, f0 + fn):
                                if half == 0 and m == 0:
                                    evacuated(pe, f"fb{f}")
                                ins = mm(bs[m][:, 0:L], w[:, f - f0, P * m:P * m + P], gT[:, f, :],
                                         f == 0, f == NFF - 1)
                            if f0 + fn == NFF:
                                close_group(ins, f"y{4 * half + m}")
                        if f0 + fn < NFF:
                            ins.then_inc(chunk_used, 1)
                        else:
                            pe.wait_ge(bank_full[groups[f"y{4 * half + 3}"][0]], groups[f"y{4 * half + 3}"][1] + 1)
                            pe.sem_inc(chunk_used, 1)

            pe.wait_ge(ev("identity_ready"), 2)
            pe.wait_ge(ev("x_loaded"), 16 * 4)
            for k in range(KD):
                b = open_group(pe, f"xT{k}")
                for t, (q0, qn) in enumerate(TT):
                    ins = nc.tensor.transpose(b[:, q0:q0 + qn], xtok[0:qn, t, P * k:P * k + P], ident[0:qn, 0:qn])
                close_group(ins, f"xT{k}")
            for l in range(DEPTH):
                feature_norm(2 * l)
                if l == 0:
                    transposed_params()
                attention(l, mixer_inputs(l, 2 * l))
                if l == 0:
                    output_projection_features(l)
                    feature_norm(1)
                    dense()
            output_projection_tokens(1)

            for j in range(4):
                b = open_group(pe, f"mh{j}")
                for k in range(2):
                    for t in range(RT):
                        if j == 0 and k == 0:
                            pe.wait_ge(ev("htok"), t + 1)
                        ins = nc.tensor.transpose(b[:, (2 * k + t) * P:(2 * k + t + 1) * P],
                                                  htok[:, t, (2 * j + k) * P:(2 * j + k + 1) * P], ident)
                close_group(ins, f"mh{j}")
            for t in range(RT):
                b = open_group(pe, f"lg{t}")
                for k in range(KD):
                    if t == 0 and k % 2 == 0:
                        evacuated(pe, f"mh{k // 2}")
                    ins = mm(b[:, 0:NE], mhT[:, k, P * t:P * t + P], router[:, k, :], k == 0, k == KD - 1)
                close_group(ins, f"lg{t}")
            chosen = sm(48, 16)
            pe.wait_ge(ev("chosen"), 1)
            for name, mats in (("rank0", [(tri, 0)]), ("rank1", [(onesF, 0), (tri, 1)]),
                               ("count", [(onesF, 0), (onesF, 1)])):
                b = open_group(pe, name)
                for i, (m, t) in enumerate(mats):
                    ins = mm(b[:, 0:NE], m, chosen[:, NE * t:NE * t + NE], i == 0, i == len(mats) - 1)
                close_group(ins, name)
            n_groups = len(groups)
            for b in range(6):
                uses = (n_groups - 1 - b) // 6 + 1
                pe.wait_ge(bank_free[b], uses)

            def gather(n):
                pe.wait_ge(ev("sel_ready"), n + 1)
                for d in range(KD):
                    b = bank[2 + d // 4]
                    for t in range(RT):
                        ins = mm(b[:, P * (d % 4):P * (d % 4) + P], htok[:, t, P * d:P * d + P], sel[:, t, :],
                                 t == 0, t == 1)
                ins.then_inc(ev("gathered"), 1)

            def three(o, x_hi, x_lo, wh, wl, start, stop):
                mm(o, x_hi, wh, start, False)
                mm(o, x_hi, wl, False, False)
                return mm(o, x_lo, wh, False, stop)

            def up(j, fb, kind):
                b = bank[2 * (fb % 2) + (kind == "w3")]
                if kind == "w1" and fb >= 2:
                    pe.wait_ge(ev("g_ready"), 7 * j + fb - 1)
                for half in range(2):
                    c = 2 * order.index((fb, kind)) + half
                    pe.wait_ge(ev("split_lo"), NC * j + c + 1)
                    for i in range(4):
                        k, w = 4 * half + i, slice(512 * i, 512 * i + 512)
                        ins = three(b[:, :], h_hi[:, k, :], h_lo[:, k, :], w_hi[:, c % SPLITS, w],
                                    w_lo[:, c % SPLITS, w], k == 0, k == KD - 1)
                    ins.then_inc(mchunk_used, 1)

            def turn(j, fb):
                pe.wait_ge(ev("g_ready"), 7 * j + fb + 1)
                for i in range(4):
                    ins = nc.tensor.transpose(bank[4][:, P * i:P * i + P], g_e[:, fb % 2, P * i:P * i + P], ident)
                ins.then_inc(ev("turned"), 1)

            def down(j, fb):
                pe.wait_ge(ev("turn_split"), 7 * j + fb + 1)
                for half in range(2):
                    c = 2 * order.index((fb, "w2")) + half
                    pe.wait_ge(ev("split_lo"), NC * j + c + 1)
                    for i in range(2):
                        f = slice(P * (2 * half + i), P * (2 * half + i) + P)
                        for col in range(2):
                            w = slice(D * i + 512 * col, D * i + 512 * col + 512)
                            ins = three(bank[6 + col][:, :], gT_hi[:, fb % 2, f], gT_lo[:, fb % 2, f],
                                        w_hi[:, c % SPLITS, w], w_lo[:, c % SPLITS, w],
                                        fb == 0 and half == 0 and i == 0, fb == 6 and half == 1 and i == 1)
                    ins.then_inc(mchunk_used, 1)

            def scatter(n):
                pe.wait_ge(ev("scat_evac"), n + 1)
                pe.wait_ge(ev("y_evac"), 2 * n + 2)
                for i in range(4):
                    t, half = i // 2, i % 2
                    mm(bank[2 + i][:, :], scat[:, P * t:P * t + P], ysb[:, 512 * half:512 * half + 512],
                       True, True).then_inc(ev("scattered"), 1)

            gather(0)
            pe.wait_ge(ev("jobs_ready"), 1)
            n_jobs = pe.value_load(ints[0:1, 3:4], min_val=NE, max_val=MAX_JOBS)
            with pe.Fori(0, n_jobs) as j:
                pe.wait_ge(ev("gather_split"), j + 1)
                for fb in range(NFB):
                    if fb == 1:
                        pe.wait_ge(ev("added"), 4 * j + 4)
                    up(j, fb, "w1")
                    if fb == 0:
                        scatter(j)
                    if fb:
                        turn(j, fb - 1)
                    up(j, fb, "w3")
                    if fb == 3:
                        pe.wait_ge(ev("selg_ready"), j + 1)
                        for t in range(RT):
                            ins = nc.tensor.transpose(bank[5][:, P * t:P * t + P], selg[:, t, :], ident)
                        ins.then_inc(ev("scat_turned"), 1)
                    if fb:
                        down(j, fb - 1)
                turn(j, NFB - 1)
                gather(j + 1)
                down(j, NFB - 1)
            scatter(n_jobs)

        @block.sync
        def _(sp):
            sp.wait_ge(ev("x_loaded"), 16 * 4)
            for i, (name, src, dst) in enumerate(chunks):
                if i >= RING:
                    sp.wait_ge(chunk_used, i - RING + 1)
                sp.dma_start(dst, src).then_inc(slot_full[i % RING], 16)

            def load(e, c):
                src, dst = expert_chunk(e, c)
                sp.dma_start(dst, src).then_inc(mslot_full[c % MRING], 16)

            n = len(chunks)
            for c in range(MRING):
                sp.wait_ge(chunk_used, n - RING + (c // 2 - n) % RING + 1)
                load(0, c)
            with sp.Fori(0, NE - 1) as e:
                for c in range(NC):
                    ee = e if c + MRING < NC else e + 1
                    sp.wait_ge(ev("split_lo"), NC * e + c + 1)
                    if (c + MRING) % NC == FIRST_DOWN:
                        sp.sem_inc(ev("down_claimed"), 1)
                    load(ee, (c + MRING) % NC)
            for c in range(MRING, NC):
                sp.wait_ge(ev("split_lo"), NC * (NE - 1) + c - MRING + 1)
                load(NE - 1, c)
            sp.wait_ge(ev("jobs_ready"), 1)
            n_jobs = sp.value_load(ints[0:1, 3:4], min_val=NE, max_val=MAX_JOBS)
            with sp.If(n_jobs > NE):
                with sp.Fori(NE, n_jobs) as j:
                    e = sp.value_load(ints[0:1, bass.ds(j - NE, 1)], min_val=0, max_val=NE - 1)
                    for c in range(NC):
                        sp.wait_ge(ev("split_lo"), NC * j + c - MRING + 1)
                        if c in (0, 2, FIRST_DOWN):
                            sp.sem_inc(ev("down_claimed"), 1)
                        load(e, c)
            sp.wait_ge(ev("out_ready"), 2)
            for t in range(RT):
                sp.dma_start(out[0, P * t:P * t + P, :], racc[:, t, :]).then_inc(ev("out_stored"), 16)
            sp.wait_ge(ev("out_stored"), 16 * RT)

        @block.gpsimd
        def _(pool):
            g = nc.gpsimd
            memsets = Chain(pool, ev("pool_memsets"))
            memsets(g.memset(ident, 0.0))
            memsets(g.memset(mask_t[:, :], 0.0))
            memsets(g.memset(tri, 1.0))
            g.affine_select(out=ident, in_=ident, compare_op=ALU.not_equal, fill=1.0, base=0,
                            pattern=[[-1, P]], channel_multiplier=1).then_inc(ev("identity_ready"), 2)
            pool.wait_ge(ev("identity_ready"), 2)
            setup = Chain(pool, ev("pool_setup"))
            setup(g.affine_select(out=mask, in_=mask, compare_op=ALU.is_ge, fill=NEG, base=0,
                                  pattern=[[P, 3], [-1, L]], channel_multiplier=1))
            setup(g.affine_select(out=tri, in_=tri, compare_op=ALU.is_ge, fill=0.0, base=-1,
                                  pattern=[[1, P]], channel_multiplier=-1))
            setup(g.memset(avgD, 1.0 / D))
            setup(g.memset(avgV, 1.0 / DV))
            setup(g.memset(eps_col, EPS))
            setup(g.memset(onesF, 1.0))
            setup(g.memset(ones_row, 1.0))
            setup(g.memset(b_exp_t[:, :], 0.0))
            setup(g.iota(slot_iota, [[1, P]], base=0, channel_multiplier=0, allow_small_or_imprecise_dtypes=True))
            setup(g.iota(time_iota, [[1, L]], base=0, channel_multiplier=0, allow_small_or_imprecise_dtypes=True))
            setup(g.iota(expert_iota, [[1, NE]], base=0, channel_multiplier=0, allow_small_or_imprecise_dtypes=True))
            g.iota(ints[:, 8:9], [[0, 1]], base=0, channel_multiplier=1).then_inc(ev("constants_ready"), 1)
            pool.wait_ge(ev("constants_ready"), 1)
            setup(g.memset(region["foxqk"][64:P, :], 0.0))
            setup(g.memset(fka[64:68, :, :], 1.0))
            setup(g.memset(fqa[96:100, :, :], 1.0 / SCALE))
            for i, v in enumerate((fka[64:68, :, :], fqa[96:100, :, :])):
                g.affine_select(out=v, in_=v, compare_op=ALU.is_equal, fill=0.0, base=0,
                                pattern=[[-1, FH], [0, L]], channel_multiplier=1).then_inc(ev("fox_select"), 1)
                pool.wait_ge(ev("fox_select"), i + 1)
            for l in range(DEPTH):
                phase_step = Chain(pool, ev(f"pool_phase_steps{l}"))
                pool.wait_ge(ev(f"angles{l}"), 1)
                for i in range(NST // 2, NST):
                    phase_tile(g, phase_step, i, o_buf[:, 0, :] if l else t_pool)
                pool.sem_inc(ev(f"phases{l}"), 1)
                step = Chain(pool, ev(f"pool_steps{l}"))
                for i in range(NST):
                    pool.wait_ge(ev(f"w_ready{l}"), i + 1)
                    if i >= 2:
                        pool.wait_ge(ev(f"y_done{l}"), i - 1)
                    co, si = cosT[:, i, :], sinT[:, i, :]
                    w0, w1 = w_scan[:, i % 2, 0, :], w_scan[:, i % 2, 1, :]
                    x0, x1 = x_ssm[:, i % 2, 0, :], x_ssm[:, i % 2, 1, :]
                    step(g.tensor_tensor(x0, w0, co, ALU.mult))
                    step(g.tensor_tensor(t_pool, w1, si, ALU.mult))
                    step(g.tensor_tensor(x0, x0, t_pool, ALU.subtract))
                    step(g.tensor_tensor(x1, w0, si, ALU.mult))
                    step(g.tensor_tensor(t_pool, w1, co, ALU.mult))
                    g.tensor_tensor(x1, x1, t_pool, ALU.add).then_inc(ev(f"x_ready{l}"), 1)
                    pool.wait_ge(ev(f"x_ready{l}"), i + 1)
            pool.wait_ge(ev("jobs_ready"), 1)
            n_jobs = pool.value_load(ints[0:1, 3:4], min_val=NE, max_val=MAX_JOBS)
            for c in range(SPLITS):
                pool.wait_ge(mslot_full[c], 16 * (NC // MRING) * n_jobs)
                pool.sem_inc(mslot_full[c], 16)

        @block.scalar
        def _(act):
            chain = Chain(act, ev("act_steps"))
            x, meta = a["x"], a["meta_tokens"]
            act.dma_start(xtok[0:N_META, 0, :], meta[:, :]).then_inc(ev("x_loaded"), 16)
            act.dma_start(xtok[N_META:P, 0, :], x[0, 0:P - N_META, :]).then_inc(ev("x_loaded"), 16)
            act.dma_start(xtok[:, 1, :], x[0, P - N_META:2 * P - N_META, :]).then_inc(ev("x_loaded"), 16)
            act.dma_start(xtok[0:N_META, 2, :], x[0, SEQ - N_META:SEQ, :]).then_inc(ev("x_loaded"), 16)

            def param(dst, src):
                act.dma_start(dst, src).then_inc(ev("params_loaded"), 16)

            param(rows_t[0:16, :], a["norm_mix_g"].rearrange("l (k p) -> (l k) p", p=P))
            param(rows_t[16:32, :], a["norm_ffn_g"].rearrange("l (k p) -> (l k) p", p=P))
            param(rows_t[32:34, :], a["diff_subln_g"][:, :])
            param(rows_t[34:38, :], a["ssm_d"].rearrange("l (m g) c -> (l m) (g c)", m=2))
            param(rows_t[38:54, :], a["ssm_lambda_re"].rearrange("l (i g) n -> (l i) (g n)", g=2))
            param(rows_t[54:70, :], a["ssm_lambda_im"].rearrange("l (i g) n -> (l i) (g n)", g=2))
            param(dt_rows[0:16, :], a["ssm_log_dt"].rearrange("l (i g) -> (l i) g", g=2))
            param(fb_t[0:FH, :], a["fox_forget_b"].rearrange("l h -> h l"))
            param(router[:, :, :], a["moe_router"][0, :, :].rearrange("(k p) e -> p k e", p=P))
            for i, n in enumerate(("q1", "k1", "q2", "k2")):
                act.dma_start(lam_v[:, i, :, :], a[f"diff_lambda_{n}"].partition_broadcast(P)).then_inc(ev("lam_loaded"), 16)
            param(sm(320, 1), a["diff_lambda_q1"][0, 0:1].partition_broadcast(P))

            def load_ssm(l):
                if l:
                    act.wait_ge(ev(f"c_blocks{l - 1}"), 1)
                for c, n in enumerate(("re", "im")):
                    act.dma_start(b_raw[:, c, :, :], a[f"ssm_b_{n}"][l, :, :, :].rearrange(
                        "(i g) n c -> (g n) i c", g=2)).then_inc(ev("ssm_loaded"), 16)
                    act.dma_start(c_raw[:, :, c, :], a[f"ssm_c_{n}"][l, :, :, :].rearrange(
                        "(m g) c n -> (g c) m n", m=2)).then_inc(ev("ssm_loaded"), 16)
                act.dma_start(w_glu[:, :, :], a["ssm_w_glu"][l, :, :].rearrange("(k p) n -> p k n", p=P)
                              ).then_inc(ev("glu_loaded"), 16)

            load_ssm(0)

            def squares(n, count):
                act.wait_ge(ev(f"res{n}"), 4)
                if n:
                    act.wait_ge(ev(f"res{n}"), count)
                nc.scalar.activation(sqT[:, 0:4, :], resT[:, 0:4, :], ACT.Square).then_inc(ev(f"squares_act{n}"), 1)

            def copy(dst, src):
                return nc.scalar.activation(dst, src, ACT.Copy)

            def rstd_first(x, event):
                chain(nc.scalar.activation(rs0_t[:, :], x, ACT.Ln, bias=eps_col))
                nc.scalar.activation(rs0_t[:, :], rs0_t[:, :], ACT.Exp, scale=-0.5).then_inc(ev(event), 1)

            def norm_rstd(n):
                rstd_first(take(act, f"ssq{n}")[:, 0:L], f"rstd_first{n}")

            def head_rstd(l, u):
                h = UNITS[u][1]
                b = take(act, f"hn{l}_{h}")
                if h:
                    act.wait_ge(ev(f"diff_out{l}"), h)
                rstd_first(b[:, 0:L], f"head_rstd_first{l}")

            def token_rstd(squares, event):
                act.wait_ge(ev(squares), RT)
                chain(nc.scalar.activation(sm(114, 2), sm(100, 2), ACT.Ln, bias=eps_col, scale=1.0 / D))
                nc.scalar.activation(sm(114, 2), sm(114, 2), ACT.Exp, scale=-0.5).then_inc(ev(event), 1)

            def params_turned():
                b = take(act, "prm")
                release(copy(prm[:, 0:70], b[:, 0:70]), "prm")
                b = take(act, "ldt")
                release(copy(prm[:, 70:86], b[:, 0:16]), "ldt")

            def ssm_tables(l):
                act.wait_ge(ev(f"phases{l}"), 2)
                nc.scalar.activation(sinT, sinT, ACT.Sin, scale=SIN_2PI)
                nc.scalar.activation(cosT, cosT, ACT.Sin, scale=SIN_2PI)
                nc.scalar.activation(sm(0), sm(8), ACT.Sin, scale=SIN_2PI)
                nc.scalar.activation(sm(16), sm(8), ACT.Sin, scale=SIN_2PI / 2).then_inc(ev(f"tables{l}"), 1)

            def ssm_weights(l):
                b = take(act, f"bT{l}")
                release(copy(bT_t[:, :], b[:, :]), f"bT{l}")
                b = take(act, f"cT{l}")
                bv, cv = (v.rearrange("p (m c n) -> p m c n", m=2, c=2) for v in (b[:, :], cT_t[:, :]))
                nc.scalar.activation(cv[:, :, 0, :], bv[:, :, 0, :], ACT.Copy)
                release(nc.scalar.activation(cv[:, :, 1, :], bv[:, :, 1, :], ACT.Copy, scale=-1.0), f"cT{l}")

            def mixer_evac(l):
                def tokens(key, cols, t):
                    b = take(act, f"z{l}{key}{t}")
                    qn, at = TT[t][1], 512 if key == "fv" else 0
                    release(copy(vtok[0:qn, t, at:at + cols], b[0:qn, 0:cols]), f"z{l}{key}{t}")

                def feature(key, dst, h):
                    b = take(act, f"z{l}{key}{h}")
                    release(copy(dst[:, h, :], b[:, 0:L]), f"z{l}{key}{h}")
                    if key == "dq" and h == DH - 1:
                        act.wait_ge(ev(f"fg_abs{l}"), 1)
                        nc.scalar.activation(fgm[0:FH, :], fgm[0:FH, :], ACT.Exp).then_inc(ev(f"fg_exp{l}"), 1)
                        act.wait_ge(ev(f"fg_exp{l}"), 1)
                        nc.scalar.activation(fgm[0:FH, :], fgm[0:FH, :], ACT.Ln, bias=onesF[0:FH, 0:1]
                                             ).then_inc(ev(f"fg_ln{l}"), 1)

                def forget():
                    b = take(act, f"z{l}fg")
                    release(nc.scalar.activation(fgz[0:FH, :], b[0:FH, 0:L], ACT.Identity, bias=fb_t[0:FH, l:l + 1]),
                            f"z{l}fg")

                def fox(i):
                    act.wait_ge(ev("fox_select"), 2)
                    b = take(act, f"z{l}fqk{i}")
                    dst, h = (fqa, fka)[i // 2], 2 * (i % 2)
                    copy(dst[0:64, h, :], b[0:64, 0:L])
                    release(copy(dst[0:64, h + 1, :], b[64:P, 0:L]), f"z{l}fqk{i}")

                steps = [lambda t=t: tokens("fv", 256, t) for t in range(3)] + [forget]
                steps += [lambda h=h, k=k, d=d: feature(k, d, h) for k, d in (("dq", dqT), ("dk", dkT)) for h in range(DH)]
                steps += [lambda t=t: tokens("dv", 512, t) for t in range(3)] + [lambda i=i: fox(i) for i in range(4)]
                for m in range(2):
                    b = take(act, f"z{l}u{m}")
                    release(copy(uT[:, m, :], b[:, 0:L]), f"z{l}u{m}")
                for j in range(EARLY):
                    steps[j]()
                    if SSM_AT[l].get(j) == 0:
                        if l == 0:
                            ssm_tables(0)
                            nc.scalar.preload_act_table_set("natural_log_exp_and_others")
                        ssm_weights(l)
                return steps[EARLY:]

            def gelu(l):
                act.wait_ge(ev(f"gelu_arg{l}"), 1)
                nc.scalar.activation(ye, yq, ACT.Exp, scale=-2.0 * math.sqrt(2.0 / math.pi)).then_inc(ev(f"gelu_exp{l}"), 1)

            def glu(l):
                for m in range(2):
                    b = take(act, f"glu{l}{2 + m}")
                    release(nc.scalar.activation(glu_e[:, m, :], b[:, 0:L], ACT.Exp, scale=-1.0), f"glu{l}{2 + m}")

            def exps(l, u):
                kind, h, t = UNITS[u]
                qn, kmax = TT[t][1], sum(TT[t])
                act.wait_ge(ev(f"scores{l}"), u + 1)
                for m in range(2 if kind == "d" else 1):
                    at = 321 + 4 * (u % 3) + m
                    nc.scalar.activation(e_buf[u % 3][0:qn, m, 0:kmax], s_buf[u % 3][0:qn, m, 0:kmax], ACT.Exp,
                                         bias=small[0:qn, at:at + 1], accum_out=small[0:qn, at + 2:at + 3]
                                         ).then_inc(ev(f"exps{l}{kind}"), 1)

            def probs_evac(l, u):
                t = UNITS[u][2]
                q0, qn = TT[t]
                name = f"at{l}_{u}"
                b = take(act, name)
                hp = (u // 3) % 2
                full = min(t + 1, 2)
                ins = copy(aT[:, hp, 0:full, q0:q0 + qn],
                           b[:, 0:P * full].rearrange("p (k q) -> p k q", q=P)[:, :, 0:qn])
                if t == 2:
                    ins = copy(aT[0:qn, hp, 2, q0:q0 + qn], b[0:qn, 2 * P:2 * P + qn])
                release(ins, name)

            def head_out(l, u):
                kind, h, _ = UNITS[u]
                name = f"o{l}_{u}"
                b = take(act, name)
                if kind == "f":
                    release(copy(mixedT[64 * (h % 2):64 * (h % 2) + 64, 6 + h // 2, :], b[0:64, 0:L]), name)
                    return
                if h >= 2:
                    act.wait_ge(ev(f"diff_out{l}"), h - 1)
                release(copy(o_buf[:, h % 2, :], b[:, 0:L]), name)
                evacuated(act, name)
                nc.scalar.activation(sq_o[:, h % 2, :], o_buf[:, h % 2, :], ACT.Square).then_inc(ev(f"o_square{l}"), 1)

            def attention(l, evacuations):
                exps(l, 0)
                exps(l, 1)
                gelu(l)
                for u in range(len(UNITS) + 2):
                    if u + 2 < len(UNITS):
                        exps(l, u + 2)
                    if u < len(evacuations):
                        evacuations[u]()
                    if 1 <= u <= len(UNITS) and UNITS[u - 1][2] == 2:
                        head_out(l, u - 1)
                    if u >= 2 and UNITS[u - 2][2] == 2 and UNITS[u - 2][0] == "d":
                        head_rstd(l, u - 2)
                    if u < len(UNITS):
                        probs_evac(l, u)
                    if u == 4:
                        glu(l)

            nc.scalar.preload_act_table_set("natural_log_exp_and_others")
            squares(0, 8)
            norm_rstd(0)
            act.wait_ge(ev("lam_dots"), 4)
            nc.scalar.activation(sm(32, 4), sm(36, 4), ACT.Exp).then_inc(ev("lam_exp"), 1)
            params_turned()
            for l in range(DEPTH):
                attention(l, mixer_evac(l))
                if l == 0:
                    load_ssm(1)
                    squares(1, 8)
                    norm_rstd(1)
                    for f in range(NFF):
                        b = take(act, f"fa{f}")
                        if f >= 2:
                            evacuated(act, f"fb{f - 2}")
                        release(nc.scalar.activation(silu_t[:, f % 2, :], b[:, 0:L], ACT.Silu), f"fa{f}")
                    ssm_tables(1)
                    nc.scalar.preload_act_table_set("natural_log_exp_and_others")
                    squares(2, 8)
                    norm_rstd(2)

            for half in range(2):
                for t in range(RT):
                    b = take(act, f"rt{t}{half}")
                    release(copy(racc[:, t, 512 * half:512 * half + 512], b[:, :]), f"rt{t}{half}")
            act.wait_ge(ev("ssm_out1"), 2)
            act.dma_start(g_ffn_b, a["norm_ffn_g"][1, :].partition_broadcast(P)).then_inc(ev("row_gains"), 16)
            act.dma_start(g_fin_b, a["final_norm_g"].partition_broadcast(P)).then_inc(ev("row_gains"), 16)
            evacuated(act, "rt01")
            evacuated(act, "rt11")
            for t in range(RT):
                nc.scalar.activation(htok[:, t, :], racc[:, t, :], ACT.Square, accum_out=sm(100 + t, 1)
                                     ).then_inc(ev("token_squares"), 1)
            token_rstd("token_squares", "token_rstd_first")
            for j in range(4):
                b = take(act, f"mh{j}")
                release(copy(mhT[:, 2 * j:2 * j + 2, :], b[:, :].rearrange("p (k t) -> p k t", k=2)), f"mh{j}")
            act.wait_ge(ev("margin"), 1)
            nc.scalar.activation(sm(104, 2), sm(106, 2), ACT.Exp).then_inc(ev("margin_exp"), 1)

            def split_hi(j, m):
                act.wait_ge(mslot_full[m % MRING], 16 * ((NC // MRING) * j + m // MRING + 1))
                copy(w_hi[:, m % SPLITS, :], mslot(m)).then_inc(ev("split_hi"), 1)

            def gather_hi():
                for b in range(2):
                    copy(h_hi[:, 4 * b:4 * b + 4, :], bank[2 + b][:, :].rearrange("p (k s) -> p k s", k=4)
                         ).then_inc(ev("gather_hi"), 1)

            def turn_hi(j, fb):
                act.wait_ge(ev("turned"), 7 * j + fb + 1)
                copy(gT_hi[:, fb % 2, :], bank[4][:, :]).then_inc(ev("turn_hi"), 1)

            act.wait_ge(chunk_used, len(chunks))
            for m in range(SPLITS):
                split_hi(0, m)
            act.wait_ge(ev("gathered"), 1)
            gather_hi()
            act.wait_ge(ev("jobs_ready"), 1)
            n_jobs = act.value_load(ints[0:1, 3:4], min_val=NE, max_val=MAX_JOBS)
            with act.Fori(0, n_jobs) as j:
                for c in range(NC):
                    act.wait_ge(mchunk_used, NC * j + c + 1)
                    if c == GATHER_AFTER:
                        turn_hi(j, NFB - 1)
                    if c == NC - 1:
                        copy(ysb[:, 0:512], bank[6][:, :]).then_inc(ev("y_evac"), 1)
                    if c in silu_after:
                        fb = silu_after[c]
                        nc.scalar.activation(e1[:, fb % 2, :], bank[2 * (fb % 2)][:, :], ACT.Silu
                                             ).then_inc(ev("silu_done"), 1)
                    split_hi(j, c + SPLITS)
                    if c in turn_after:
                        turn_hi(j, turn_after[c])
                    if c == SCATTER_AFTER:
                        act.wait_ge(ev("scat_turned"), j + 1)
                        copy(scat, bank[5][:, 0:SEQ]).then_inc(ev("scat_evac"), 1)
                    if c == GATHER_AFTER:
                        act.wait_ge(ev("gathered"), j + 2)
                        gather_hi()

            act.wait_ge(ev("final_ready"), 1)
            for t in range(RT):
                nc.scalar.activation(htok[:, t, :], racc[:, t, :], ACT.Square, accum_out=sm(100 + t, 1)
                                     ).then_inc(ev("final_squares"), 1)
            token_rstd("final_squares", "final_rstd_first")

        @block.vector
        def _(dve):
            v = nc.vector
            step = Chain(dve, ev("dve_steps"))

            for k in range(KD):
                b = take(dve, f"xT{k}")
                release(v.tensor_copy(resT[:, k, :], b[:, 0:L]), f"xT{k}")
                evacuated(dve, f"xT{k}")
                dve.sem_inc(ev("res0"), 1)

            def squares(n):
                v.tensor_tensor(sqT[:, 4:8, :], resT[:, 4:8, :], resT[:, 4:8, :], ALU.mult).then_inc(ev(f"squares_dve{n}"), 1)

            def rsqrt(x, name):
                step(v.tensor_tensor(rs_t[:, :], rs0_t[:, :], rs0_t[:, :], ALU.mult))
                release(v.scalar_tensor_tensor(rs_t[:, :], x, EPS, rs_t[:, :], ALU.add, ALU.mult), name)
                evacuated(dve, name)
                step(v.tensor_scalar(rs_t[:, :], rs_t[:, :], -0.5, 1.5, ALU.mult, ALU.add))
                step(v.tensor_tensor(rs_t[:, :], rs_t[:, :], rs0_t[:, :], ALU.mult))

            def normalise(n):
                l, kind = n // 2, n % 2
                b = take(dve, f"ssq{n}")
                dve.wait_ge(ev(f"rstd_first{n}"), 1)
                rsqrt(b[:, 0:L], f"ssq{n}")
                for k in range(KD):
                    col = 16 * kind + 8 * l + k
                    v.scalar_tensor_tensor(hT[:, k, :], resT[:, k, :], prm[:, col:col + 1], rs_t[:, :],
                                           ALU.mult, ALU.mult).then_inc(ev(f"h{n}"), 1)

            x, k, f, q, dt = (sm(120 + 8 * i) for i in range(5))
            e, r, th, cm, ni, den, cr, ci, nr = (sm(176 + 8 * i) for i in range(9))
            t1, t2, mag = sm(248), sm(256), sm(264)

            def eigenvalues(l):
                return prm[:, 38 + 8 * l:46 + 8 * l], prm[:, 54 + 8 * l:62 + 8 * l]

            def discretise(l):
                lr, li = eigenvalues(l)
                step(v.tensor_scalar(x, prm[:, 70 + 8 * l:78 + 8 * l], -87.0, 88.0, ALU.max, ALU.min))
                step(v.tensor_scalar(k, x, 1.0 / math.log(2.0), MAGIC, ALU.mult, ALU.add))
                step(v.tensor_scalar(k, k, -MAGIC, None, ALU.add))
                step(v.scalar_tensor_tensor(f, k, -LN2_HI, x, ALU.mult, ALU.add))
                step(v.scalar_tensor_tensor(f, k, -LN2_LO, f, ALU.mult, ALU.add))
                step(v.tensor_scalar(q, f, 1.0 / math.factorial(7), None, ALU.mult))
                for n in range(6, 0, -1):
                    step(v.scalar_tensor_tensor(q, q, 1.0 / math.factorial(n), f, ALU.add, ALU.mult))
                step(v.tensor_scalar(k, k, 127.0, 8388608.0, ALU.add, ALU.mult))
                step(v.tensor_copy(ints[:, 0:8], k))
                step(v.scalar_tensor_tensor(dt, q, 1.0, ints[:, 0:8].bitcast(F32), ALU.add, ALU.mult))
                step(v.tensor_tensor(r, lr, dt, ALU.mult))
                step(v.tensor_scalar(r, r, -60.0, 60.0, ALU.max, ALU.min))
                step(v.tensor_scalar(r, r, 1.0 / 256, None, ALU.mult))
                step(v.tensor_scalar(e, r, 1.0 / 120, None, ALU.mult))
                for n in (4, 3, 2, 1):
                    step(v.scalar_tensor_tensor(e, e, 1.0 / math.factorial(n), r, ALU.add, ALU.mult))
                for _ in range(8):
                    step(v.scalar_tensor_tensor(e, e, 2.0, e, ALU.add, ALU.mult))
                step(v.tensor_scalar(mag, e, 1.0, None, ALU.add))
                step(v.tensor_tensor(th, li, dt, ALU.mult))
                step(v.tensor_scalar(th, th, 1.0 / (2.0 * math.pi), None, ALU.mult))
                step(v.tensor_scalar(t1, th, MAGIC, -MAGIC, ALU.add, ALU.add))
                step(v.tensor_tensor(sm(8), th, t1, ALU.subtract))
                dve.sem_inc(ev(f"angles{l}"), 1)
                for i in range(NST // 2):
                    phase_tile(v, step, i, rs_t[:, :] if l else t_dve)
                dve.sem_inc(ev(f"phases{l}"), 1)

            def coefficients(l):
                lr, li = eigenvalues(l)
                dve.wait_ge(ev(f"tables{l}"), 1)
                step(v.scalar_tensor_tensor(cm, sm(16), -2.0, sm(16), ALU.mult, ALU.mult))
                step(v.tensor_scalar(t1, cm, 1.0, None, ALU.add))
                step(v.tensor_tensor(t1, e, t1, ALU.mult))
                step(v.tensor_tensor(nr, t1, cm, ALU.add))
                step(v.tensor_tensor(ni, mag, sm(0), ALU.mult))
                step(v.tensor_tensor(t1, lr, lr, ALU.mult))
                step(v.tensor_tensor(t2, li, li, ALU.mult))
                step(v.tensor_tensor(den, t1, t2, ALU.add))
                step(v.reciprocal(den, den))
                for o, p0, p1, op in ((cr, nr, ni, ALU.add), (ci, ni, nr, ALU.subtract)):
                    step(v.tensor_tensor(t1, p0, lr, ALU.mult))
                    step(v.tensor_tensor(t2, p1, li, ALU.mult))
                    step(v.tensor_tensor(t1, t1, t2, op))
                    step(v.tensor_tensor(o, t1, den, ALU.mult))
                dve.wait_ge(ev("ssm_loaded"), 64 * (l + 1))
                br, bi = b_raw[:, 0, :, :], b_raw[:, 1, :, :]
                crb, cib = (w.unsqueeze(2).to_broadcast([P, NST, 16]) for w in (cr, ci))
                ta, tb = cut(rs_t, 0, NST, 16), cut(rs_t, P, NST, 16)
                for c, (p0, p1, op) in enumerate(((br, bi, ALU.subtract), (bi, br, ALU.add))):
                    step(v.tensor_tensor(ta, p0, crb, ALU.mult))
                    step(v.tensor_tensor(tb, p1, cib, ALU.mult))
                    for g in range(2):
                        hs = slice(64 * g, 64 * g + 64)
                        step(v.tensor_tensor(b_exp[hs, c, :, 16 * g:16 * g + 16], ta[hs], tb[hs], op))
                dve.sem_inc(ev(f"b_blocks{l}"), 1)
                cflat = c_raw_t[:, :].rearrange("p (i n) -> p i n", n=STATE)
                for g in range(2):
                    step(v.tensor_scalar(c_exp[:, :, 64 * g:64 * g + 64], cflat, sm(40 + g, 1), None, ALU.mult))
                dve.sem_inc(ev(f"c_blocks{l}"), 1)

            def ssm_scan(l, i):
                co, si = cosT[:, i, :], sinT[:, i, :]
                bre = take(dve, f"bu{l}{i}0")[:, 0:L]
                bim = take(dve, f"bu{l}{i}1")[:, 0:L]
                if i >= 2:
                    dve.wait_ge(ev(f"x_ready{l}"), i - 1)
                w0, w1 = w_scan[:, i % 2, 0, :], w_scan[:, i % 2, 1, :]
                v.tensor_tensor(w0, bre, co, ALU.mult)
                step(v.tensor_tensor(t_dve, bim, si, ALU.mult))
                step(v.tensor_tensor(w0, w0, t_dve, ALU.add))
                release(v.tensor_tensor(w1, bim, co, ALU.mult), f"bu{l}{i}1")
                evacuated(dve, f"bu{l}{i}1")
                release(v.tensor_tensor(t_dve, bre, si, ALU.mult), f"bu{l}{i}0")
                evacuated(dve, f"bu{l}{i}0")
                step(v.tensor_tensor(w1, w1, t_dve, ALU.subtract))
                m = sm(264)[:, i:i + 1].to_broadcast([P, L])
                step(v.tensor_tensor_scan(w0, m, w0, 0.0, ALU.mult, ALU.add))
                v.tensor_tensor_scan(w1, m, w1, 0.0, ALU.mult, ALU.add).then_inc(ev(f"w_ready{l}"), 1)
                dve.wait_ge(ev(f"w_ready{l}"), i + 1)

            def forget_gate(l):
                evacuated(dve, f"z{l}fg")
                v.scalar_tensor_tensor(fgm[0:FH, :], fgz[0:FH, :], -1.0, fgz[0:FH, :], ALU.mult, ALU.min).then_inc(ev(f"fg_abs{l}"), 1)

            def decay(l):
                dve.wait_ge(ev(f"fg_ln{l}"), 1)
                step(v.scalar_tensor_tensor(fgz[0:FH, :], fgz[0:FH, :], 0.0, fgm[0:FH, :], ALU.min, ALU.subtract))
                step(v.tensor_tensor_scan(fgc[0:FH, :], ones_row[0:FH, :], fgz[0:FH, :], 0.0, ALU.mult, ALU.add))
                dve.wait_ge(ev("fox_select"), 2)
                c = fgc[0:FH, :].unsqueeze(1).to_broadcast([FH, FH, L])
                v.tensor_scalar(fqa[64:68, :, :], c, 1.0 / SCALE, None, ALU.mult).then_inc(ev(f"decay_rows{l}"), 1)
                v.tensor_scalar(fka[96:100, :, :], c, -1.0, None, ALU.mult).then_inc(ev(f"decay_rows{l}"), 1)
                dve.wait_ge(ev(f"decay_rows{l}"), 2)

            def gelu(l):
                dve.wait_ge(ev(f"y_done{l}"), NST)
                for m in range(2):
                    col = 34 + 2 * l + m
                    step(v.scalar_tensor_tensor(ys[:, m, :], uT[:, m, :], prm[:, col:col + 1], bank[6 + m][:, 0:L],
                                                ALU.mult, ALU.add))
                step(v.tensor_tensor(yq, ys, ys, ALU.mult))
                step(v.tensor_scalar(yq, yq, 0.044715, 1.0, ALU.mult, ALU.add))
                v.tensor_tensor(yq, yq, ys, ALU.mult).then_inc(ev(f"gelu_arg{l}"), 1)

            def gelu_end(l):
                dve.wait_ge(ev(f"gelu_exp{l}"), 1)
                step(v.tensor_scalar(ye, ye, 1.0, None, ALU.add))
                step(v.reciprocal(ye, ye))
                v.tensor_tensor(gy, ys, ye, ALU.mult).then_inc(ev(f"gelu_ready{l}"), 1)

            def glu(l):
                for m in range(2):
                    evacuated(dve, f"glu{l}{2 + m}")
                step(v.tensor_scalar(glu_e, glu_e, 1.0, None, ALU.add))
                step(v.reciprocal(glu_e, glu_e))
                for m in range(2):
                    b = take(dve, f"glu{l}{m}")
                    release(v.tensor_tensor(mixedT[:, m, :], glu_e[:, m, :], b[:, 0:L], ALU.mult), f"glu{l}{m}")
                    evacuated(dve, f"glu{l}{m}")
                    dve.sem_inc(ev(f"ssm_out{l}"), 1)

            def unit_scores(l, u):
                kind, h, t = UNITS[u]
                qn, kmax = TT[t][1], sum(TT[t])
                maps = 2 if kind == "d" else 1
                for m in range(maps):
                    name = f"s{l}_{u}_{m}"
                    b = take(dve, name)
                    release(v.scalar_tensor_tensor(s_buf[u % 3][0:qn, m, 0:kmax], b[0:qn, 0:kmax], SCALE,
                                                   mask[0:qn, t, 0:kmax], ALU.mult, ALU.add), name)
                    evacuated(dve, name)
                at = 321 + 4 * (u % 3)
                v.tensor_reduce(small[0:qn, at:at + maps], s_buf[u % 3][0:qn, 0:maps, 0:kmax], AX.X, ALU.max,
                                negate=True).then_inc(ev(f"scores{l}"), 1)

            def unit_probs(l, u):
                kind, h, t = UNITS[u]
                qn, kmax = TT[t][1], sum(TT[t])
                maps = 2 if kind == "d" else 1
                done = 2 * (u + 1) if kind == "d" else u - 11
                dve.wait_ge(ev(f"exps{l}{kind}"), done)
                if u >= 2:
                    take(dve, f"at{l}_{u - 2}")
                at = 321 + 4 * (u % 3) + 2
                su = small[0:qn, at:at + 2]
                step(v.reciprocal(su[:, 0:maps], su[:, 0:maps]))
                o, e = a_buf[0:qn, u % 2, 0:kmax], e_buf[u % 3][0:qn, :, 0:kmax]
                if kind == "d":
                    step(v.tensor_scalar(su[:, 1:2], su[:, 1:2], sm(44 + l, 1)[0:qn], None, ALU.mult))
                    step(v.tensor_scalar(o, e[:, 0, :], su[:, 0:1], None, ALU.mult))
                    ins = v.scalar_tensor_tensor(o, e[:, 1, :], su[:, 1:2], o, ALU.mult, ALU.add)
                else:
                    ins = v.tensor_scalar(o, e[:, 0, :], su[:, 0:1], None, ALU.mult)
                ins.then_inc(ev(f"probs{l}"), 1)

            def head_norm(l, h):
                b = take(dve, f"hn{l}_{h}")
                dve.wait_ge(ev(f"head_rstd_first{l}"), h + 1)
                rsqrt(b[:, 0:L], f"hn{l}_{h}")
                v.scalar_tensor_tensor(mixedT[:, 2 + h, :], o_buf[:, h % 2, :], sm(46 + l, 1), rs_t[:, :],
                                       ALU.mult, ALU.mult).then_inc(ev(f"diff_out{l}"), 1)
                dve.wait_ge(ev(f"diff_out{l}"), h + 1)

            def attention(l):
                unit_scores(l, 0)
                unit_scores(l, 1)
                gelu(l)
                for u in range(len(UNITS) + 2):
                    if u + 2 < len(UNITS):
                        unit_scores(l, u + 2)
                    if u < len(UNITS):
                        unit_probs(l, u)
                    if u >= 2 and UNITS[u - 2][2] == 2 and UNITS[u - 2][0] == "d":
                        head_norm(l, UNITS[u - 2][1])
                    if u == 1:
                        gelu_end(l)
                    if u == 5:
                        glu(l)

            def dense():
                for f in range(NFF):
                    evacuated(dve, f"fa{f}")
                    s = silu_t[:, f % 2, :]
                    bb = take(dve, f"fb{f}")
                    release(v.tensor_tensor(gT[:, f, :], s, bb[:, 0:L], ALU.mult), f"fb{f}")
                    evacuated(dve, f"fb{f}")

            def add_residual(prefix, n):
                for k in range(KD):
                    b = take(dve, f"{prefix}{k}")
                    release(v.tensor_tensor(resT[:, k, :], resT[:, k, :], b[:, 0:L], ALU.add), f"{prefix}{k}")
                    evacuated(dve, f"{prefix}{k}")
                    dve.sem_inc(ev(f"res{n}"), 1)

            squares(0)
            dve.wait_ge(ev("params_loaded"), 16 * N_PARAM)
            dve.wait_ge(ev("constants_ready"), 1)
            for g in range(2):
                ins = v.tensor_copy(dt_wide[0:16, 64 * g:64 * g + 64], dt_rows[0:16, g:g + 1].to_broadcast([16, 64]))
            ins.then_inc(ev("dt_wide_ready"), 1)
            dve.wait_ge(ev("lam_loaded"), 16 * 4)
            step(v.tensor_tensor(lam_v[:, 0, :, :], lam_v[:, 0, :, :], lam_v[:, 1, :, :], ALU.mult))
            step(v.tensor_tensor(lam_v[:, 2, :, :], lam_v[:, 2, :, :], lam_v[:, 3, :, :], ALU.mult))
            for i in range(2):
                for l in range(DEPTH):
                    v.tensor_reduce(sm(36 + 2 * i + l, 1), lam_v[:, 2 * i, l, :], AX.X, ALU.add).then_inc(ev("lam_dots"), 1)
            step(v.tensor_single_scalar(ints[:, 9:10], ints[:, 8:9], 16, ALU.bitwise_and))
            step(v.tensor_copy(sm(42, 1), ints[:, 9:10]))
            step(v.tensor_scalar(sm(41, 1), sm(42, 1), 1.0 / 16, None, ALU.mult))
            step(v.tensor_scalar(sm(40, 1), sm(41, 1), -1.0, 1.0, ALU.mult, ALU.add))
            evacuated(dve, "prm")
            normalise(0)
            dve.wait_ge(ev("h0"), KD)
            dve.wait_ge(ev("lam_exp"), 1)
            step(v.tensor_tensor(sm(44, 2), sm(34, 2), sm(32, 2), ALU.subtract))
            for l in range(DEPTH):
                lam_init = 0.8 - 0.6 * math.exp(-0.3 * l)
                step(v.tensor_scalar(sm(44 + l, 1), sm(44 + l, 1), -lam_init, None, ALU.add))
            evacuated(dve, "ldt")
            for l in range(DEPTH):
                lam_init = 0.8 - 0.6 * math.exp(-0.3 * l)
                step(v.tensor_scalar(sm(46 + l, 1), prm[:, 32 + l:33 + l], 1.0 - lam_init, None, ALU.mult))
            discretise(0)
            coefficients(0)
            for l in range(DEPTH):
                if l == 0:
                    forget_gate(l)
                for i in range(NST):
                    ssm_scan(l, i)
                    if l == 1 and i == 2:
                        forget_gate(l)
                decay(l)
                attention(l)
                if l == 0:
                    add_residual("r0", 1)
                    squares(1)
                    normalise(1)
                    discretise(1)
                    dense()
                    coefficients(1)
                    add_residual("y", 2)
                    squares(2)
                    normalise(2)
                    dve.wait_ge(ev("h2"), KD)

            def token_rstd(step, event):
                dve.wait_ge(ev(event), 1)
                step(v.tensor_scalar(sm(116, 2), sm(100, 2), 1.0 / D, EPS, ALU.mult, ALU.add))
                step(v.tensor_tensor(sm(116, 2), sm(116, 2), sm(114, 2), ALU.mult))
                step(v.tensor_tensor(sm(116, 2), sm(116, 2), sm(114, 2), ALU.mult))
                step(v.tensor_scalar(sm(116, 2), sm(116, 2), -0.5, 1.5, ALU.mult, ALU.add))
                step(v.tensor_tensor(sm(102, 2), sm(116, 2), sm(114, 2), ALU.mult))

            token_rstd(step, "token_rstd_first")
            dve.wait_ge(ev("row_gains"), 32)
            for t in range(RT):
                v.scalar_tensor_tensor(htok[:, t, :], racc[:, t, :], sm(102 + t, 1), g_ffn_b, ALU.mult, ALU.mult
                                       ).then_inc(ev("htok"), 1)
            lg, gate, chosen, pos = sm(272, 16), sm(288, 16), sm(48, 16), sm(64, 16)
            eq, cs, sel1, sel2 = sm(304, 16), sm(120, 16), sm(136, 16), sm(152, 16)
            m1, m2 = sm(168, 2), sm(170, 2)
            g1, g2, den = sm(108, 2), sm(110, 2), sm(112, 2)

            def two(w):
                return w.rearrange("p (t e) -> p t e", t=RT)

            for t in range(RT):
                b = take(dve, f"lg{t}")
                release(v.tensor_copy(lg[:, NE * t:NE * t + NE], b[:, 0:NE]), f"lg{t}")
                evacuated(dve, f"lg{t}")

            def first_largest(best, pick):
                step(v.tensor_reduce(best, two(lg), AX.X, ALU.max))
                step(v.tensor_tensor(two(eq), two(lg), best.unsqueeze(2).to_broadcast([P, RT, NE]), ALU.is_equal))
                for t in range(RT):
                    w = slice(NE * t, NE * t + NE)
                    step(v.tensor_tensor_scan(cs[:, w], ones_row[:, 0:NE], eq[:, w], 0.0, ALU.mult, ALU.add))
                step(v.scalar_tensor_tensor(pick, cs, 1.0, eq, ALU.is_equal, ALU.mult))

            first_largest(m1, sel1)
            step(v.scalar_tensor_tensor(lg, sel1, NEG, lg, ALU.mult, ALU.add))
            first_largest(m2, sel2)
            v.tensor_tensor(sm(106, 2), m2, m1, ALU.subtract).then_inc(ev("margin"), 1)
            v.tensor_tensor(chosen, sel1, sel2, ALU.add).then_inc(ev("chosen"), 1)
            dve.wait_ge(ev("chosen"), 1)
            dve.wait_ge(ev("margin_exp"), 1)
            step(v.tensor_scalar(den, sm(104, 2), 1.0, None, ALU.add))
            step(v.reciprocal(g1, den))
            step(v.tensor_tensor(g2, g1, sm(104, 2), ALU.mult))
            for t in range(RT):
                w = slice(NE * t, NE * t + NE)
                step(v.tensor_scalar(gate[:, w], sel1[:, w], g1[:, t:t + 1], None, ALU.mult))
                step(v.scalar_tensor_tensor(gate[:, w], sel2[:, w], g2[:, t:t + 1], gate[:, w], ALU.mult, ALU.add))
            for t in range(RT):
                w = slice(NE * t, NE * t + NE)
                b = take(dve, f"rank{t}")
                release(v.scalar_tensor_tensor(pos[:, w], b[:, 0:NE], 1.0, chosen[:, w], ALU.add, ALU.mult), f"rank{t}")
                evacuated(dve, f"rank{t}")
            step(v.tensor_scalar(pos, pos, -1.0, None, ALU.add))
            jpos_t, jgate_t = sb("job_place", RT * 12), sb("job_gate", RT * 12)
            jpos, jgate = cut(jpos_t, 0, RT, 12), cut(jgate_t, 0, RT, 12)
            step(v.tensor_copy(jpos[:, :, 0:NE], two(pos)))
            step(v.tensor_copy(jgate[:, :, 0:NE], two(gate)))
            step(v.memset(jpos[:, :, NE:12], -1.0e6))
            step(v.memset(jgate[:, :, NE:12], 0.0))
            full, before, pick, tmp, row = (sm(176 + 8 * i) for i in range(5))
            b = take(dve, "count")
            release(v.tensor_scalar(full, b[:, 0:NE], float(P), None, ALU.is_gt), "count")
            evacuated(dve, "count")
            step(v.tensor_tensor_scan(before, ones_row[:, 0:NE], full, 0.0, ALU.mult, ALU.add))
            step(v.tensor_scalar(row[:, 3:4], before[:, NE - 1:NE], float(NE), None, ALU.add))
            wide = eq
            for n in range(3):
                step(v.scalar_tensor_tensor(pick, before, float(n + 1), full, ALU.is_equal, ALU.mult))
                step(v.tensor_tensor(tmp, pick, expert_iota, ALU.mult))
                step(v.tensor_reduce(row[:, n:n + 1], tmp, AX.X, ALU.add))
                step(v.tensor_reduce(sm(232, 1), pick, AX.X, ALU.add))
                step(v.tensor_scalar(sm(232, 1), sm(232, 1), -1.0, 1.0e6, ALU.add, ALU.mult))
                pb = pick.unsqueeze(1).to_broadcast([P, RT, NE])
                step(v.scalar_tensor_tensor(two(wide), two(pos), -float(P), pb, ALU.add, ALU.mult))
                step(v.tensor_reduce(jpos[:, :, NE + n], two(wide), AX.X, ALU.add))
                step(v.tensor_scalar(jpos[:, :, NE + n], jpos[:, :, NE + n], sm(232, 1), None, ALU.add))
                step(v.tensor_tensor(two(wide), two(gate), pb, ALU.mult))
                step(v.tensor_reduce(jgate[:, :, NE + n], two(wide), AX.X, ALU.add))
            v.tensor_copy(ints[:, 0:4], row[:, 0:4]).then_inc(ev("jobs_ready"), 1)
            dve.wait_ge(ev("jobs_ready"), 1)

            cur_t = sb("current_job", 8)
            moe_step = Chain(dve, ev("expert_steps"))

            def select(j):
                moe_step(v.tensor_copy(cur_t[:, 0:2], jpos[:, :, bass.ds(j, 1)] if not isinstance(j, int)
                                       else jpos[:, :, j:j + 1]))
                for t in range(RT):
                    ins = v.tensor_scalar(sel[:, t, :], slot_iota, cur_t[:, t:t + 1], None, ALU.is_equal)
                ins.then_inc(ev("sel_ready"), 1)

            def gather_lo(n):
                for b in range(2):
                    dve.wait_ge(ev("gather_hi"), n + 1 + b)
                    k = slice(4 * b, 4 * b + 4)
                    ins = v.tensor_tensor(h_lo[:, k, :], bank[2 + b][:, :].rearrange("p (k s) -> p k s", k=4),
                                          h_hi[:, k, :].bitcast(F32), ALU.subtract)
                ins.then_inc(ev("gather_split"), 1)

            def split_lo(j, m):
                dve.wait_ge(ev("split_hi"), NC * j + m + 1)
                v.tensor_tensor(w_lo[:, m % SPLITS, :], mslot(m), w_hi[:, m % SPLITS, :].bitcast(F32), ALU.subtract
                                ).then_inc(ev("split_lo"), 1)

            def turn_lo(j, fb):
                dve.wait_ge(ev("turn_hi"), 7 * j + fb + 1)
                v.tensor_tensor(gT_lo[:, fb % 2, :], bank[4][:, :], gT_hi[:, fb % 2, :].bitcast(F32), ALU.subtract
                                ).then_inc(ev("turn_split"), 1)

            def add_scattered(n):
                for i in range(4):
                    r = racc[:, i // 2, 512 * (i % 2):512 * (i % 2) + 512]
                    dve.wait_ge(ev("scattered"), 4 * n + i + 1)
                    v.tensor_tensor(r, r, bank[2 + i][:, :], ALU.add).then_inc(ev("added"), 1)

            v.memset(ysb, 0.0).then_inc(ev("y_evac"), 2)
            v.memset(scat, 0.0).then_inc(ev("scat_evac"), 1)
            for m in range(SPLITS):
                split_lo(0, m)
            select(0)
            first = moe_step.n
            gather_lo(0)
            n_jobs = dve.value_load(ints[0:1, 3:4], min_val=NE, max_val=MAX_JOBS)
            STEPS = 3
            with dve.Fori(0, n_jobs) as j:
                moe_step.base, moe_step.n = STEPS * j + first, 0
                for c in range(NC):
                    if c == GATHER_AFTER:
                        turn_lo(j, NFB - 1)
                    if c == NC - 1:
                        dve.wait_ge(mchunk_used, NC * j + NC)
                        v.tensor_copy(ysb[:, 512:D], bank[7][:, :]).then_inc(ev("y_evac"), 1)
                    if c in gate_after:
                        fb = gate_after[c]
                        dve.wait_ge(ev("silu_done"), 7 * j + fb + 1)
                        dve.wait_ge(mchunk_used, NC * j + c + 1)
                        v.tensor_tensor(g_e[:, fb % 2, :], e1[:, fb % 2, :], bank[2 * (fb % 2) + 1][:, :], ALU.mult
                                        ).then_inc(ev("g_ready"), 1)
                    split_lo(j, c + SPLITS)
                    if c in turn_after:
                        turn_lo(j, turn_after[c])
                    if c == 1:
                        add_scattered(j)
                    if c == 3:
                        moe_step(v.tensor_copy(cur_t[:, 2:4], jpos[:, :, bass.ds(j, 1)]))
                        moe_step(v.tensor_copy(cur_t[:, 4:6], jgate[:, :, bass.ds(j, 1)]))
                        for t in range(RT):
                            ins = v.tensor_scalar(selg[:, t, :], slot_iota, cur_t[:, 2 + t:3 + t],
                                                  cur_t[:, 4 + t:5 + t], ALU.is_equal, ALU.mult)
                        ins.then_inc(ev("selg_ready"), 1)
                    if c == 28:
                        select(j + 1)
                    if c == GATHER_AFTER:
                        gather_lo(2 * j + 2)
                assert moe_step.n == STEPS
            add_scattered(n_jobs)
            dve.wait_ge(ev("added"), 4 * n_jobs + 4)

            end = Chain(dve, ev("final_steps"))
            dve.sem_inc(ev("final_ready"), 1)
            token_rstd(end, "final_rstd_first")
            for t in range(RT):
                v.scalar_tensor_tensor(racc[:, t, :], racc[:, t, :], sm(102 + t, 1), g_fin_b, ALU.mult, ALU.mult
                                       ).then_inc(ev("out_ready"), 1)


_INS = ["x", "meta_tokens", "norm_mix_g", "w_in", "w_out", "ssm_lambda_re", "ssm_lambda_im", "ssm_log_dt",
        "ssm_b_re", "ssm_b_im", "ssm_c_re", "ssm_c_im", "ssm_d", "ssm_w_glu", "diff_lambda_q1", "diff_lambda_k1",
        "diff_lambda_q2", "diff_lambda_k2", "diff_subln_g", "fox_forget_b", "norm_ffn_g", "dense_w1", "dense_w3",
        "dense_w2", "moe_router", "moe_w1", "moe_w3", "moe_w2", "final_norm_g"]


def kernel(**inputs):
    import numpy as _np
    import concourse.bacc as _bacc
    from concourse import mybir as _mybir
    from concourse.bass_utils import run_bass_kernel_spmd as _run

    nc = _bacc.Bacc("TRN2", target_bir_lowering=False, num_devices=1)
    arrays, args = {}, {}
    for name in _INS:
        x = _np.ascontiguousarray(inputs[name])
        arrays[f"in_{name}"] = x
        args[name] = nc.dram_tensor(f"in_{name}", x.shape, _mybir.dt.from_np(x.dtype), kind="ExternalInput").ap()
    out = nc.dram_tensor("out_0", (1, SEQ, D), _mybir.dt.float32, kind="ExternalOutput").ap()
    build(nc, args, out)
    r = _run(nc, [arrays], core_ids=[0])
    return r.results[0]["out_0"]
```

```python
import math

import concourse.bass as bass
from concourse import mybir
from contextlib import ExitStack

F32 = mybir.dt.float32
I32 = mybir.dt.int32
F32R = mybir.dt.float32r
ALU = mybir.AluOpType
ACT = mybir.ActivationFunctionType
AX = mybir.AxisListType

P = 128
DEPTH = 2
D = 1024
KD = D // P
N_META, SEQ = 16, 256
L = N_META + SEQ
TT = [(0, 128), (128, 128), (256, 16)]
RT = SEQ // P
EPS = 1e-6
SSM_W, SSM_C, STATE = 256, 16, 64
NST = 8
DH, DQK, DV = 4, 64, 128
FH, FD = 4, 64
FF = 2816
NFF = FF // P
NE, FE = 8, 3584
NFB = FE // 512
MAX_JOBS = 11
SCALE = DQK ** -0.5
MAGIC = 12582912.0
LN2_HI, LN2_LO = 0.693359375, -2.12194440e-4
SIN_2PI = 6.2831850
NEG = -1.0e30
SLOT = 4096
RING = 5
HALF = SLOT // 2
MRING, SPLITS = 7, 3
DRAW = 4
DPARTS = [(0, 12), (12, 10)]
TAIL = 32
UNITS = [u for k in ("d", "f") for u in [(k, None, 2)] + [(k, h, t) for h in range(4) for t in range(2)]]
KIND_UNITS = len(UNITS) // 2

def heads_last(u):
    return UNITS[u][2] == 1

def head_unit(kind, h):
    return UNITS.index((kind, h, 1))


def build(nc, a, out):
    ctx = ExitStack()
    with ctx:
        ctx.enter_context(nc.allow_non_contiguous_dma(reason="small parameter loads"))

        def sb(name, cols, dt=F32):
            return ctx.enter_context(nc.sbuf_tensor(name, [P, cols], dt))

        ring_at = -(-nc.sbuf_base // 32) * 32
        ring = sb("weight_ring", RING * SLOT)
        late = sb("late_region", 2 * SLOT)
        res_at = ring_at + 4 * (RING + 2) * SLOT
        region = {n: sb(n, KD * L) for n in ("resT", "mixedT", "hT", "cosT", "sinT", "foxqk")}
        attn = sb("attn_temps", 2720)
        bank = [ctx.enter_context(nc.psum_tensor(f"bank{i}", [P, 512], F32)) for i in range(8)]

        def cut(tensor, start, *dims):
            n = math.prod(dims)
            v = tensor[:, start:start + n]
            if len(dims) == 2:
                v = v.rearrange("p (a b) -> p a b", b=dims[1])
            if len(dims) == 3:
                v = v.rearrange("p (a b c) -> p a b c", b=dims[1], c=dims[2])
            return v

        resT, hT, mixedT = (cut(region[n], 0, KD, L) for n in ("resT", "hT", "mixedT"))
        cosT, sinT = (cut(region[n], 0, NST, L) for n in ("cosT", "sinT"))
        fqa, fka = cut(region["foxqk"], 0, FH, L), cut(region["foxqk"], FH * L, FH, L)
        sqT = mixedT
        dqT, dkT = cut(late, 0, DH, L), cut(late, 1088, DH, L)
        uT = cut(late, 2176, 2, L)
        vtok = cut(late, 2720, 3, 768)
        w_scan = cut(late, 5024, 2, 2, L)
        x_ssm = cut(late, 6112, 2, 2, L)
        t_dve, t_pool = cut(late, 7200, L), cut(late, 7472, L)
        silu_t = cut(late, 2 * DPARTS[0][1] * L, 2, L)
        g_raw = cut(region["mixedT"], 0, 2, L)
        xtok = cut(late, 0, 3, D)
        s_buf = [cut(attn, 0, 2, L), cut(attn, 544, 2, L), cut(region["sinT"], 1088, 2, L)]
        e_buf = [cut(attn, 1088, 2, L), cut(attn, 1632, 2, L), cut(region["sinT"], 544, 2, L)]
        a_buf = cut(attn, 2176, 2, L)
        aT_tail = cut(late, 7744, 2, 3, 64)
        aT = cut(late, 5024, 2, 2, 2 * P)
        o_buf_t, sq_o_t, rs_t = sb("o_buf", 2 * L), sb("o_square", 2 * L), sb("rstd", L)
        t_dve2, t_pool2 = cut(late, 7744, L), sq_o_t[:, 0:L]
        rs0_t = sb("rstd_first", L)
        o_buf, sq_o = cut(o_buf_t, 0, 2, L), cut(sq_o_t, 0, 2, L)
        fgz, fgm, fgc = (cut(attn, i * L, L) for i in range(3))
        ys, yq, ye, gy = (cut(region["cosT"], i * 544, 2, L) for i in range(4))
        glu_e = cut(region["sinT"], 0, 2, L)
        racc = cut(region["foxqk"], 0, RT, D)
        mhT = cut(region["hT"], 0, KD, SEQ)
        htok = cut(region["cosT"], 0, RT, D)
        g_ffn_b, g_fin_b = cut(region["sinT"], 0, D), cut(region["sinT"], D, D)
        ysb = cut(region["hT"], 0, D)
        def split_pair(name, at, *dims):
            n = math.prod(dims)
            pair = []
            for i, part in enumerate(("hi", "lo")):
                t = nc.alloc_sbuf_tensor_at(f"{name}_{part}", [P, n], F32R, offset=at + 4 * n * i)
                pair.append(t[:, :].rearrange("p (a b) -> p a b", b=dims[-1]))
            return pair

        dw = nc.alloc_sbuf_tensor_at("dense_weights", [P, SPLITS * SLOT], F32R, offset=ring_at + 4 * DRAW * HALF
                                     )[:, :].rearrange("p (s h n) -> p s h n", h=2, n=HALF)
        dw_hi, dw_lo = dw[:, :, 0, :], dw[:, :, 1, :]
        dg_hi, dg_lo = split_pair("dense_gT", ring_at + 4 * RING * SLOT, DPARTS[0][1], L)
        dh_hi, dh_lo = (nc.alloc_sbuf_tensor_at(f"dense_hT_{part}", [P, KD * L], F32R, offset=res_at + 4 * KD * L * at
                                                )[:, :].rearrange("p (a b) -> p a b", b=L)
                        for part, at in (("hi", 6), ("lo", 2)))
        w_hi, w_lo = split_pair("weights", ring_at + 4 * MRING * HALF, SPLITS, HALF)
        gT_hi, gT_lo = split_pair("expert_gT", res_at, 2, 512)
        h_hi, h_lo = split_pair("expert_hT", res_at + 4 * KD * L, KD, P)
        e1, g_e = cut(attn, 0, 2, 512), cut(region["hT"], 1024, 2, 512)
        sel, selg, scat = cut(attn, 1024, RT, P), cut(attn, 1280, RT, P), cut(attn, 1536, SEQ)
        const_t = sb("constants", 6 * P + 2 * L + 9)
        ident, avgD, avgV, onesF, tri, slot_iota = (cut(const_t, i * P, P) for i in range(6))
        time_iota, ones_row = cut(const_t, 6 * P, L), cut(const_t, 6 * P + L, L)
        expert_iota = cut(const_t, 6 * P + 2 * L, 8)
        eps_col = cut(const_t, 6 * P + 2 * L + 8, 1)
        mask_t = sb("causal_mask", 3 * L)
        mask = cut(mask_t, 0, 3, L)
        rows_t, prm_t = sb("param_rows", P), sb("param_cols", 70 + 16)
        prm = prm_t
        dt_rows, dt_wide = sb("dt_rows", 2), sb("dt_wide", P)
        b_raw_t, c_raw_t = sb("b_raw", 2 * NST * 16), sb("c_raw", 4 * STATE)
        b_raw, c_raw = cut(b_raw_t, 0, 2, NST, 16), cut(c_raw_t, 0, 2, 2, STATE)
        b_exp_t, c_exp_t = sb("b_blocks", 512), sb("c_blocks", 512)
        b_exp, c_exp = cut(b_exp_t, 0, 2, NST, 32), cut(c_exp_t, 0, 4, P)
        bT_t, cT_t = sb("bT", 512), sb("cT", 512)
        bT, cT = cut(bT_t, 0, 2, 2, P), cut(cT_t, 0, 2, 2, P)
        glu_t = sb("w_glu", 1024)
        w_glu = cut(glu_t, 0, 2, 512)
        lam_t = sb("lambda_vectors", 4 * 2 * 64)
        lam_v = cut(lam_t, 0, 4, 2, 64)
        fb_t = sb("forget_bias", 2)
        router_t = sb("router", KD * NE)
        router = cut(router_t, 0, KD, NE)
        small = sb("small", 340)
        ints = sb("ints", 20, I32)

        def sm(i, n=8):
            return small[:, i:i + n]

        events = {}

        def ev(name):
            if name not in events:
                events[name] = ctx.enter_context(nc.semaphore(name))
            return events[name]

        bank_full = [ctx.enter_context(nc.semaphore(f"bank_full{b}")) for b in range(6)]
        bank_free = [ctx.enter_context(nc.semaphore(f"bank_free{b}")) for b in range(6)]
        dslot_full = [ctx.enter_context(nc.semaphore(f"dense_slot_full{s}")) for s in range(DRAW)]
        slot_full = [ctx.enter_context(nc.semaphore(f"slot_full{s}")) for s in range(RING)]
        chunk_used = ctx.enter_context(nc.semaphore("chunk_used"))
        mslot_full = [ctx.enter_context(nc.semaphore(f"expert_slot_full{s}")) for s in range(MRING)]
        mchunk_used = ctx.enter_context(nc.semaphore("expert_chunk_used"))
        groups = {}

        def open_group(pe, name):
            n = len(groups)
            groups[name] = (n % 6, n // 6)
            if n >= 6:
                pe.wait_ge(bank_free[n % 6], n // 6)
            return bank[n % 6]

        def close_group(ins, name):
            ins.then_inc(bank_full[groups[name][0]], 1)

        def take(eng, name):
            b, use = groups[name]
            eng.wait_ge(bank_full[b], use + 1)
            return bank[b]

        def release(ins, name):
            ins.then_inc(bank_free[groups[name][0]], 1)

        def evacuated(eng, name):
            b, use = groups[name]
            eng.wait_ge(bank_free[b], use + 1)

        class Chain:

            def __init__(self, eng, sem):
                self.eng, self.sem, self.base, self.n = eng, sem, 0, 0

            def __call__(self, ins):
                self.n += 1
                ins.then_inc(self.sem, 1)
                self.eng.wait_ge(self.sem, self.base + self.n)

        chunks, FIRST_PART = [], 8

        SLOTS = [0, 1, 2, 3, 4, 0, 1, 2] + [0, 1, 2, 3, 4, 0, 3, 4]

        def slot_of(i):
            return SLOTS[i]

        def slot_free(eng, slot, before):
            eng.wait_ge(chunk_used, max(i for i in range(before) if slot_of(i) == slot) + 1)

        def chunk(name, src, k, cols):
            at = slot_of(len(chunks)) * SLOT
            v = ring[:, at:at + k * cols]
            chunks.append((name, src, v.rearrange("p (k n) -> p k n", n=cols)))

        for l in range(DEPTH):
            w_in = a["w_in"][l, :, :].rearrange("(k p) n -> p k n", p=P)
            for name, lo, hi in (("u", 0, 256), ("fvg", 2304, 2564), ("dq", 256, 768), ("dk", 768, 1280),
                                 ("dv", 1280, 1792), ("fqk", 1792, 2304)):
                chunk(f"{name}{l}", w_in[:, :, lo:hi], KD, hi - lo)
            w_out = a["w_out"][l, :, :].rearrange("(k p) n -> p k n", p=P)
            for half in range(2):
                chunk(f"out{l}{half}", w_out[:, :, 512 * half:512 * half + 512], KD, 512)
            assert len(chunks) == FIRST_PART * (l + 1)
        where = {c[0]: i for i, c in enumerate(chunks)}

        def chunk_ready(pe, name):
            i = where[name]
            pe.wait_ge(slot_full[slot_of(i)], 16 * sum(slot_of(c) == slot_of(i) for c in range(i + 1)))
            return chunks[i][2]

        dense_order = []
        for f0, n in DPARTS:
            dense_order += [(kind, f, 2, None) for f in range(f0, f0 + n, 2) for kind in ("w1", "w3")]
            dense_order += [("w2", f, min(4, f0 + n - f), half) for half in range(2) for f in range(f0, f0 + n, 4)]
        NDC = len(dense_order)

        def dense_chunk(c):
            kind, f, n, half = dense_order[c]
            if kind == "w2":
                src = a["dense_w2"][0, P * f:P * (f + n), 512 * half:512 * half + 512]
            else:
                src = a[f"dense_{kind}"][0, :, P * f:P * (f + n)]
            return src.rearrange("(k p) n -> p k n", p=P), n * (512 if kind == "w2" else D)

        def dslot(c):
            return ring[:, (c % DRAW) * HALF:(c % DRAW) * HALF + dense_chunk(c)[1]]

        def dsplit(c):
            return (c + 1) % SPLITS

        order = [(0, "w1"), (0, "w3")]
        for fb in range(1, NFB):
            order += [(fb, "w1"), (fb, "w3"), (fb - 1, "w2")]
        order += [(NFB - 1, "w2")]
        NC = 2 * len(order)
        assert NC % MRING == 0 and NC % SPLITS == 0

        def mslot(c):
            return ring[:, (c % MRING) * HALF:(c % MRING) * HALF + HALF]

        def expert_chunk(e, c):
            (fb, kind), half = order[c // 2], c % 2
            if kind == "w2":
                lo = 512 * fb + 256 * half
                src = a["moe_w2"][0, e, lo:lo + 256, :].rearrange("(k p) n -> p k n", p=P)
                return src, mslot(c).rearrange("p (k n) -> p k n", n=D)
            src = a[f"moe_{kind}"][0, e, 512 * half:512 * half + 512, 512 * fb:512 * fb + 512]
            return src.rearrange("(k p) n -> p k n", p=P), mslot(c).rearrange("p (k n) -> p k n", n=512)

        def last_chunk(fb, kind):
            return 2 * order.index((fb, kind)) + 1

        silu_after = {last_chunk(fb, "w1"): fb for fb in range(NFB)}
        gate_after = {last_chunk(fb, "w3"): fb for fb in range(NFB)}
        turn_after = {last_chunk(fb + 1, "w1"): fb for fb in range(NFB - 1)}
        FIRST_DOWN = last_chunk(0, "w2") - 1
        SCATTER_AFTER = last_chunk(3, "w3") + 1
        GATHER_AFTER = NC - 3

        N_PARAM = 9
        EARLY = (15, 13)
        POOL_PHASES = 6
        VECTOR_TURNS = (2, 5)

        def turned_states(eng, l, i):
            if i in VECTOR_TURNS:
                eng.wait_ge(ev(f"x_vector{l}"), VECTOR_TURNS.index(i) + 1)
            else:
                eng.wait_ge(ev(f"x_pool{l}"), i + 1 - sum(j < i for j in VECTOR_TURNS))

        GLU_AT = 2
        SSM_AT = [{6: 0, 7: 1, 8: 2, 9: 3, 10: 4, 11: 5, 12: 6, 13: 7},
                  {0: 0, 1: 1, 3: 2, 4: 3, 6: 4, 7: 5, 9: 6, 10: 7}]

        def phase_tile(engine, step, i, tmp):
            step(engine.tensor_scalar(sinT[:, i, :], time_iota, sm(192)[:, i:i + 1], None, ALU.mult))
            step(engine.tensor_scalar(cosT[:, i, :], sinT[:, i, :], 0.25, None, ALU.add))
            for tab in (sinT, cosT):
                step(engine.tensor_scalar(tmp, tab[:, i, :], MAGIC, -MAGIC, ALU.add, ALU.add))
                step(engine.tensor_tensor(tab[:, i, :], tab[:, i, :], tmp, ALU.subtract))

        def probs_ready(eng, l, u):
            if u < KIND_UNITS:
                eng.wait_ge(ev(f"probs_d{l}"), u + 1)
            else:
                eng.wait_ge(ev(f"probs_f{l}"), u + 1 - KIND_UNITS)

        dense_done, downs = {}, []

        def dense_used(eng, c):
            if isinstance(dense_done[c], str):
                take(eng, dense_done[c])
            else:
                eng.wait_ge(ev("dense_down_used"), dense_done[c])

        def load_ssm(eng, l):
            if l:
                eng.wait_ge(ev(f"c_blocks{l - 1}"), 1)
            for c, n in enumerate(("re", "im")):
                eng.dma_start(b_raw[:, c, :, :], a[f"ssm_b_{n}"][l, :, :, :].rearrange(
                    "(i g) n c -> (g n) i c", g=2)).then_inc(ev("ssm_loaded"), 16)
                eng.dma_start(c_raw[:, :, c, :], a[f"ssm_c_{n}"][l, :, :, :].rearrange(
                    "(m g) c n -> (g c) m n", m=2)).then_inc(ev("ssm_loaded"), 16)
            eng.dma_start(w_glu[:, :, :], a["ssm_w_glu"][l, :, :].rearrange("(k p) n -> p k n", p=P)
                          ).then_inc(ev("glu_loaded"), 16)


        block = ctx.enter_context(nc.Block())

        @block.tensor
        def _(pe):
            def mm(o, lhsT, rhs, start, stop):
                return nc.tensor.matmul(o, lhsT, rhs, start=start, stop=stop)

            def done_with_chunk(ins):
                ins.then_inc(chunk_used, 1)

            def transposed_params():
                pe.wait_ge(ev("identity_ready"), 2)
                pe.wait_ge(ev("params_loaded"), 16 * N_PARAM)
                b = open_group(pe, "prm")
                close_group(nc.tensor.transpose(b[:, 0:70], rows_t[0:70, :], ident[0:70, 0:70]), "prm")
                pe.wait_ge(ev("dt_wide_ready"), 1)
                b = open_group(pe, "ldt")
                close_group(nc.tensor.transpose(b[:, 0:16], dt_wide[0:16, :], ident[0:16, 0:16]), "ldt")

            def ssm_weights(l):
                pe.wait_ge(ev(f"b_blocks{l}"), 1)
                b = open_group(pe, f"bT{l}")
                for m in range(2):
                    for c in range(2):
                        ins = nc.tensor.transpose(b[:, (2 * m + c) * P:(2 * m + c + 1) * P],
                                                  b_exp[:, c, 4 * m:4 * m + 4, :], ident)
                close_group(ins, f"bT{l}")
                pe.wait_ge(ev(f"c_blocks{l}"), 1)
                b = open_group(pe, f"cT{l}")
                for i in range(4):
                    ins = nc.tensor.transpose(b[:, i * P:(i + 1) * P], c_exp[:, i, :], ident)
                close_group(ins, f"cT{l}")

            def feature_norm(n, tiles):
                b = open_group(pe, f"ssq{n}") if tiles[0] == 0 else bank[groups[f"ssq{n}"][0]]
                for k in tiles:
                    if k == 0:
                        pe.wait_ge(ev("constants_ready"), 1)
                        pe.wait_ge(ev(f"squares_act{n}"), 1)
                    if k == 4:
                        pe.wait_ge(ev(f"squares_act{n}"), 2)
                    if k == 6:
                        pe.wait_ge(ev(f"squares_dve{n}"), 1)
                    ins = mm(b[:, 0:L], avgD, sqT[:, k, :], k == 0, k == KD - 1)
                if tiles[-1] == KD - 1:
                    close_group(ins, f"ssq{n}")

            def project(n, name, w, lo, m, rhs_ready):
                b = open_group(pe, name)
                for k in range(KD):
                    if rhs_ready:
                        pe.wait_ge(ev(f"h{n}"), k + 1)
                    ins = mm(b[0:m, 0:L], w[:, k, lo:lo + m], hT[:, k, :], k == 0, k == KD - 1)
                close_group(ins, name)
                return ins

            def ssm_in(l, i):
                r = i % 4
                if i == 0:
                    evacuated(pe, f"bT{l}")
                    evacuated(pe, f"z{l}u1")
                for c in range(2):
                    name = f"bu{l}{i}{c}"
                    b = open_group(pe, name)
                    close_group(mm(b[:, 0:L], bT[32 * r:32 * r + 32, i // 4, c, :],
                                   uT[32 * r:32 * r + 32, i // 4, :], True, True), name)

            def ssm_out(l, i):
                r, m = i % 4, i // 4
                if i == 0:
                    evacuated(pe, f"cT{l}")
                turned_states(pe, l, i)
                for c in range(2):
                    ins = mm(bank[6 + m][32 * r:32 * r + 32, 0:L], cT[:, m, c, 32 * r:32 * r + 32],
                             x_ssm[:, i % 2, c, :], c == 0, c == 1)
                ins.then_inc(ev(f"y_done{l}"), 1)

            def mixer_inputs(l, n):
                steps = []

                def feature(cname, key, cols, last):
                    def f(key=key, cols=cols, last=last):
                        w = chunk_ready(pe, f"{cname}{l}")
                        ins = project(n, f"z{l}{key}", w, cols[0], cols[1], False)
                        if last:
                            pe.wait_ge(bank_full[groups[f"z{l}{key}"][0]], groups[f"z{l}{key}"][1] + 1)
                            pe.sem_inc(chunk_used, 1)
                    steps.append(f)

                def tokens(cname, key, cols, t, last):
                    def f():
                        w = chunk_ready(pe, f"{cname}{l}")
                        q0, qn = TT[t]
                        name = f"z{l}{key}{t}"
                        b = open_group(pe, name)
                        for k in range(KD):
                            ins = mm(b[0:qn, 0:cols], hT[:, k, q0:q0 + qn], w[:, k, 0:cols], k == 0, k == KD - 1)
                        close_group(ins, name)
                        if last:
                            pe.wait_ge(bank_full[groups[name][0]], groups[name][1] + 1)
                            pe.sem_inc(chunk_used, 1)
                    steps.append(f)

                w = chunk_ready(pe, f"u{l}")
                for m in range(2):
                    ins = project(n, f"z{l}u{m}", w, P * m, P, m == 0)
                name = f"z{l}u1"
                pe.wait_ge(bank_full[groups[name][0]], groups[name][1] + 1)
                pe.sem_inc(chunk_used, 1)
                for t in range(3):
                    tokens("fvg", "fv", 256, t, False)
                feature("fvg", "fg", (256, FH), True)
                for cname in ("dq", "dk"):
                    for h in range(DH):
                        feature(cname, f"{cname}{h}", (P * h, P), h == DH - 1)
                for t in range(3):
                    tokens("dv", "dv", 512, t, t == 2)
                for i in range(4):
                    feature("fqk", f"fqk{i}", (P * i, P), i == 3)
                def tile_of_states(i):
                    if i == 0:
                        ssm_weights(l)
                    ssm_in(l, i)
                    if i >= 2:
                        ssm_out(l, i - 2)

                for j in range(EARLY[l]):
                    steps[j]()
                    if j in SSM_AT[l]:
                        tile_of_states(SSM_AT[l][j])
                for i in range(len(SSM_AT[l]), NST):
                    tile_of_states(i)
                return steps[EARLY[l]:]

            def scores(l, u):
                kind, h, t = UNITS[u]
                q0, kmax = P * t, sum(TT[t])
                if u == 0:
                    evacuated(pe, f"z{l}dk3")
                    evacuated(pe, f"z{l}dq3")
                if u == KIND_UNITS:
                    evacuated(pe, f"z{l}fqk3")
                    pe.wait_ge(ev(f"decay_rows{l}"), 2)
                for m in range(2 if kind == "d" else 1):
                    name = f"s{l}_{u}_{m}"
                    b = open_group(pe, name)
                    if kind == "d":
                        q, k = (x[64 * m:64 * m + 64, :, :] for x in (dqT, dkT))
                    else:
                        q, k = fqa[0:100, :, :], fka[0:100, :, :]
                    if h is None:
                        for hh in range(4):
                            ins = mm(b[TAIL * hh:TAIL * (hh + 1), 0:L], q[:, hh, L - TAIL:L], k[:, hh, :], True, True)
                    else:
                        ins = mm(b[:, 0:kmax], q[:, h, q0:q0 + P], k[:, h, 0:kmax], True, True)
                    close_group(ins, name)

            def turn_probs(l, u):
                t = UNITS[u][2]
                probs_ready(pe, l, u)
                name = f"at{l}_{u}"
                b = open_group(pe, name)
                for kt in range(t + 1):
                    k0, kn = TT[kt]
                    ins = nc.tensor.transpose(b[0:kn, P * kt:P * kt + P], a_buf[:, u % 2, k0:k0 + kn], ident)
                close_group(ins, name)

            def values(l, u):
                kind, h, _ = UNITS[u]
                evacuated(pe, f"at{l}_{u}")
                if kind == "f":
                    evacuated(pe, f"z{l}fv2")
                    v, dv = vtok[:, :, 512 + FD * h:512 + FD * h + FD], FD
                else:
                    evacuated(pe, f"z{l}dv2")
                    v, dv = vtok[:, :, DV * h:DV * h + DV], DV
                name = f"o{l}_{u}"
                b = open_group(pe, name)
                for kt in range(2):
                    mm(b[0:dv, P * kt:2 * P], v[:, kt, :], aT[:, h % 2, kt, P * kt:2 * P], kt == 0, kt == 1)
                for kt, (k0, kn) in enumerate(TT):
                    ins = mm(b[0:dv, 2 * P:L], v[0:kn, kt, :], aT_tail[0:kn, "df".index(kind), kt, 16 * h:16 * h + 16],
                             kt == 0, kt == 2)
                close_group(ins, name)

            def head_norm(l, u):
                h = UNITS[u][1]
                pe.wait_ge(ev(f"o_square{l}"), h + 1)
                name = f"hn{l}_{h}"
                b = open_group(pe, name)
                close_group(mm(b[:, 0:L], avgV, sq_o[:, h % 2, :], True, True), name)

            def glu(l):
                pe.wait_ge(ev("glu_loaded"), 16 * (l + 1))
                pe.wait_ge(ev(f"gelu_ready{l}"), 1)
                for m in range(4):
                    name = f"glu{l}{m}"
                    b = open_group(pe, name)
                    for k in range(2):
                        ins = mm(b[:, 0:L], w_glu[:, k, P * m:P * m + P], gy[:, k, :], k == 0, k == 1)
                    close_group(ins, name)

            def attention(l, projections):
                scores(l, 0)
                scores(l, 1)
                ssm_out(l, NST - 2)
                ssm_out(l, NST - 1)
                scores(l, 2)
                for u in range(len(UNITS) + 2):
                    if u < len(projections):
                        projections[u]()
                    if u + 3 < len(UNITS):
                        scores(l, u + 3)
                    if 1 <= u <= len(UNITS) and heads_last(u - 1):
                        values(l, u - 1)
                    if u >= 2 and heads_last(u - 2) and UNITS[u - 2][0] == "d":
                        head_norm(l, u - 2)
                    if u < len(UNITS):
                        turn_probs(l, u)
                    if u == GLU_AT:
                        glu(l)

            def mix_ready(l, k):
                if k == 0:
                    pe.wait_ge(ev(f"ssm_out{l}"), 2)
                elif k == 2:
                    pe.wait_ge(ev(f"diff_out{l}"), DH)
                elif k == 6:
                    for h in range(FH):
                        evacuated(pe, f"o{l}_{head_unit('f', h)}")

            def output_projection_features(l):
                for half in range(2):
                    w = chunk_ready(pe, f"out{l}{half}")
                    for m in range(4):
                        name = f"r{l}{4 * half + m}"
                        b = open_group(pe, name)
                        for k in range(KD):
                            if half == 0 and m == 0:
                                mix_ready(l, k)
                            ins = mm(b[:, 0:L], w[:, k, P * m:P * m + P], mixedT[:, k, :], k == 0, k == KD - 1)
                        close_group(ins, name)
                    pe.wait_ge(bank_full[groups[name][0]], groups[name][1] + 1)
                    pe.sem_inc(chunk_used, 1)

            def output_projection_tokens(l):
                for half in range(2):
                    w = chunk_ready(pe, f"out{l}{half}")
                    for t in range(RT):
                        tok = slice(N_META + P * t, N_META + P * t + P)
                        name = f"rt{t}{half}"
                        b = open_group(pe, name)
                        for k in range(KD):
                            if half == 0 and t == 0:
                                mix_ready(l, k)
                            mm(b[:, :], mixedT[:, k, tok], w[:, k, :], k == 0, False)
                        for j in range(4):
                            ins = mm(b[:, P * j:P * j + P], resT[:, 4 * half + j, tok], ident, False, j == 3)
                        close_group(ins, name)
                    pe.wait_ge(bank_full[groups[name][0]], groups[name][1] + 1)
                    pe.sem_inc(chunk_used, 1)

            def dense_up(c):
                kind, f0, n, _ = dense_order[c]
                pe.wait_ge(ev("dense_split_lo"), c + 1)
                wh, wl = (w[:, dsplit(c), :].rearrange("p (k n) -> p k n", k=KD) for w in (dw_hi, dw_lo))
                for f in range(f0, f0 + n):
                    name = f"f{'a' if kind == 'w1' else 'b'}{f}"
                    b, cols = open_group(pe, name), slice(P * (f - f0), P * (f - f0) + P)
                    for k in range(KD):
                        if c == 0 and f == 0:
                            pe.wait_ge(ev("dense_h_lo"), k + 1)
                        mm(b[:, 0:L], wh[:, k, cols], dh_hi[:, k, :], k == 0, False)
                        mm(b[:, 0:L], wh[:, k, cols], dh_lo[:, k, :], False, False)
                        ins = mm(b[:, 0:L], wl[:, k, cols], dh_hi[:, k, :], False, k == KD - 1)
                    close_group(ins, name)
                dense_done[c] = name

            def dense_down(c, part):
                kind, f0, n, half = dense_order[c]
                first, count = DPARTS[part]
                pe.wait_ge(ev("dense_split_lo"), c + 1)
                wh, wl = (w[:, dsplit(c), 0:512 * n].rearrange("p (k n) -> p k n", k=n) for w in (dw_hi, dw_lo))
                names = [f"y{part}{4 * half + m}" for m in range(4)]
                for m in range(4):
                    b = open_group(pe, names[m]) if f0 == first else bank[groups[names[m]][0]]
                    cols = slice(P * m, P * m + P)
                    for f in range(f0, f0 + n):
                        if half == 0 and m == 0:
                            pe.wait_ge(ev("dense_g_lo"), f + 1)
                        mm(b[:, 0:L], wh[:, f - f0, cols], dg_hi[:, f - first, :], f == first, False)
                        mm(b[:, 0:L], wh[:, f - f0, cols], dg_lo[:, f - first, :], False, False)
                        ins = mm(b[:, 0:L], wl[:, f - f0, cols], dg_hi[:, f - first, :], False,
                                 f == first + count - 1)
                    if f0 + n == first + count:
                        close_group(ins, names[m])
                        dense_done[c] = names[m]
                if f0 + n < first + count:
                    downs.append(c)
                    ins.then_inc(ev("dense_down_used"), 1)
                    dense_done[c] = len(downs)

            def dense():
                for c in range(NDC):
                    kind, f, _, _ = dense_order[c]
                    if c == NDC - 1:
                        feature_norm(2, range(0, 4))
                    if kind == "w2":
                        dense_down(c, int(f >= DPARTS[1][0]))
                    else:
                        dense_up(c)

            pe.wait_ge(ev("identity_ready"), 2)
            pe.wait_ge(ev("x_loaded"), 16 * 4)
            for k in range(KD):
                b = open_group(pe, f"xT{k}")
                for t, (q0, qn) in enumerate(TT):
                    ins = nc.tensor.transpose(b[:, q0:q0 + qn], xtok[0:qn, t, P * k:P * k + P], ident[0:qn, 0:qn])
                close_group(ins, f"xT{k}")
                if k == 5:
                    feature_norm(0, range(0, 4))
            for l in range(DEPTH):
                feature_norm(2 * l, range(4, KD))
                if l == 0:
                    transposed_params()
                attention(l, mixer_inputs(l, 2 * l))
                if l == 0:
                    output_projection_features(l)
                    feature_norm(1, range(0, KD))
                    dense()
            output_projection_tokens(1)

            for j in range(4):
                b = open_group(pe, f"mh{j}")
                for k in range(2):
                    for t in range(RT):
                        if j == 0 and k == 0:
                            pe.wait_ge(ev("htok"), t + 1)
                        ins = nc.tensor.transpose(b[:, (2 * k + t) * P:(2 * k + t + 1) * P],
                                                  htok[:, t, (2 * j + k) * P:(2 * j + k + 1) * P], ident)
                close_group(ins, f"mh{j}")
            pe.wait_ge(ev("router_loaded"), 16)
            for t in range(RT):
                b = open_group(pe, f"lg{t}")
                for k in range(KD):
                    if t == 0 and k % 2 == 0:
                        evacuated(pe, f"mh{k // 2}")
                    ins = mm(b[:, 0:NE], mhT[:, k, P * t:P * t + P], router[:, k, :], k == 0, k == KD - 1)
                close_group(ins, f"lg{t}")
            chosen = sm(48, 16)
            pe.wait_ge(ev("chosen"), 1)
            for name, mats in (("rank0", [(tri, 0)]), ("rank1", [(onesF, 0), (tri, 1)]),
                               ("count", [(onesF, 0), (onesF, 1)])):
                b = open_group(pe, name)
                for i, (m, t) in enumerate(mats):
                    ins = mm(b[:, 0:NE], m, chosen[:, NE * t:NE * t + NE], i == 0, i == len(mats) - 1)
                close_group(ins, name)
            n_groups = len(groups)
            for b in range(6):
                uses = (n_groups - 1 - b) // 6 + 1
                pe.wait_ge(bank_free[b], uses)

            def gather(n):
                pe.wait_ge(ev("sel_ready"), n + 1)
                for d in range(KD):
                    b = bank[2 + d // 4]
                    for t in range(RT):
                        ins = mm(b[:, P * (d % 4):P * (d % 4) + P], htok[:, t, P * d:P * d + P], sel[:, t, :],
                                 t == 0, t == 1)
                ins.then_inc(ev("gathered"), 1)

            def three(o, x_hi, x_lo, wh, wl, start, stop):
                mm(o, x_hi, wh, start, False)
                mm(o, x_hi, wl, False, False)
                return mm(o, x_lo, wh, False, stop)

            def up(j, fb, kind):
                b = bank[2 * (fb % 2) + (kind == "w3")]
                if kind == "w1" and fb >= 2:
                    pe.wait_ge(ev("g_ready"), 7 * j + fb - 1)
                for half in range(2):
                    c = 2 * order.index((fb, kind)) + half
                    pe.wait_ge(ev("split_lo"), NC * j + c + 1)
                    for i in range(4):
                        k, w = 4 * half + i, slice(512 * i, 512 * i + 512)
                        ins = three(b[:, :], h_hi[:, k, :], h_lo[:, k, :], w_hi[:, c % SPLITS, w],
                                    w_lo[:, c % SPLITS, w], k == 0, k == KD - 1)
                    ins.then_inc(mchunk_used, 1)

            def turn(j, fb):
                pe.wait_ge(ev("g_ready"), 7 * j + fb + 1)
                for i in range(4):
                    ins = nc.tensor.transpose(bank[4][:, P * i:P * i + P], g_e[:, fb % 2, P * i:P * i + P], ident)
                ins.then_inc(ev("turned"), 1)

            def down(j, fb):
                pe.wait_ge(ev("turn_split"), 7 * j + fb + 1)
                for half in range(2):
                    c = 2 * order.index((fb, "w2")) + half
                    pe.wait_ge(ev("split_lo"), NC * j + c + 1)
                    for i in range(2):
                        f = slice(P * (2 * half + i), P * (2 * half + i) + P)
                        for col in range(2):
                            w = slice(D * i + 512 * col, D * i + 512 * col + 512)
                            ins = three(bank[6 + col][:, :], gT_hi[:, fb % 2, f], gT_lo[:, fb % 2, f],
                                        w_hi[:, c % SPLITS, w], w_lo[:, c % SPLITS, w],
                                        fb == 0 and half == 0 and i == 0, fb == 6 and half == 1 and i == 1)
                    ins.then_inc(mchunk_used, 1)

            def scatter(n):
                pe.wait_ge(ev("scat_evac"), n + 1)
                pe.wait_ge(ev("y_evac"), 2 * n + 2)
                for i in range(4):
                    t, half = i // 2, i % 2
                    mm(bank[2 + i][:, :], scat[:, P * t:P * t + P], ysb[:, 512 * half:512 * half + 512],
                       True, True).then_inc(ev("scattered"), 1)

            gather(0)
            pe.wait_ge(ev("jobs_ready"), 1)
            n_jobs = pe.value_load(ints[0:1, 3:4], min_val=NE, max_val=MAX_JOBS)
            with pe.Fori(0, n_jobs) as j:
                pe.wait_ge(ev("gather_split"), j + 1)
                for fb in range(NFB):
                    if fb == 1:
                        pe.wait_ge(ev("added"), 4 * j + 4)
                    up(j, fb, "w1")
                    if fb == 0:
                        scatter(j)
                    if fb:
                        turn(j, fb - 1)
                    up(j, fb, "w3")
                    if fb == 3:
                        pe.wait_ge(ev("selg_ready"), j + 1)
                        for t in range(RT):
                            ins = nc.tensor.transpose(bank[5][:, P * t:P * t + P], selg[:, t, :], ident)
                        ins.then_inc(ev("scat_turned"), 1)
                    if fb:
                        down(j, fb - 1)
                turn(j, NFB - 1)
                gather(j + 1)
                down(j, NFB - 1)
            scatter(n_jobs)

        @block.sync
        def _(sp):
            sp.wait_ge(ev("x_sent"), 1)

            def param(dst, src):
                sp.dma_start(dst, src).then_inc(ev("params_loaded"), 16)

            param(rows_t[0:16, :], a["norm_mix_g"].rearrange("l (k p) -> (l k) p", p=P))
            param(rows_t[16:32, :], a["norm_ffn_g"].rearrange("l (k p) -> (l k) p", p=P))
            param(rows_t[32:34, :], a["diff_subln_g"][:, :])
            param(rows_t[34:38, :], a["ssm_d"].rearrange("l (m g) c -> (l m) (g c)", m=2))
            param(rows_t[38:54, :], a["ssm_lambda_re"].rearrange("l (i g) n -> (l i) (g n)", g=2))
            param(rows_t[54:70, :], a["ssm_lambda_im"].rearrange("l (i g) n -> (l i) (g n)", g=2))
            param(dt_rows[0:16, :], a["ssm_log_dt"].rearrange("l (i g) -> (l i) g", g=2))
            param(fb_t[0:FH, :], a["fox_forget_b"].rearrange("l h -> h l"))
            for i, n in enumerate(("q1", "k1", "q2", "k2")):
                sp.dma_start(lam_v[:, i, :, :], a[f"diff_lambda_{n}"].partition_broadcast(P)).then_inc(ev("lam_loaded"), 16)
            param(sm(320, 1), a["diff_lambda_q1"][0, 0:1].partition_broadcast(P))

            def stream(i):
                _, src, dst = chunks[i]
                sp.dma_start(dst, src).then_inc(slot_full[slot_of(i)], 16)

            for i in range(FIRST_PART):
                if i >= RING:
                    slot_free(sp, slot_of(i), i)
                stream(i)
                if i == 1:
                    load_ssm(sp, 0)
                if i == RING - 1:
                    sp.dma_start(router[:, :, :], a["moe_router"][0, :, :].rearrange("(k p) e -> p k e", p=P)
                                 ).then_inc(ev("router_loaded"), 16)
            for c in range(NDC):
                if c < DRAW:
                    slot_free(sp, c // 2, FIRST_PART)
                else:
                    sp.wait_ge(ev("dense_split_lo"), c - DRAW + 1)
                sp.dma_start(dslot(c).rearrange("p (k n) -> p k n", k=dense_chunk(c)[0].shape[1]), dense_chunk(c)[0]
                             ).then_inc(dslot_full[c % DRAW], 16)
            for i in range(FIRST_PART, len(chunks)):
                if i >= FIRST_PART + RING:
                    slot_free(sp, slot_of(i), i)
                elif slot_of(i) < DRAW // 2:
                    sp.wait_ge(ev("dense_split_lo"), NDC)
                else:
                    dense_used(sp, NDC - 1)
                stream(i)

            def load(e, c):
                src, dst = expert_chunk(e, c)
                sp.dma_start(dst, src).then_inc(mslot_full[c % MRING], 16)

            for c in range(MRING):
                slot_free(sp, c // 2, len(chunks))
                load(0, c)
            with sp.Fori(0, NE - 1) as e:
                for c in range(NC):
                    ee = e if c + MRING < NC else e + 1
                    sp.wait_ge(ev("split_lo"), NC * e + c + 1)
                    if (c + MRING) % NC == FIRST_DOWN:
                        sp.sem_inc(ev("down_claimed"), 1)
                    load(ee, (c + MRING) % NC)
            for c in range(MRING, NC):
                sp.wait_ge(ev("split_lo"), NC * (NE - 1) + c - MRING + 1)
                load(NE - 1, c)
            sp.wait_ge(ev("jobs_ready"), 1)
            n_jobs = sp.value_load(ints[0:1, 3:4], min_val=NE, max_val=MAX_JOBS)
            with sp.If(n_jobs > NE):
                with sp.Fori(NE, n_jobs) as j:
                    e = sp.value_load(ints[0:1, bass.ds(j - NE, 1)], min_val=0, max_val=NE - 1)
                    for c in range(NC):
                        sp.wait_ge(ev("split_lo"), NC * j + c - MRING + 1)
                        if c in (0, 2, FIRST_DOWN):
                            sp.sem_inc(ev("down_claimed"), 1)
                        load(e, c)
            sp.wait_ge(ev("out_ready"), 2)
            for t in range(RT):
                sp.dma_start(out[0, P * t:P * t + P, :], racc[:, t, :]).then_inc(ev("out_stored"), 16)
            sp.wait_ge(ev("out_stored"), 16 * RT)

        @block.gpsimd
        def _(pool):
            g = nc.gpsimd
            step = Chain(pool, ev("pool_steps"))
            step(g.memset(ident, 0.0))
            g.affine_select(out=ident, in_=ident, compare_op=ALU.not_equal, fill=1.0, base=0,
                            pattern=[[-1, P]], channel_multiplier=1).then_inc(ev("identity_ready"), 2)
            pool.wait_ge(ev("identity_ready"), 2)
            step(g.memset(avgD, 1.0 / D))
            step(g.memset(eps_col, EPS))
            step(g.memset(onesF, 1.0))
            g.iota(ints[:, 8:9], [[0, 1]], base=0, channel_multiplier=1).then_inc(ev("constants_ready"), 1)
            pool.wait_ge(ev("constants_ready"), 1)
            step(g.memset(mask_t[:, :], 0.0))
            step(g.memset(tri, 1.0))
            step(g.affine_select(out=mask[:, 0:2, :], in_=mask[:, 0:2, :], compare_op=ALU.is_ge, fill=NEG, base=0,
                                  pattern=[[P, 2], [-1, L]], channel_multiplier=1))
            for h in range(4):
                rows = mask[TAIL * h:TAIL * (h + 1), 2, :]
                step(g.affine_select(out=rows, in_=rows, compare_op=ALU.is_ge, fill=NEG, base=L - TAIL,
                                      pattern=[[-1, L]], channel_multiplier=1))
            step(g.affine_select(out=tri, in_=tri, compare_op=ALU.is_ge, fill=0.0, base=-1,
                                  pattern=[[1, P]], channel_multiplier=-1))
            step(g.memset(avgV, 1.0 / DV))
            step(g.memset(ones_row, 1.0))
            step(g.memset(b_exp_t[:, :], 0.0))
            step(g.iota(slot_iota, [[1, P]], base=0, channel_multiplier=0, allow_small_or_imprecise_dtypes=True))
            step(g.iota(time_iota, [[1, L]], base=0, channel_multiplier=0, allow_small_or_imprecise_dtypes=True))
            step(g.iota(expert_iota, [[1, NE]], base=0, channel_multiplier=0, allow_small_or_imprecise_dtypes=True))
            pool.sem_inc(ev("constants_ready"), 1)
            step(g.memset(region["foxqk"][64:P, :], 0.0))
            step(g.memset(fka[64:68, :, :], 1.0))
            step(g.memset(fqa[96:100, :, :], 1.0 / SCALE))
            for i, v in enumerate((fka[64:68, :, :], fqa[96:100, :, :])):
                g.affine_select(out=v, in_=v, compare_op=ALU.is_equal, fill=0.0, base=0,
                                pattern=[[-1, FH], [0, L]], channel_multiplier=1).then_inc(ev("fox_select"), 1)
                pool.wait_ge(ev("fox_select"), i + 1)
            def unit_probs(l, u):
                kmax, at = sum(TT[UNITS[u][2]]), 321 + 4 * (u % 3) + 2
                pool.wait_ge(ev(f"row_scales{l}"), u + 1)
                if u >= 2:
                    take(pool, f"at{l}_{u - 2}")
                o, e = a_buf[:, u % 2, 0:kmax], e_buf[u % 3][:, :, 0:kmax]
                g.tensor_scalar(o, e[:, 0, :], small[:, at:at + 1], None, ALU.mult)
                step(g.tensor_scalar(e[:, 1, :], e[:, 1, :], small[:, at + 1:at + 2], None, ALU.mult))
                g.tensor_tensor(o, o, e[:, 1, :], ALU.add).then_inc(ev(f"probs_d{l}"), 1)

            for l in range(DEPTH):
                pool.wait_ge(ev(f"angles{l}"), 1)
                for i in range(POOL_PHASES, NST):
                    phase_tile(g, step, i, o_buf[:, 0, :] if l else t_pool)
                    if i % 2:
                        pool.sem_inc(ev(f"pool_phases{l}"), 1)
                for i in [i for i in range(NST) if i not in VECTOR_TURNS]:
                    pool.wait_ge(ev(f"w_ready{l}"), i + 1)
                    if i >= 2:
                        pool.wait_ge(ev(f"y_done{l}"), i - 1)
                    co, si = cosT[:, i, :], sinT[:, i, :]
                    w0, w1 = w_scan[:, i % 2, 0, :], w_scan[:, i % 2, 1, :]
                    x0, x1 = x_ssm[:, i % 2, 0, :], x_ssm[:, i % 2, 1, :]
                    g.tensor_tensor(x0, w0, co, ALU.mult)
                    g.tensor_tensor(t_pool, w1, si, ALU.mult)
                    g.tensor_tensor(x1, w0, si, ALU.mult)
                    step(g.tensor_tensor(t_pool2, w1, co, ALU.mult))
                    g.tensor_tensor(x0, x0, t_pool, ALU.subtract)
                    g.tensor_tensor(x1, x1, t_pool2, ALU.add).then_inc(ev(f"x_pool{l}"), 1)
                    turned_states(pool, l, i)
                for u in range(KIND_UNITS):
                    unit_probs(l, u)
            pool.wait_ge(ev("jobs_ready"), 1)
            n_jobs = pool.value_load(ints[0:1, 3:4], min_val=NE, max_val=MAX_JOBS)
            for c in range(SPLITS):
                pool.wait_ge(mslot_full[c], 16 * (NC // MRING) * n_jobs)
                pool.sem_inc(mslot_full[c], 16)

        @block.scalar
        def _(act):
            chain = Chain(act, ev("act_steps"))
            x, meta = a["x"], a["meta_tokens"]
            act.dma_start(xtok[0:N_META, 0, :], meta[:, :]).then_inc(ev("x_loaded"), 16)
            act.dma_start(xtok[N_META:P, 0, :], x[0, 0:P - N_META, :]).then_inc(ev("x_loaded"), 16)
            act.dma_start(xtok[:, 1, :], x[0, P - N_META:2 * P - N_META, :]).then_inc(ev("x_loaded"), 16)
            act.dma_start(xtok[0:N_META, 2, :], x[0, SEQ - N_META:SEQ, :]).then_inc(ev("x_loaded"), 16)
            act.sem_inc(ev("x_sent"), 1)

            def squares(n, count):
                act.wait_ge(ev(f"res{n}"), count)
                nc.scalar.activation(sqT[:, 0:4, :], resT[:, 0:4, :], ACT.Square).then_inc(ev(f"squares_act{n}"), 1)
                act.wait_ge(ev(f"res{n}"), max(6, count))
                nc.scalar.activation(sqT[:, 4:6, :], resT[:, 4:6, :], ACT.Square).then_inc(ev(f"squares_act{n}"), 1)

            def copy(dst, src):
                return nc.scalar.activation(dst, src, ACT.Copy)

            def rstd_first(x, event):
                chain(nc.scalar.activation(rs0_t[:, :], x, ACT.Ln, bias=eps_col))
                nc.scalar.activation(rs0_t[:, :], rs0_t[:, :], ACT.Exp, scale=-0.5).then_inc(ev(event), 1)

            def norm_rstd(n):
                rstd_first(take(act, f"ssq{n}")[:, 0:L], f"rstd_first{n}")

            def head_rstd(l, u):
                h = UNITS[u][1]
                b = take(act, f"hn{l}_{h}")
                if h:
                    act.wait_ge(ev(f"diff_out{l}"), h)
                rstd_first(b[:, 0:L], f"head_rstd_first{l}")

            def token_rstd(squares, event):
                act.wait_ge(ev(squares), RT)
                chain(nc.scalar.activation(sm(114, 2), sm(100, 2), ACT.Ln, bias=eps_col, scale=1.0 / D))
                nc.scalar.activation(sm(114, 2), sm(114, 2), ACT.Exp, scale=-0.5).then_inc(ev(event), 1)

            def params_turned():
                b = take(act, "prm")
                release(copy(prm[:, 0:70], b[:, 0:70]), "prm")
                b = take(act, "ldt")
                release(copy(prm[:, 70:86], b[:, 0:16]), "ldt")

            def ssm_sines(l):
                act.wait_ge(ev(f"angles{l}"), 1)
                nc.scalar.activation(sm(0), sm(8), ACT.Sin, scale=SIN_2PI)
                nc.scalar.activation(sm(16), sm(8), ACT.Sin, scale=SIN_2PI / 2).then_inc(ev(f"sines{l}"), 1)

            def ssm_tables(l, tiles):
                for i in tiles:
                    if i < POOL_PHASES:
                        act.wait_ge(ev(f"phases{l}"), i // 2 + 1)
                    else:
                        act.wait_ge(ev(f"pool_phases{l}"), (i - POOL_PHASES) // 2 + 1)
                    nc.scalar.activation(sinT[:, i:i + 2, :], sinT[:, i:i + 2, :], ACT.Sin, scale=SIN_2PI)
                    nc.scalar.activation(cosT[:, i:i + 2, :], cosT[:, i:i + 2, :], ACT.Sin, scale=SIN_2PI
                                         ).then_inc(ev(f"tables{l}"), 1)

            def ssm_weights(l):
                b = take(act, f"bT{l}")
                release(copy(bT_t[:, :], b[:, :]), f"bT{l}")
                b = take(act, f"cT{l}")
                bv, cv = (v.rearrange("p (m c n) -> p m c n", m=2, c=2) for v in (b[:, :], cT_t[:, :]))
                nc.scalar.activation(cv[:, :, 0, :], bv[:, :, 0, :], ACT.Copy)
                release(nc.scalar.activation(cv[:, :, 1, :], bv[:, :, 1, :], ACT.Copy, scale=-1.0), f"cT{l}")

            def mixer_evac(l):
                def tokens(key, cols, t):
                    b = take(act, f"z{l}{key}{t}")
                    qn, at = TT[t][1], 512 if key == "fv" else 0
                    release(copy(vtok[0:qn, t, at:at + cols], b[0:qn, 0:cols]), f"z{l}{key}{t}")

                def feature(key, dst, h):
                    b = take(act, f"z{l}{key}{h}")
                    release(copy(dst[:, h, :], b[:, 0:L]), f"z{l}{key}{h}")
                    if key == "dq" and h == DH - 1:
                        act.wait_ge(ev(f"fg_abs{l}"), 1)
                        chain(nc.scalar.activation(fgm[0:FH, :], fgm[0:FH, :], ACT.Exp))
                        nc.scalar.activation(fgm[0:FH, :], fgm[0:FH, :], ACT.Ln, bias=onesF[0:FH, 0:1]
                                             ).then_inc(ev(f"fg_ln{l}"), 1)

                def forget():
                    b = take(act, f"z{l}fg")
                    release(nc.scalar.activation(fgz[0:FH, :], b[0:FH, 0:L], ACT.Identity, bias=fb_t[0:FH, l:l + 1]),
                            f"z{l}fg")

                def fox(i):
                    act.wait_ge(ev("fox_select"), 2)
                    b = take(act, f"z{l}fqk{i}")
                    dst, h = (fqa, fka)[i // 2], 2 * (i % 2)
                    copy(dst[0:64, h, :], b[0:64, 0:L])
                    release(copy(dst[0:64, h + 1, :], b[64:P, 0:L]), f"z{l}fqk{i}")

                steps = [lambda t=t: tokens("fv", 256, t) for t in range(3)] + [forget]
                steps += [lambda h=h, k=k, d=d: feature(k, d, h) for k, d in (("dq", dqT), ("dk", dkT)) for h in range(DH)]
                steps += [lambda t=t: tokens("dv", 512, t) for t in range(3)] + [lambda i=i: fox(i) for i in range(4)]
                for m in range(2):
                    b = take(act, f"z{l}u{m}")
                    release(copy(uT[:, m, :], b[:, 0:L]), f"z{l}u{m}")
                for j in range(EARLY[l]):
                    steps[j]()
                    if SSM_AT[l].get(j) == 0:
                        ssm_weights(l)
                    if l == 0 and j == 2:
                        ssm_sines(0)
                    if l == 0 and j == 4:
                        ssm_tables(0, (0, 2))
                    if l == 0 and j == 5:
                        ssm_tables(0, (4, 6))
                        nc.scalar.preload_act_table_set("natural_log_exp_and_others")
                return steps[EARLY[l]:]

            def gelu(l):
                act.wait_ge(ev(f"gelu_arg{l}"), 1)
                nc.scalar.activation(ye, yq, ACT.Exp, scale=-2.0 * math.sqrt(2.0 / math.pi)).then_inc(ev(f"gelu_exp{l}"), 1)

            def glu(l):
                for m in range(2):
                    b = take(act, f"glu{l}{m}")
                    release(copy(mixedT[:, m, :], b[:, 0:L]), f"glu{l}{m}")
                for m in range(2):
                    b = take(act, f"glu{l}{2 + m}")
                    release(nc.scalar.activation(glu_e[:, m, :], b[:, 0:L], ACT.Exp, scale=-1.0), f"glu{l}{2 + m}")

            def exps(l, u):
                kind, h, t = UNITS[u]
                kmax = sum(TT[t])
                if u >= 3:
                    probs_ready(act, l, u - 3)
                act.wait_ge(ev(f"scores{l}"), u + 1)
                for m in range(2 if kind == "d" else 1):
                    at = 321 + 4 * (u % 3) + m
                    nc.scalar.activation(e_buf[u % 3][:, m, 0:kmax], s_buf[u % 3][:, m, 0:kmax], ACT.Exp,
                                         bias=small[:, at:at + 1], accum_out=small[:, at + 2:at + 3]
                                         ).then_inc(ev(f"exps{l}{kind}"), 1)

            def probs_evac(l, u):
                kind, h, t = UNITS[u]
                name = f"at{l}_{u}"
                b = take(act, name)
                tiles = b[:, 0:3 * P].rearrange("p (k q) -> p k q", q=P)
                if h is None:
                    dst = aT_tail[:, "df".index(kind), :, :].rearrange("p k (h q) -> p k h q", q=16)
                    src = b[:, 0:3 * P].rearrange("p (k h q) -> p k h q", h=4, q=TAIL)[:, :, :, TAIL - 16:TAIL]
                    for kt, (_, kn) in enumerate(TT):
                        ins = copy(dst[0:kn, kt, :, :], src[0:kn, kt, :, :])
                else:
                    ins = copy(aT[:, h % 2, 0:t + 1, P * t:P * t + P], tiles[:, 0:t + 1, :])
                release(ins, name)

            def head_out(l, u):
                kind, h, _ = UNITS[u]
                name = f"o{l}_{u}"
                b = take(act, name)
                if kind == "f":
                    release(copy(mixedT[64 * (h % 2):64 * (h % 2) + 64, 6 + h // 2, :], b[0:64, 0:L]), name)
                    return
                if h >= 2:
                    act.wait_ge(ev(f"diff_out{l}"), h - 1)
                release(copy(o_buf[:, h % 2, :], b[:, 0:L]), name)
                evacuated(act, name)
                nc.scalar.activation(sq_o[:, h % 2, :], o_buf[:, h % 2, :], ACT.Square).then_inc(ev(f"o_square{l}"), 1)

            def attention(l, evacuations):
                exps(l, 0)
                exps(l, 1)
                gelu(l)
                for u in range(len(UNITS) + 2):
                    if u >= 3 and heads_last(u - 3) and UNITS[u - 3][0] == "d":
                        head_rstd(l, u - 3)
                    if u + 2 < len(UNITS):
                        exps(l, u + 2)
                    if u < len(evacuations):
                        evacuations[u]()
                    if 1 <= u <= len(UNITS) and heads_last(u - 1):
                        head_out(l, u - 1)
                    if u < len(UNITS):
                        probs_evac(l, u)
                    if u == GLU_AT:
                        glu(l)

            def dense_split_hi(c):
                n = dense_chunk(c)[1]
                act.wait_ge(dslot_full[c % DRAW], 16 * (c // DRAW + 1))
                if c >= SPLITS:
                    dense_used(act, c - SPLITS)
                copy(dw_hi[:, dsplit(c), 0:n], dslot(c)).then_inc(ev("dense_split_hi"), 1)

            def dense():
                for c in range(NDC):
                    kind, f0, n, _ = dense_order[c]
                    if kind == "w1":
                        for f in range(f0, f0 + n):
                            b = take(act, f"fa{f}")
                            if f >= 2:
                                evacuated(act, f"fb{f - 2}")
                            release(nc.scalar.activation(silu_t[:, f % 2, :], b[:, 0:L], ACT.Silu), f"fa{f}")
                    if c + SPLITS < NDC:
                        dense_split_hi(c + SPLITS)
                    if c == NDC - 6:
                        ssm_sines(1)
                        ssm_tables(1, (0,))
                    if c == NDC - 5:
                        ssm_tables(1, (2,))
                    if c == NDC - 4:
                        ssm_tables(1, (4, 6))
                    if kind == "w3":
                        for f in range(f0, f0 + n):
                            act.wait_ge(ev("dense_g"), f + 1)
                            copy(dg_hi[:, f - (f0 >= DPARTS[1][0]) * DPARTS[1][0], :], g_raw[:, f % 2, :]
                                 ).then_inc(ev("dense_g_hi"), 1)

            nc.scalar.preload_act_table_set("natural_log_exp_and_others")
            squares(0, 4)
            norm_rstd(0)
            act.wait_ge(ev("lam_dots"), 4)
            nc.scalar.activation(sm(32, 4), sm(36, 4), ACT.Exp).then_inc(ev("lam_exp"), 1)
            params_turned()
            for l in range(DEPTH):
                attention(l, mixer_evac(l))
                if l == 0:
                    load_ssm(act, 1)
                    dense_split_hi(0)
                    dense_split_hi(1)
                    squares(1, 8)
                    norm_rstd(1)
                    for k in range(KD):
                        act.wait_ge(ev("h1"), k + 1)
                        copy(dh_hi[:, k, :], hT[:, k, :]).then_inc(ev("dense_h_hi"), 1)
                    act.wait_ge(chunk_used, FIRST_PART)
                    dense_split_hi(2)
                    dense()
                    nc.scalar.preload_act_table_set("natural_log_exp_and_others")
                    squares(2, 4)
                    norm_rstd(2)

            probs_ready(act, 1, len(UNITS) - 1)
            act.wait_ge(ev("ssm_out1"), 2)
            act.dma_start(g_ffn_b, a["norm_ffn_g"][1, :].partition_broadcast(P)).then_inc(ev("row_gains"), 16)
            act.dma_start(g_fin_b, a["final_norm_g"].partition_broadcast(P)).then_inc(ev("row_gains"), 16)
            for half in range(2):
                for t in range(RT):
                    b = take(act, f"rt{t}{half}")
                    release(copy(racc[:, t, 512 * half:512 * half + 512], b[:, :]), f"rt{t}{half}")
            evacuated(act, "rt01")
            evacuated(act, "rt11")
            for t in range(RT):
                nc.scalar.activation(htok[:, t, :], racc[:, t, :], ACT.Square, accum_out=sm(100 + t, 1)
                                     ).then_inc(ev("token_squares"), 1)
            token_rstd("token_squares", "token_rstd_first")
            def split_hi(j, m):
                act.wait_ge(mslot_full[m % MRING], 16 * ((NC // MRING) * j + m // MRING + 1))
                copy(w_hi[:, m % SPLITS, :], mslot(m)).then_inc(ev("split_hi"), 1)

            act.wait_ge(chunk_used, len(chunks))
            split_hi(0, 0)
            split_hi(0, 1)
            for j in range(4):
                b = take(act, f"mh{j}")
                release(copy(mhT[:, 2 * j:2 * j + 2, :], b[:, :].rearrange("p (k t) -> p k t", k=2)), f"mh{j}")
            split_hi(0, 2)
            act.wait_ge(ev("margin"), 1)
            nc.scalar.activation(sm(104, 2), sm(106, 2), ACT.Exp).then_inc(ev("margin_exp"), 1)

            def gather_hi():
                for b in range(2):
                    copy(h_hi[:, 4 * b:4 * b + 4, :], bank[2 + b][:, :].rearrange("p (k s) -> p k s", k=4)
                         ).then_inc(ev("gather_hi"), 1)

            def turn_hi(j, fb):
                act.wait_ge(ev("turned"), 7 * j + fb + 1)
                copy(gT_hi[:, fb % 2, :], bank[4][:, :]).then_inc(ev("turn_hi"), 1)

            act.wait_ge(ev("gathered"), 1)
            gather_hi()
            act.wait_ge(ev("jobs_ready"), 1)
            n_jobs = act.value_load(ints[0:1, 3:4], min_val=NE, max_val=MAX_JOBS)
            with act.Fori(0, n_jobs) as j:
                nc.scalar.preload_act_table_set("silu_and_others")
                for c in range(NC):
                    act.wait_ge(mchunk_used, NC * j + c + 1)
                    if c == GATHER_AFTER:
                        turn_hi(j, NFB - 1)
                    if c == NC - 1:
                        copy(ysb[:, 0:512], bank[6][:, :]).then_inc(ev("y_evac"), 1)
                    if c in silu_after:
                        fb = silu_after[c]
                        nc.scalar.activation(e1[:, fb % 2, :], bank[2 * (fb % 2)][:, :], ACT.Silu
                                             ).then_inc(ev("silu_done"), 1)
                    split_hi(j, c + SPLITS)
                    if c in turn_after:
                        turn_hi(j, turn_after[c])
                    if c == SCATTER_AFTER:
                        act.wait_ge(ev("scat_turned"), j + 1)
                        copy(scat, bank[5][:, 0:SEQ]).then_inc(ev("scat_evac"), 1)
                    if c == GATHER_AFTER:
                        act.wait_ge(ev("gathered"), j + 2)
                        gather_hi()

            nc.scalar.preload_act_table_set("natural_log_exp_and_others")
            for t in range(RT):
                act.wait_ge(ev("final_ready"), t + 1)
                nc.scalar.activation(htok[:, t, :], racc[:, t, :], ACT.Square, accum_out=sm(100 + t, 1)
                                     ).then_inc(ev("final_squares"), 1)
            token_rstd("final_squares", "final_rstd_first")

        @block.vector
        def _(dve):
            v = nc.vector
            step = Chain(dve, ev("dve_steps"))

            for k in range(KD):
                b = take(dve, f"xT{k}")
                release(v.tensor_copy(resT[:, k, :], b[:, 0:L]), f"xT{k}")
                evacuated(dve, f"xT{k}")
                dve.sem_inc(ev("res0"), 1)

            def squares(n):
                v.tensor_tensor(sqT[:, 6:8, :], resT[:, 6:8, :], resT[:, 6:8, :], ALU.mult).then_inc(ev(f"squares_dve{n}"), 1)

            def rsqrt(x, name):
                step(v.tensor_tensor(rs_t[:, :], rs0_t[:, :], rs0_t[:, :], ALU.mult))
                release(v.scalar_tensor_tensor(rs_t[:, :], x, EPS, rs_t[:, :], ALU.add, ALU.mult), name)
                evacuated(dve, name)
                step(v.tensor_scalar(rs_t[:, :], rs_t[:, :], -0.5, 1.5, ALU.mult, ALU.add))
                step(v.tensor_tensor(rs_t[:, :], rs_t[:, :], rs0_t[:, :], ALU.mult))

            def normalise(n, after_tile=None):
                l, kind = n // 2, n % 2
                b = take(dve, f"ssq{n}")
                dve.wait_ge(ev(f"rstd_first{n}"), 1)
                rsqrt(b[:, 0:L], f"ssq{n}")
                for k in range(KD):
                    col = 16 * kind + 8 * l + k
                    v.scalar_tensor_tensor(hT[:, k, :], resT[:, k, :], prm[:, col:col + 1], rs_t[:, :],
                                           ALU.mult, ALU.mult).then_inc(ev(f"h{n}"), 1)
                    if after_tile:
                        after_tile(k)

            x, k, f, q, dt = (sm(120 + 8 * i) for i in range(5))
            e, r, th, cm, ni, den, cr, ci, nr = (sm(176 + 8 * i) for i in range(9))
            t1, t2, mag = sm(248), sm(256), sm(264)

            def eigenvalues(l):
                return prm[:, 38 + 8 * l:46 + 8 * l], prm[:, 54 + 8 * l:62 + 8 * l]

            def discretise(l):
                lr, li = eigenvalues(l)
                step(v.tensor_scalar(x, prm[:, 70 + 8 * l:78 + 8 * l], -87.0, 88.0, ALU.max, ALU.min))
                step(v.tensor_scalar(k, x, 1.0 / math.log(2.0), MAGIC, ALU.mult, ALU.add))
                step(v.tensor_scalar(k, k, -MAGIC, None, ALU.add))
                step(v.scalar_tensor_tensor(f, k, -LN2_HI, x, ALU.mult, ALU.add))
                step(v.scalar_tensor_tensor(f, k, -LN2_LO, f, ALU.mult, ALU.add))
                step(v.tensor_scalar(q, f, 1.0 / math.factorial(7), None, ALU.mult))
                for n in range(6, 0, -1):
                    step(v.scalar_tensor_tensor(q, q, 1.0 / math.factorial(n), f, ALU.add, ALU.mult))
                step(v.tensor_scalar(k, k, 127.0, 8388608.0, ALU.add, ALU.mult))
                step(v.tensor_copy(ints[:, 0:8], k))
                step(v.scalar_tensor_tensor(dt, q, 1.0, ints[:, 0:8].bitcast(F32), ALU.add, ALU.mult))
                step(v.tensor_tensor(r, lr, dt, ALU.mult))
                step(v.tensor_scalar(r, r, -60.0, 60.0, ALU.max, ALU.min))
                step(v.tensor_scalar(r, r, 1.0 / 256, None, ALU.mult))
                step(v.tensor_scalar(e, r, 1.0 / 120, None, ALU.mult))
                for n in (4, 3, 2, 1):
                    step(v.scalar_tensor_tensor(e, e, 1.0 / math.factorial(n), r, ALU.add, ALU.mult))
                for _ in range(8):
                    step(v.scalar_tensor_tensor(e, e, 2.0, e, ALU.add, ALU.mult))
                step(v.tensor_scalar(mag, e, 1.0, None, ALU.add))
                step(v.tensor_tensor(th, li, dt, ALU.mult))
                step(v.tensor_scalar(th, th, 1.0 / (2.0 * math.pi), None, ALU.mult))
                step(v.tensor_scalar(t1, th, MAGIC, -MAGIC, ALU.add, ALU.add))
                step(v.tensor_tensor(sm(8), th, t1, ALU.subtract))
                dve.sem_inc(ev(f"angles{l}"), 1)

            def dve_phases(l, lo, hi):
                for i in range(lo, hi):
                    phase_tile(v, step, i, rs_t[:, :] if l else t_dve)
                dve.sem_inc(ev(f"phases{l}"), 1)

            def coefficients(l):
                lr, li = eigenvalues(l)
                dve.wait_ge(ev(f"sines{l}"), 1)
                step(v.scalar_tensor_tensor(cm, sm(16), -2.0, sm(16), ALU.mult, ALU.mult))
                step(v.tensor_scalar(t1, cm, 1.0, None, ALU.add))
                step(v.tensor_tensor(t1, e, t1, ALU.mult))
                step(v.tensor_tensor(nr, t1, cm, ALU.add))
                step(v.tensor_tensor(ni, mag, sm(0), ALU.mult))
                step(v.tensor_tensor(t1, lr, lr, ALU.mult))
                step(v.tensor_tensor(t2, li, li, ALU.mult))
                step(v.tensor_tensor(den, t1, t2, ALU.add))
                step(v.reciprocal(den, den))
                for o, p0, p1, op in ((cr, nr, ni, ALU.add), (ci, ni, nr, ALU.subtract)):
                    step(v.tensor_tensor(t1, p0, lr, ALU.mult))
                    step(v.tensor_tensor(t2, p1, li, ALU.mult))
                    step(v.tensor_tensor(t1, t1, t2, op))
                    step(v.tensor_tensor(o, t1, den, ALU.mult))
                dve.wait_ge(ev("ssm_loaded"), 64 * (l + 1))
                br, bi = b_raw[:, 0, :, :], b_raw[:, 1, :, :]
                crb, cib = (w.unsqueeze(2).to_broadcast([P, NST, 16]) for w in (cr, ci))
                ta, tb = cut(rs_t, 0, NST, 16), cut(rs_t, P, NST, 16)
                for c, (p0, p1, op) in enumerate(((br, bi, ALU.subtract), (bi, br, ALU.add))):
                    step(v.tensor_tensor(ta, p0, crb, ALU.mult))
                    step(v.tensor_tensor(tb, p1, cib, ALU.mult))
                    for g in range(2):
                        hs = slice(64 * g, 64 * g + 64)
                        step(v.tensor_tensor(b_exp[hs, c, :, 16 * g:16 * g + 16], ta[hs], tb[hs], op))
                dve.sem_inc(ev(f"b_blocks{l}"), 1)
                cflat = c_raw_t[:, :].rearrange("p (i n) -> p i n", n=STATE)
                for g in range(2):
                    step(v.tensor_scalar(c_exp[:, :, 64 * g:64 * g + 64], cflat, sm(40 + g, 1), None, ALU.mult))
                dve.sem_inc(ev(f"c_blocks{l}"), 1)

            def ssm_scan(l, i):
                co, si = cosT[:, i, :], sinT[:, i, :]
                bre = take(dve, f"bu{l}{i}0")[:, 0:L]
                bim = take(dve, f"bu{l}{i}1")[:, 0:L]
                if i % 2 == 0:
                    dve.wait_ge(ev(f"tables{l}"), i // 2 + 1)
                if i >= 2:
                    turned_states(dve, l, i - 2)
                w0, w1 = w_scan[:, i % 2, 0, :], w_scan[:, i % 2, 1, :]
                v.tensor_tensor(w0, bre, co, ALU.mult)
                release(v.tensor_tensor(t_dve2, bre, si, ALU.mult), f"bu{l}{i}0")
                v.tensor_tensor(t_dve, bim, si, ALU.mult)
                release(v.tensor_tensor(w1, bim, co, ALU.mult), f"bu{l}{i}1")
                evacuated(dve, f"bu{l}{i}0")
                evacuated(dve, f"bu{l}{i}1")
                v.tensor_tensor(w0, w0, t_dve, ALU.add)
                step(v.tensor_tensor(w1, w1, t_dve2, ALU.subtract))
                m = sm(264)[:, i:i + 1].to_broadcast([P, L])
                step(v.tensor_tensor_scan(w0, m, w0, 0.0, ALU.mult, ALU.add))
                v.tensor_tensor_scan(w1, m, w1, 0.0, ALU.mult, ALU.add).then_inc(ev(f"w_ready{l}"), 1)
                dve.wait_ge(ev(f"w_ready{l}"), i + 1)
                if i in VECTOR_TURNS:
                    if i >= 2:
                        dve.wait_ge(ev(f"y_done{l}"), i - 1)
                    x0, x1 = x_ssm[:, i % 2, 0, :], x_ssm[:, i % 2, 1, :]
                    v.tensor_tensor(x0, w0, co, ALU.mult)
                    v.tensor_tensor(t_dve, w1, si, ALU.mult)
                    v.tensor_tensor(x1, w0, si, ALU.mult)
                    step(v.tensor_tensor(t_dve2, w1, co, ALU.mult))
                    v.tensor_tensor(x0, x0, t_dve, ALU.subtract)
                    v.tensor_tensor(x1, x1, t_dve2, ALU.add).then_inc(ev(f"x_vector{l}"), 1)
                    turned_states(dve, l, i)

            def forget_gate(l):
                evacuated(dve, f"z{l}fg")
                v.scalar_tensor_tensor(fgm[0:FH, :], fgz[0:FH, :], -1.0, fgz[0:FH, :], ALU.mult, ALU.min).then_inc(ev(f"fg_abs{l}"), 1)

            def decay(l):
                dve.wait_ge(ev(f"fg_ln{l}"), 1)
                step(v.scalar_tensor_tensor(fgz[0:FH, :], fgz[0:FH, :], 0.0, fgm[0:FH, :], ALU.min, ALU.subtract))
                step(v.tensor_tensor_scan(fgc[0:FH, :], ones_row[0:FH, :], fgz[0:FH, :], 0.0, ALU.mult, ALU.add))
                dve.wait_ge(ev("fox_select"), 2)
                c = fgc[0:FH, :].unsqueeze(1).to_broadcast([FH, FH, L])
                v.tensor_scalar(fqa[64:68, :, :], c, 1.0 / SCALE, None, ALU.mult).then_inc(ev(f"decay_rows{l}"), 1)
                v.tensor_scalar(fka[96:100, :, :], c, -1.0, None, ALU.mult).then_inc(ev(f"decay_rows{l}"), 1)
                dve.wait_ge(ev(f"decay_rows{l}"), 2)

            def gelu(l):
                dve.wait_ge(ev(f"y_done{l}"), NST)
                for m in range(2):
                    col = 34 + 2 * l + m
                    step(v.scalar_tensor_tensor(ys[:, m, :], uT[:, m, :], prm[:, col:col + 1], bank[6 + m][:, 0:L],
                                                ALU.mult, ALU.add))
                step(v.tensor_tensor(yq, ys, ys, ALU.mult))
                step(v.tensor_scalar(yq, yq, 0.044715, 1.0, ALU.mult, ALU.add))
                v.tensor_tensor(yq, yq, ys, ALU.mult).then_inc(ev(f"gelu_arg{l}"), 1)

            def gelu_end(l):
                dve.wait_ge(ev(f"gelu_exp{l}"), 1)
                step(v.tensor_scalar(ye, ye, 1.0, None, ALU.add))
                step(v.reciprocal(ye, ye))
                v.tensor_tensor(gy, ys, ye, ALU.mult).then_inc(ev(f"gelu_ready{l}"), 1)

            def glu(l, m):
                evacuated(dve, f"glu{l}{2 + m}")
                step(v.tensor_scalar(glu_e[:, m, :], glu_e[:, m, :], 1.0, None, ALU.add))
                step(v.reciprocal(glu_e[:, m, :], glu_e[:, m, :]))
                evacuated(dve, f"glu{l}{m}")
                v.tensor_tensor(mixedT[:, m, :], mixedT[:, m, :], glu_e[:, m, :], ALU.mult).then_inc(ev(f"ssm_out{l}"), 1)

            def unit_scores(l, u):
                kind, h, t = UNITS[u]
                kmax = sum(TT[t])
                maps = 2 if kind == "d" else 1
                for m in range(maps):
                    name = f"s{l}_{u}_{m}"
                    b = take(dve, name)
                    release(v.scalar_tensor_tensor(s_buf[u % 3][:, m, 0:kmax], b[:, 0:kmax], SCALE,
                                                   mask[:, t, 0:kmax], ALU.mult, ALU.add), name)
                    evacuated(dve, name)
                at = 321 + 4 * (u % 3)
                v.tensor_reduce(small[:, at:at + maps], s_buf[u % 3][:, 0:maps, 0:kmax], AX.X, ALU.max,
                                negate=True).then_inc(ev(f"scores{l}"), 1)

            def unit_probs(l, u):
                kind, h, t = UNITS[u]
                kmax = sum(TT[t])
                maps = 2 if kind == "d" else 1
                done = 2 * (u + 1) if kind == "d" else u + 1 - KIND_UNITS
                dve.wait_ge(ev(f"exps{l}{kind}"), done)
                at = 321 + 4 * (u % 3) + 2
                su = small[:, at:at + 2]
                if kind == "d":
                    step(v.reciprocal(su, su))
                    v.tensor_scalar(su[:, 1:2], su[:, 1:2], sm(44 + l, 1), None, ALU.mult).then_inc(ev(f"row_scales{l}"), 1)
                    return
                step(v.reciprocal(su[:, 0:1], su[:, 0:1]))
                take(dve, f"at{l}_{u - 2}")
                v.tensor_scalar(a_buf[:, u % 2, 0:kmax], e_buf[u % 3][:, 0, 0:kmax], su[:, 0:1], None, ALU.mult
                                ).then_inc(ev(f"probs_f{l}"), 1)

            def head_norm(l, h):
                b = take(dve, f"hn{l}_{h}")
                dve.wait_ge(ev(f"head_rstd_first{l}"), h + 1)
                rsqrt(b[:, 0:L], f"hn{l}_{h}")
                v.scalar_tensor_tensor(mixedT[:, 2 + h, :], o_buf[:, h % 2, :], sm(46 + l, 1), rs_t[:, :],
                                       ALU.mult, ALU.mult).then_inc(ev(f"diff_out{l}"), 1)
                dve.wait_ge(ev(f"diff_out{l}"), h + 1)

            def attention(l):
                unit_scores(l, 0)
                unit_scores(l, 1)
                unit_probs(l, 0)
                gelu(l)
                for u in range(len(UNITS) + 2):
                    if u + 2 < len(UNITS):
                        unit_scores(l, u + 2)
                    if u + 1 < len(UNITS):
                        unit_probs(l, u + 1)
                    if u >= 3 and heads_last(u - 3) and UNITS[u - 3][0] == "d":
                        head_norm(l, UNITS[u - 3][1])
                    if u == 1:
                        gelu_end(l)
                    if u in (GLU_AT + 1, GLU_AT + 2):
                        glu(l, u - GLU_AT - 1)

            def add_residual(prefix, n, tiles=range(KD)):
                for k in tiles:
                    b = take(dve, f"{prefix}{k}")
                    release(v.tensor_tensor(resT[:, k, :], resT[:, k, :], b[:, 0:L], ALU.add), f"{prefix}{k}")
                    evacuated(dve, f"{prefix}{k}")
                    if n is not None:
                        dve.sem_inc(ev(f"res{n}"), 1)

            def dense_split_lo(c):
                n = dense_chunk(c)[1]
                dve.wait_ge(ev("dense_split_hi"), c + 1)
                v.tensor_tensor(dw_lo[:, dsplit(c), 0:n], dslot(c), dw_hi[:, dsplit(c), 0:n].bitcast(F32), ALU.subtract
                                ).then_inc(ev("dense_split_lo"), 1)

            def dense_input_lo(k):
                dve.wait_ge(ev("dense_h_hi"), k + 1)
                v.tensor_tensor(dh_lo[:, k, :], hT[:, k, :], dh_hi[:, k, :].bitcast(F32), ALU.subtract
                                ).then_inc(ev("dense_h_lo"), 1)

            def dense():
                for c in range(NDC):
                    kind, f0, n, half = dense_order[c]
                    part = int(f0 >= DPARTS[1][0])
                    first, count = DPARTS[part]
                    if kind == "w3":
                        for f in range(f0, f0 + n):
                            evacuated(dve, f"fa{f}")
                            if f >= 2:
                                dve.wait_ge(ev("dense_g_lo"), f - 1)
                            b = take(dve, f"fb{f}")
                            release(v.tensor_tensor(g_raw[:, f % 2, :], silu_t[:, f % 2, :], b[:, 0:L], ALU.mult), f"fb{f}")
                            evacuated(dve, f"fb{f}")
                            dve.sem_inc(ev("dense_g"), 1)
                    if kind == "w2" and f0 + n == first + count:
                        add_residual(f"y{part}", 2 if part else None, range(4 * half, 4 * half + 4))
                    if c + SPLITS < NDC:
                        dense_split_lo(c + SPLITS)
                    if c == 2:
                        discretise(1)
                    if c == NDC - 3:
                        coefficients(1)
                    if kind == "w3":
                        for f in range(f0, f0 + n):
                            dve.wait_ge(ev("dense_g_hi"), f + 1)
                            v.tensor_tensor(dg_lo[:, f - first, :], g_raw[:, f % 2, :], dg_hi[:, f - first, :].bitcast(F32),
                                            ALU.subtract).then_inc(ev("dense_g_lo"), 1)
                    if c in (5, 6, 8):
                        dve_phases(1, 2 * (c - 5 - (c > 7)), 2 * (c - 5 - (c > 7)) + 2)

            squares(0)
            dve.wait_ge(ev("params_loaded"), 16 * N_PARAM)
            dve.wait_ge(ev("constants_ready"), 1)
            for g in range(2):
                ins = v.tensor_copy(dt_wide[0:16, 64 * g:64 * g + 64], dt_rows[0:16, g:g + 1].to_broadcast([16, 64]))
            ins.then_inc(ev("dt_wide_ready"), 1)
            dve.wait_ge(ev("lam_loaded"), 16 * 4)
            step(v.tensor_tensor(lam_v[:, 0, :, :], lam_v[:, 0, :, :], lam_v[:, 1, :, :], ALU.mult))
            step(v.tensor_tensor(lam_v[:, 2, :, :], lam_v[:, 2, :, :], lam_v[:, 3, :, :], ALU.mult))
            for i in range(2):
                for l in range(DEPTH):
                    v.tensor_reduce(sm(36 + 2 * i + l, 1), lam_v[:, 2 * i, l, :], AX.X, ALU.add).then_inc(ev("lam_dots"), 1)
            step(v.tensor_single_scalar(ints[:, 9:10], ints[:, 8:9], 16, ALU.bitwise_and))
            step(v.tensor_copy(sm(42, 1), ints[:, 9:10]))
            step(v.tensor_scalar(sm(41, 1), sm(42, 1), 1.0 / 16, None, ALU.mult))
            step(v.tensor_scalar(sm(40, 1), sm(41, 1), -1.0, 1.0, ALU.mult, ALU.add))
            evacuated(dve, "prm")
            normalise(0)
            dve.wait_ge(ev("h0"), KD)
            dve.wait_ge(ev("lam_exp"), 1)
            step(v.tensor_tensor(sm(44, 2), sm(34, 2), sm(32, 2), ALU.subtract))
            for l in range(DEPTH):
                lam_init = 0.8 - 0.6 * math.exp(-0.3 * l)
                step(v.tensor_scalar(sm(44 + l, 1), sm(44 + l, 1), -lam_init, None, ALU.add))
            evacuated(dve, "ldt")
            for l in range(DEPTH):
                lam_init = 0.8 - 0.6 * math.exp(-0.3 * l)
                step(v.tensor_scalar(sm(46 + l, 1), prm[:, 32 + l:33 + l], 1.0 - lam_init, None, ALU.mult))
            dve.wait_ge(ev("constants_ready"), 2)
            discretise(0)
            for i in range(0, POOL_PHASES, 2):
                dve_phases(0, i, i + 2)
            coefficients(0)
            for l in range(DEPTH):
                if l == 0:
                    forget_gate(l)
                for i in range(NST):
                    ssm_scan(l, i)
                    if l == 1 and i == 2:
                        forget_gate(l)
                decay(l)
                attention(l)
                if l == 0:
                    dense_split_lo(0)
                    dense_split_lo(1)
                    add_residual("r0", 1)
                    squares(1)
                    normalise(1, lambda k: k and dense_input_lo(k - 1))
                    dense_input_lo(KD - 1)
                    dense_split_lo(2)
                    dense()
                    squares(2)
                    normalise(2)
                    dve.wait_ge(ev("h2"), KD)

            def token_rstd(step, event):
                dve.wait_ge(ev(event), 1)
                step(v.tensor_scalar(sm(116, 2), sm(100, 2), 1.0 / D, EPS, ALU.mult, ALU.add))
                step(v.tensor_tensor(sm(116, 2), sm(116, 2), sm(114, 2), ALU.mult))
                step(v.tensor_tensor(sm(116, 2), sm(116, 2), sm(114, 2), ALU.mult))
                step(v.tensor_scalar(sm(116, 2), sm(116, 2), -0.5, 1.5, ALU.mult, ALU.add))
                step(v.tensor_tensor(sm(102, 2), sm(116, 2), sm(114, 2), ALU.mult))

            token_rstd(step, "token_rstd_first")
            dve.wait_ge(ev("row_gains"), 32)
            for t in range(RT):
                v.scalar_tensor_tensor(htok[:, t, :], racc[:, t, :], sm(102 + t, 1), g_ffn_b, ALU.mult, ALU.mult
                                       ).then_inc(ev("htok"), 1)
            def split_lo(j, m):
                dve.wait_ge(ev("split_hi"), NC * j + m + 1)
                v.tensor_tensor(w_lo[:, m % SPLITS, :], mslot(m), w_hi[:, m % SPLITS, :].bitcast(F32), ALU.subtract
                                ).then_inc(ev("split_lo"), 1)

            split_lo(0, 0)
            split_lo(0, 1)
            lg, gate, chosen, pos = sm(272, 16), sm(288, 16), sm(48, 16), sm(64, 16)
            eq, cs, sel1, sel2 = sm(304, 16), sm(120, 16), sm(136, 16), sm(152, 16)
            m1, m2 = sm(168, 2), sm(170, 2)
            g1, g2, den = sm(108, 2), sm(110, 2), sm(112, 2)

            def two(w):
                return w.rearrange("p (t e) -> p t e", t=RT)

            for t in range(RT):
                b = take(dve, f"lg{t}")
                release(v.tensor_copy(lg[:, NE * t:NE * t + NE], b[:, 0:NE]), f"lg{t}")
                evacuated(dve, f"lg{t}")

            def first_largest(best, pick):
                step(v.tensor_reduce(best, two(lg), AX.X, ALU.max))
                step(v.tensor_tensor(two(eq), two(lg), best.unsqueeze(2).to_broadcast([P, RT, NE]), ALU.is_equal))
                for t in range(RT):
                    w = slice(NE * t, NE * t + NE)
                    step(v.tensor_tensor_scan(cs[:, w], ones_row[:, 0:NE], eq[:, w], 0.0, ALU.mult, ALU.add))
                step(v.scalar_tensor_tensor(pick, cs, 1.0, eq, ALU.is_equal, ALU.mult))

            first_largest(m1, sel1)
            step(v.scalar_tensor_tensor(lg, sel1, NEG, lg, ALU.mult, ALU.add))
            first_largest(m2, sel2)
            v.tensor_tensor(sm(106, 2), m2, m1, ALU.subtract).then_inc(ev("margin"), 1)
            v.tensor_tensor(chosen, sel1, sel2, ALU.add).then_inc(ev("chosen"), 1)
            dve.wait_ge(ev("chosen"), 1)
            dve.wait_ge(ev("margin_exp"), 1)
            step(v.tensor_scalar(den, sm(104, 2), 1.0, None, ALU.add))
            step(v.reciprocal(g1, den))
            step(v.tensor_tensor(g2, g1, sm(104, 2), ALU.mult))
            for t in range(RT):
                w = slice(NE * t, NE * t + NE)
                step(v.tensor_scalar(gate[:, w], sel1[:, w], g1[:, t:t + 1], None, ALU.mult))
                step(v.scalar_tensor_tensor(gate[:, w], sel2[:, w], g2[:, t:t + 1], gate[:, w], ALU.mult, ALU.add))
            for t in range(RT):
                w = slice(NE * t, NE * t + NE)
                b = take(dve, f"rank{t}")
                release(v.scalar_tensor_tensor(pos[:, w], b[:, 0:NE], 1.0, chosen[:, w], ALU.add, ALU.mult), f"rank{t}")
                evacuated(dve, f"rank{t}")
            full, before, row, have = (sm(176 + 8 * i) for i in range(4))
            b = take(dve, "count")
            release(v.tensor_scalar(full, b[:, 0:NE], float(P), None, ALU.is_gt), "count")
            evacuated(dve, "count")
            step(v.tensor_scalar(pos, pos, -1.0, None, ALU.add))
            jpos_t, jgate_t = sb("job_place", RT * 12), sb("job_gate", RT * 12)
            jpos, jgate = cut(jpos_t, 0, RT, 12), cut(jgate_t, 0, RT, 12)
            step(v.tensor_copy(jpos[:, :, 0:NE], two(pos)))
            step(v.tensor_copy(jgate[:, :, 0:NE], two(gate)))
            step(v.memset(jpos[:, :, NE:12], -1.0e6))
            step(v.memset(jgate[:, :, NE:12], 0.0))
            cur_t = sb("current_job", 8)
            moe_step = Chain(dve, ev("expert_steps"))

            def select(j):
                moe_step(v.tensor_copy(cur_t[:, 0:2], jpos[:, :, bass.ds(j, 1)] if not isinstance(j, int)
                                       else jpos[:, :, j:j + 1]))
                for t in range(RT):
                    ins = v.tensor_scalar(sel[:, t, :], slot_iota, cur_t[:, t:t + 1], None, ALU.is_equal)
                ins.then_inc(ev("sel_ready"), 1)

            def gather_lo(n):
                for b in range(2):
                    dve.wait_ge(ev("gather_hi"), n + 1 + b)
                    k = slice(4 * b, 4 * b + 4)
                    ins = v.tensor_tensor(h_lo[:, k, :], bank[2 + b][:, :].rearrange("p (k s) -> p k s", k=4),
                                          h_hi[:, k, :].bitcast(F32), ALU.subtract)
                ins.then_inc(ev("gather_split"), 1)

            def turn_lo(j, fb):
                dve.wait_ge(ev("turn_hi"), 7 * j + fb + 1)
                v.tensor_tensor(gT_lo[:, fb % 2, :], bank[4][:, :], gT_hi[:, fb % 2, :].bitcast(F32), ALU.subtract
                                ).then_inc(ev("turn_split"), 1)

            def add_scattered(n):
                for i in range(4):
                    r = racc[:, i // 2, 512 * (i % 2):512 * (i % 2) + 512]
                    dve.wait_ge(ev("scattered"), 4 * n + i + 1)
                    v.tensor_tensor(r, r, bank[2 + i][:, :], ALU.add).then_inc(ev("added"), 1)

            select(0)
            first = moe_step.n
            pick, tmp = cut(attn, 1792, 3, NE), cut(attn, 1824, 3, NE)
            wide, wide_g = (cut(attn, 1856 + 64 * i, RT, 3, NE) for i in range(2))
            step(v.tensor_tensor_scan(before, ones_row[:, 0:NE], full, 0.0, ALU.mult, ALU.add))
            v.tensor_scalar(row[:, 3:4], before[:, NE - 1:NE], float(NE), None, ALU.add)
            for n in range(3):
                ins = v.scalar_tensor_tensor(pick[:, n, :], before, float(n + 1), full, ALU.is_equal, ALU.mult)
            step(ins)
            v.tensor_tensor(tmp, pick, expert_iota.unsqueeze(1).to_broadcast([P, 3, NE]), ALU.mult)
            for t in range(RT):
                w = slice(NE * t, NE * t + NE)
                v.scalar_tensor_tensor(wide[:, t, :, :], pos[:, w].unsqueeze(1).to_broadcast([P, 3, NE]), -float(P), pick,
                                       ALU.add, ALU.mult)
                v.tensor_tensor(wide_g[:, t, :, :], gate[:, w].unsqueeze(1).to_broadcast([P, 3, NE]), pick, ALU.mult)
            step(v.tensor_reduce(have[:, 0:3], pick, AX.X, ALU.add))
            v.tensor_reduce(row[:, 0:3], tmp, AX.X, ALU.add)
            for t in range(RT):
                v.tensor_reduce(jgate[:, t, NE:NE + 3], wide_g[:, t, :, :], AX.X, ALU.add)
                v.tensor_reduce(jpos[:, t, NE:NE + 3], wide[:, t, :, :], AX.X, ALU.add)
            step(v.tensor_scalar(have[:, 0:3], have[:, 0:3], -1.0, 1.0e6, ALU.add, ALU.mult))
            for t in range(RT):
                ins = v.tensor_tensor(jpos[:, t, NE:NE + 3], jpos[:, t, NE:NE + 3], have[:, 0:3], ALU.add)
            step(ins)
            v.tensor_copy(ints[:, 0:4], row[:, 0:4]).then_inc(ev("jobs_ready"), 1)
            dve.wait_ge(ev("jobs_ready"), 1)

            split_lo(0, 2)
            gather_lo(0)
            v.memset(ysb, 0.0).then_inc(ev("y_evac"), 2)
            v.memset(scat, 0.0).then_inc(ev("scat_evac"), 1)
            n_jobs = dve.value_load(ints[0:1, 3:4], min_val=NE, max_val=MAX_JOBS)
            STEPS = 3
            with dve.Fori(0, n_jobs) as j:
                moe_step.base, moe_step.n = STEPS * j + first, 0
                for c in range(NC):
                    if c == GATHER_AFTER:
                        turn_lo(j, NFB - 1)
                    if c == NC - 1:
                        dve.wait_ge(mchunk_used, NC * j + NC)
                        v.tensor_copy(ysb[:, 512:D], bank[7][:, :]).then_inc(ev("y_evac"), 1)
                    if c in gate_after:
                        fb = gate_after[c]
                        dve.wait_ge(ev("silu_done"), 7 * j + fb + 1)
                        dve.wait_ge(mchunk_used, NC * j + c + 1)
                        v.tensor_tensor(g_e[:, fb % 2, :], e1[:, fb % 2, :], bank[2 * (fb % 2) + 1][:, :], ALU.mult
                                        ).then_inc(ev("g_ready"), 1)
                    split_lo(j, c + SPLITS)
                    if c in turn_after:
                        turn_lo(j, turn_after[c])
                    if c == 1:
                        add_scattered(j)
                    if c == 3:
                        moe_step(v.tensor_copy(cur_t[:, 2:4], jpos[:, :, bass.ds(j, 1)]))
                        moe_step(v.tensor_copy(cur_t[:, 4:6], jgate[:, :, bass.ds(j, 1)]))
                        for t in range(RT):
                            ins = v.tensor_scalar(selg[:, t, :], slot_iota, cur_t[:, 2 + t:3 + t],
                                                  cur_t[:, 4 + t:5 + t], ALU.is_equal, ALU.mult)
                        ins.then_inc(ev("selg_ready"), 1)
                    if c == 28:
                        select(j + 1)
                    if c == GATHER_AFTER:
                        gather_lo(2 * j + 2)
                assert moe_step.n == STEPS
            add_scattered(n_jobs)

            end = Chain(dve, ev("final_steps"))
            for t in range(RT):
                dve.wait_ge(ev("added"), 4 * n_jobs + 2 * t + 2)
                dve.sem_inc(ev("final_ready"), 1)
            token_rstd(end, "final_rstd_first")
            for t in range(RT):
                v.scalar_tensor_tensor(racc[:, t, :], racc[:, t, :], sm(102 + t, 1), g_fin_b, ALU.mult, ALU.mult
                                       ).then_inc(ev("out_ready"), 1)


_INS = ["x", "meta_tokens", "norm_mix_g", "w_in", "w_out", "ssm_lambda_re", "ssm_lambda_im", "ssm_log_dt",
        "ssm_b_re", "ssm_b_im", "ssm_c_re", "ssm_c_im", "ssm_d", "ssm_w_glu", "diff_lambda_q1", "diff_lambda_k1",
        "diff_lambda_q2", "diff_lambda_k2", "diff_subln_g", "fox_forget_b", "norm_ffn_g", "dense_w1", "dense_w3",
        "dense_w2", "moe_router", "moe_w1", "moe_w3", "moe_w2", "final_norm_g"]


def kernel(**inputs):
    import numpy as _np
    import concourse.bacc as _bacc
    from concourse import mybir as _mybir
    from concourse.bass_utils import run_bass_kernel_spmd as _run

    nc = _bacc.Bacc("TRN2", target_bir_lowering=False, num_devices=1)
    arrays, args = {}, {}
    for name in _INS:
        x = _np.ascontiguousarray(inputs[name])
        arrays[f"in_{name}"] = x
        args[name] = nc.dram_tensor(f"in_{name}", x.shape, _mybir.dt.from_np(x.dtype), kind="ExternalInput").ap()
    out = nc.dram_tensor("out_0", (1, SEQ, D), _mybir.dt.float32, kind="ExternalOutput").ap()
    build(nc, args, out)
    r = _run(nc, [arrays], core_ids=[0])
    return r.results[0]["out_0"]
```
